# Optimizing a Trainium2 kernel written in Bass

```python
import jax, jax.numpy as jnp
from jax import lax
import numpy as np

D_MODEL = 1024
BATCH = 1
SEQ = 128
DEPTH = 4
DEC_BATCH = 1
DEC_SEQ = 128
PAST_LEN = 128

GRID_W = 64
N_MIXERS = 3
N_POOL_LAYERS = (DEPTH + 2) // 3
N_ATTN_LAYERS = (DEPTH + 1) // 3
N_FOURIER_LAYERS = DEPTH // 3
POOL_WINDOWS = (2, 4, 8, 16)
POOL_GROUPS = 4
POOL_CH = D_MODEL // POOL_GROUPS
HEAD_DIM = 64
N_HEADS = D_MODEL // HEAD_DIM
WIN_ROWS = 8
WIN_COLS = 16
FOURIER_GROUPS = 4
N_EXPERTS = 16
N_EXPERT_GROUPS = 4
EXPERTS_PER_GROUP = N_EXPERTS // N_EXPERT_GROUPS
TOP_K = 2
D_EXPERT = 512
EPS = 1e-6
ATTN_SCALE = HEAD_DIM ** -0.5

kernel_name = 'hybrid_pool_natten_fourier_moe_dit_step'

def rms_norm(x, g):
    xf = x.astype(jnp.float32)
    y = xf * lax.rsqrt(jnp.mean(xf * xf, axis=-1, keepdims=True) + EPS) * g.astype(jnp.float32)
    return y.astype(x.dtype)

def pool_mix(h, w, scale):
    B, N, D = h.shape
    hf = h.astype(jnp.float32)
    cs = jnp.concatenate([jnp.zeros((B, 1, D), jnp.float32), jnp.cumsum(hf, axis=1)], axis=1)
    t = jnp.arange(N)
    outs = []
    for g, win in enumerate(POOL_WINDOWS):
        lo = jnp.clip(t - win // 2, 0, N)
        hi = jnp.clip(t - win // 2 + win, 0, N)
        sl = slice(g * POOL_CH, (g + 1) * POOL_CH)
        mean = (cs[:, hi, sl] - cs[:, lo, sl]) / (hi - lo).astype(jnp.float32)[None, :, None]
        outs.append(mean - hf[:, :, sl])
    p = jnp.stack(outs, axis=2).astype(h.dtype)
    y = jnp.einsum('bngc,gcd->bngd', p, w).reshape(B, N, D)
    return y * scale

def fourier_mix(h, w):
    B, N, D = h.shape
    hg = h.astype(jnp.float32).reshape(B, N, FOURIER_GROUPS, D // FOURIER_GROUPS)
    f = jnp.fft.fft2(hg, axes=(1, 3), norm='ortho').real.astype(h.dtype).reshape(B, N, D)
    return f @ w

def na_context(h, wqkv, wo):
    B, N, D = h.shape
    qkv = (h @ wqkv).reshape(B, N, 3, N_HEADS, HEAD_DIM)
    q, k, v = qkv[:, :, 0], qkv[:, :, 1], qkv[:, :, 2]
    s = jnp.einsum('bqhd,bkhd->bhqk', q, k).astype(jnp.float32) * ATTN_SCALE
    p = jax.nn.softmax(s, axis=-1).astype(v.dtype)
    o = jnp.einsum('bhqk,bkhd->bqhd', p, v).reshape(B, N, D)
    return o @ wo, k, v

def na_latent(h, ctx_k, ctx_v, wqkv, wo, rpb):
    B, N, D = h.shape
    R = N // GRID_W
    KR = min(WIN_ROWS, R)
    qkv = (h @ wqkv).reshape(B, R, GRID_W, 3, N_HEADS, HEAD_DIM)
    q, k, v = qkv[:, :, :, 0], qkv[:, :, :, 1], qkv[:, :, :, 2]
    r = jnp.arange(R)
    rs = jnp.clip(r - KR // 2, 0, R - KR)
    row_idx = rs[:, None] + jnp.arange(KR)[None, :]
    kg = k[:, row_idx]
    vg = v[:, row_idx]
    cq = jnp.arange(GRID_W)
    cstart = jnp.clip(cq - WIN_COLS // 2, 0, GRID_W - WIN_COLS)
    ck = jnp.arange(GRID_W)
    valid_col = (ck[None, :] >= cstart[:, None]) & (ck[None, :] < cstart[:, None] + WIN_COLS)
    row_b = (row_idx - r[:, None]) + (WIN_ROWS - 1)
    col_b = jnp.clip(ck[None, :] - cq[:, None] + (WIN_COLS - 1), 0, 2 * WIN_COLS - 2)
    bias = rpb[:, row_b[:, None, :, None], col_b[None, :, None, :]].astype(jnp.float32)
    s_loc = jnp.einsum('brqhd,brkwhd->bhrqkw', q, kg).astype(jnp.float32) * ATTN_SCALE + bias[None]
    s_loc = jnp.where(valid_col[:, None, :], s_loc, -jnp.inf)
    s_ctx = jnp.einsum('brqhd,bmhd->bhrqm', q, ctx_k).astype(jnp.float32) * ATTN_SCALE
    n_loc = KR * GRID_W
    s = jnp.concatenate([s_loc.reshape(B, N_HEADS, R, GRID_W, n_loc), s_ctx], axis=-1)
    p = jax.nn.softmax(s, axis=-1).astype(v.dtype)
    p_loc = p[..., :n_loc].reshape(B, N_HEADS, R, GRID_W, KR, GRID_W)
    p_ctx = p[..., n_loc:]
    o = (jnp.einsum('bhrqkw,brkwhd->brqhd', p_loc, vg)
         + jnp.einsum('bhrqm,bmhd->brqhd', p_ctx, ctx_v)).reshape(B, N, D)
    return o @ wo

def moe(h, router_w, router_b, w_gate, w_up, w_down):
    scores = jax.nn.sigmoid((h @ router_w).astype(jnp.float32))
    sel = scores + router_b.astype(jnp.float32)
    sel_g = sel.reshape(sel.shape[:-1] + (N_EXPERT_GROUPS, EXPERTS_PER_GROUP))
    group_score = lax.top_k(sel_g, 2)[0].sum(-1)
    best = jnp.argmax(group_score, axis=-1)
    in_group = (jnp.arange(N_EXPERTS) // EXPERTS_PER_GROUP) == best[..., None]
    _, idx = lax.top_k(jnp.where(in_group, sel, -jnp.inf), TOP_K)
    wts = jnp.take_along_axis(scores, idx, axis=-1)
    wts = wts / jnp.sum(wts, axis=-1, keepdims=True)
    gates = jnp.sum(jax.nn.one_hot(idx, N_EXPERTS, dtype=jnp.float32) * wts[..., None], axis=-2)
    g = jnp.einsum('bnd,edf->bnef', h, w_gate)
    u = jnp.einsum('bnd,edf->bnef', h, w_up)
    a = jax.nn.silu(g) * u * gates[..., None].astype(h.dtype)
    return jnp.einsum('bnef,efd->bnd', a, w_down)

def trunk(x, cond, ctx_k, ctx_v, ada_w, ada_b, norm1_g, norm2_g, pool_w, pool_scale,
          attn_wqkv, attn_wo, attn_rpb, fourier_w, router_w, router_b,
          moe_w_gate, moe_w_up, moe_w_down, final_norm_g):
    D = x.shape[-1]
    ks, vs = [], []
    cond_act = jax.nn.silu(cond)
    for i in range(DEPTH):
        mod = (cond_act @ ada_w[i] + ada_b[i])[:, None, :]
        sh1, sc1, g1, sh2, sc2, g2 = [mod[..., n * D:(n + 1) * D] for n in range(6)]
        h = rms_norm(x, norm1_g[i]) * (1 + sc1) + sh1
        kind, j = i % N_MIXERS, i // N_MIXERS
        if kind == 0:
            m = pool_mix(h, pool_w[j], pool_scale[j])
        elif kind == 1:
            if ctx_k is None:
                m, k, v = na_context(h, attn_wqkv[j], attn_wo[j])
                ks.append(k)
                vs.append(v)
            else:
                m = na_latent(h, ctx_k[:, j], ctx_v[:, j], attn_wqkv[j], attn_wo[j], attn_rpb[j])
        else:
            m = fourier_mix(h, fourier_w[j])
        x = x + g1 * m
        h = rms_norm(x, norm2_g[i]) * (1 + sc2) + sh2
        x = x + g2 * moe(h, router_w, router_b, moe_w_gate[i], moe_w_up[i], moe_w_down[i])
    return rms_norm(x, final_norm_g), ks, vs

def setup_inputs(seed: int = 0) -> dict:
    key = jax.random.key(seed)
    kk = jax.random.split(key, 24)
    D = D_MODEL

    def nrm(k, shape, s):
        return jax.random.normal(k, shape, jnp.float32) * s

    return {
        'x_prompt': nrm(kk[0], (BATCH, SEQ, D), 1.0),
        'x_sample': nrm(kk[1], (DEC_BATCH, DEC_SEQ, D), 1.0),
        'cache_k': nrm(kk[2], (DEC_BATCH, N_ATTN_LAYERS, PAST_LEN, N_HEADS, HEAD_DIM), 1.0),
        'cache_v': nrm(kk[3], (DEC_BATCH, N_ATTN_LAYERS, PAST_LEN, N_HEADS, HEAD_DIM), 1.0),
        'c': nrm(kk[4], (DEC_BATCH, D), 1.0),
        'c_ctx': nrm(kk[5], (D,), 1.0),
        'ada_w': nrm(kk[6], (DEPTH, D, 6 * D), 0.5 * D ** -0.5),
        'ada_b': nrm(kk[7], (DEPTH, 6 * D), 0.01),
        'norm1_g': 1.0 + nrm(kk[8], (DEPTH, D), 0.1),
        'norm2_g': 1.0 + nrm(kk[9], (DEPTH, D), 0.1),
        'pool_w': nrm(kk[10], (N_POOL_LAYERS, POOL_GROUPS, POOL_CH, POOL_CH), POOL_CH ** -0.5),
        'pool_scale': 1.0 + nrm(kk[11], (N_POOL_LAYERS, D), 0.1),
        'attn_wqkv': nrm(kk[12], (N_ATTN_LAYERS, D, 3 * D), D ** -0.5),
        'attn_wo': nrm(kk[13], (N_ATTN_LAYERS, D, D), D ** -0.5),
        'attn_rpb': nrm(kk[14], (N_ATTN_LAYERS, N_HEADS, 2 * WIN_ROWS - 1, 2 * WIN_COLS - 1), 0.1),
        'fourier_w': nrm(kk[15], (N_FOURIER_LAYERS, D, D), D ** -0.5),
        'router_w': nrm(kk[16], (D, N_EXPERTS), D ** -0.5),
        'router_b': nrm(kk[17], (N_EXPERTS,), 0.01),
        'moe_w_gate': nrm(kk[18], (DEPTH, N_EXPERTS, D, D_EXPERT), D ** -0.5),
        'moe_w_up': nrm(kk[19], (DEPTH, N_EXPERTS, D, D_EXPERT), D ** -0.5),
        'moe_w_down': nrm(kk[20], (DEPTH, N_EXPERTS, D_EXPERT, D), D_EXPERT ** -0.5),
        'final_norm_g': 1.0 + nrm(kk[21], (D,), 0.1),
    }

def reference(x_prompt, x_sample, cache_k, cache_v, c, c_ctx, ada_w, ada_b, norm1_g, norm2_g,
              pool_w, pool_scale, attn_wqkv, attn_wo, attn_rpb, fourier_w, router_w, router_b,
              moe_w_gate, moe_w_up, moe_w_down, final_norm_g):
    y_prompt, ks, vs = trunk(x_prompt, c_ctx[None, :], None, None, ada_w, ada_b, norm1_g, norm2_g,
                             pool_w, pool_scale, attn_wqkv, attn_wo, attn_rpb, fourier_w,
                             router_w, router_b, moe_w_gate, moe_w_up, moe_w_down, final_norm_g)
    new_cache_k = jnp.stack(ks, axis=1)
    new_cache_v = jnp.stack(vs, axis=1)
    y_sample, _, _ = trunk(x_sample, c, cache_k, cache_v, ada_w, ada_b, norm1_g, norm2_g,
                           pool_w, pool_scale, attn_wqkv, attn_wo, attn_rpb, fourier_w,
                           router_w, router_b, moe_w_gate, moe_w_up, moe_w_down, final_norm_g)
    return (y_prompt, y_sample, new_cache_k, new_cache_v)


_drawn_inputs = setup_inputs


def setup_inputs(seed=0):
    import zlib

    import numpy as np

    out = dict(_drawn_inputs(seed))
    spreads = {}
    factors = {}
    for name, (base, spread) in spreads.items():
        noise = np.random.default_rng([zlib.crc32(name.encode()), seed]).standard_normal(out[name].shape)
        drawn = base * np.exp(spread * noise) if base else spread * noise
        out[name] = __import__('jax').numpy.asarray(drawn.astype(out[name].dtype))
    for name, factor in factors.items():
        out[name] = (out[name] * factor).astype(out[name].dtype)
    return out
```

```python
from contextlib import ExitStack

import numpy as np

import concourse.bass as bass
from concourse import mybir

F32 = mybir.dt.float32
F32R = mybir.dt.float32r
I32 = mybir.dt.int32
ALU = mybir.AluOpType
ACT = mybir.ActivationFunctionType
AX_X = mybir.AxisListType.X

P = 128
D = 1024
DB = D // P
SEQ = 128
NSEQ = 2
T = NSEQ * SEQ
DEPTH = 4
HEADS = 16
HD = 64
PAIRS = HEADS // 2
E = 16
GROUP = 4
NG = E // GROUP
F = 512
FB = F // P
SLOTS = 64
MAX_ROUNDS = T // SLOTS
EPS = 1e-6
SCALE = HD ** -0.5
GRID_W = 64
WIN_ROWS, WIN_COLS = 8, 16
MASKED = -1e30

BLOCKS = [("gu", 0), ("gu", 1), ("dn", 0), ("gu", 2), ("dn", 1), ("gu", 3), ("dn", 2), ("dn", 3)]
UNITS = [(kind, e, i) for kind, e in BLOCKS for i in range(DB if kind == "gu" else FB)]
NU = len(UNITS)
FIRST = {b: UNITS.index((b[0], b[1], 0)) for b in BLOCKS}
END = {b: FIRST[b] + (DB if b[0] == "gu" else FB) - 1 for b in BLOCKS}
RAW = 6
PAIR_LOADS = NU // 2
RING = 4
GRANT = 1
RAW_CREDIT = 2 * RAW

AFTER_GATE_UP = {END[("gu", e)] + 1: e for e in range(GROUP)}
AFTER_HIDDEN = {END[("gu", 0)] + 3: 0, END[("dn", 0)] + 2: 1, END[("dn", 1)] + 2: 2, END[("dn", 2)] + 2: 3}
AFTER_DOWN = {END[("dn", e)] + 1: e for e in range(GROUP - 1)}

ADA_COLS = 6 * D // (NG * 4)
ADA_NB = ADA_COLS // P
ADA_CHUNKS = 16
NB_MOD = 6 * DB

C_IDENT, C_TRI, C_ONES, C_HALVES, C_IOTA = 0, 128, 256, 384, 448
C_LIMITS, C_BEFORE, C_AFTER, C_END = 576, 579, 595, 611
WM_COLS = 256
WM_RING = 3


def host_constants():
    i = np.arange(P)
    base = np.zeros((P, C_END), np.float32)
    base[:, C_IDENT:C_IDENT + P] = np.eye(P)
    base[:, C_TRI:C_TRI + P] = i[:, None] < i[None, :]
    base[:, C_ONES:C_ONES + P] = 1.0
    base[:, C_HALVES:C_HALVES + SLOTS] = (i[:, None] % SLOTS) == np.arange(SLOTS)[None, :]
    base[:, C_IOTA:C_IOTA + P] = (i % SLOTS)[None, :]
    base[:, C_LIMITS:C_LIMITS + 3] = SLOTS * np.arange(1, 4)[None, :]
    j = np.arange(GROUP)
    base[:, C_BEFORE:C_BEFORE + 16] = (j[None, :] < j[:, None]).reshape(1, 16)
    base[:, C_AFTER:C_AFTER + 16] = (j[None, :] > j[:, None]).reshape(1, 16)
    pool = np.zeros((P, 4, P), np.float32)
    for g, win in enumerate((2, 4, 8, 16)):
        lo = np.clip(i - win // 2, 0, SEQ)
        hi = np.clip(i - win // 2 + win, 0, SEQ)
        pool[:, g, :] = (1.0 / (hi - lo))[None, :]
    attn = np.zeros((P, 2, P), np.float32)
    cq = i % GRID_W
    start = np.clip(cq - WIN_COLS // 2, 0, GRID_W - WIN_COLS)
    ok = (cq[None, :] >= start[:, None]) & (cq[None, :] < start[:, None] + WIN_COLS)
    attn[:, 0, :] = np.where(ok, 0.0, MASKED)
    attn[i, 1, (i // GRID_W) * GRID_W + GRID_W - 1 - cq] = 1.0
    four = np.zeros((P, 2 * P + 2 * 512), np.float32)
    wn = 2 * np.pi * np.outer(i, i) / SEQ
    four[:, 0:P] = np.cos(wn) / np.sqrt(SEQ)
    four[:, P:2 * P] = -np.sin(wn) / np.sqrt(SEQ)
    c = np.arange(256)
    wc = 2 * np.pi * np.outer(c, c) / 256
    both = np.concatenate([np.cos(wc), np.sin(wc)], axis=1) / 16.0
    four[:, 2 * P:] = both.reshape(2, P, 512).transpose(1, 0, 2).reshape(P, 1024)
    return {"k_base": base, "k_pool": pool.reshape(P, 512), "k_attn": attn.reshape(P, 256), "k_four": four}


def build(nc, x_prompt, x_sample, cache_k, cache_v, c, c_ctx, ada_w, ada_b, norm1_g, norm2_g, pool_w,
          pool_scale, attn_wqkv, attn_wo, attn_rpb, fourier_w, router_w, router_b, moe_w_gate, moe_w_up,
          moe_w_down, final_norm_g, k_base, k_pool, k_attn, k_four,
          y_prompt, y_sample, new_cache_k, new_cache_v):
    ctx = ExitStack()
    with ctx:
        def sb(name, shape, dt=F32, stack=ctx):
            return stack.enter_context(nc.sbuf_tensor(name, shape, dt))

        def sem(name):
            return ctx.enter_context(nc.semaphore(name))

        xT = sb("xT", [P, DB, T])
        hT = sb("hT", [P, DB, T])
        raw = sb("raw", [P, RAW, 2, D])
        ada_in = sb("ada_in", [P, 2, DB, ADA_COLS])
        const = sb("const", [P, C_END])
        mods = sb("mods", [P, DEPTH, NB_MOD, NSEQ])
        vecs = sb("vecs", [P, 104])
        adab = sb("adab", [P, DEPTH * NB_MOD])
        cact = sb("cact", [P, NSEQ, DB])
        rw = sb("rw", [P, DB, E])
        rb = sb("rb", [P, E])
        amul = sb("amul", [P, DB, NSEQ])
        pcoef = sb("pcoef", [P, DB, NSEQ])
        ms = sb("ms", [P, T])
        rstd = sb("rstd", [P, T])
        newton = sb("newton", [P, T])
        posx = sb("posx", [P, MAX_ROUNDS * NG, NSEQ, GROUP])
        gx = sb("gx", [P, NG, NSEQ, GROUP])
        rounds = sb("rounds", [P, DEPTH], I32)
        credit = sb("credit", [P, 8])

        ident = const[:, C_IDENT:C_IDENT + P]
        tri = const[:, C_TRI:C_TRI + P]
        ones = const[:, C_ONES:C_ONES + P]
        halves = const[:, C_HALVES:C_HALVES + SLOTS]
        iota = const[:, C_IOTA:C_IOTA + P]
        limits = const[:, C_LIMITS:C_LIMITS + 3]
        before = const[:, C_BEFORE:C_BEFORE + 16]
        after = const[:, C_AFTER:C_AFTER + 16]
        cond = vecs[:, 0:16]
        n1g, n2g = vecs[:, 16:48], vecs[:, 48:80]
        fing, pscale = vecs[:, 80:88], vecs[:, 88:104]

        with ExitStack() as moe:
            w_hi = sb("w_hi", [P, RING, D], F32R, moe)
            w_lo = sb("w_lo", [P, RING, D], F32R, moe)
            xg = sb("xg", [P, DB, GROUP, 2 * SLOTS], F32R, moe)
            h_hi = sb("h_hi", [P, NSEQ, D], F32R, moe)
            h_lo = sb("h_lo", [P, NSEQ, D], F32R, moe)
            y_hi = sb("y_hi", [P, 2, D], F32R, moe)
            y_lo = sb("y_lo", [P, 2, D], F32R, moe)
            onehot = sb("onehot", [P, NSEQ, GROUP, 2 * SLOTS], F32R, moe)
            onehotT = sb("onehotT", [P, GROUP, T], F32R, moe)
            gsel = sb("gsel", [P, NSEQ, GROUP], F32, moe)
            gcol = sb("gcol", [P, GROUP], F32, moe)
            gu = sb("gu", [P, 2 * F], F32, moe)
            sg = sb("sg", [P, FB * SLOTS], F32, moe)
            act = sb("act", [P, FB * SLOTS], F32, moe)
            a_hl = sb("a_hl", [P, FB, 2 * SLOTS], F32R, moe)
        with ExitStack() as mix:
            work = sb("work", [P, DB, T], F32, mix)
            wm = sb("wm", [P, WM_RING, DB, WM_COLS], F32, mix)
            kT = sb("kT", [P, DB, T], F32, mix)
            vtok = sb("vtok", [P, NSEQ, D], F32, mix)
            ck = sb("ck", [P, D], F32, mix)
            cv = sb("cv", [P, D], F32, mix)
            ckT = sb("ckT", [P, DB, SEQ], F32, mix)
            knew = sb("knew", [P, D], F32, mix)
            bias = sb("bias", [P, HEADS, P], F32, mix)
            oT = sb("oT", [P, DB, T], F32, mix)
            soft = sb("soft", [P, 2, 2, 3 * P], F32, mix)
            pT = sb("pT", [P, 2, 2, 3 * P], F32, mix)
            kattn = sb("kattn", [P, 2, P], F32, mix)
            mstat = sb("mstat", [P, 2, 3, 4], F32, mix)
            rpad = sb("rpad", [HEADS, 3, P], F32, mix)
        with ExitStack() as mix2:
            work2 = sb("work2", [P, DB, T], F32, mix2)
            wm2 = sb("wm2", [P, WM_RING, DB, WM_COLS], F32, mix2)
            zpad = sb("zpad", [P, DB, NSEQ, 144], F32, mix2)
            wsum = sb("wsum", [P, DB, NSEQ, 144], F32, mix2)
            poolT = sb("poolT", [P, DB, T], F32, mix2)
            kpool = sb("kpool", [P, 4, P], F32, mix2)
            wp = sb("wp", [P, 4, 2, 256], F32, mix2)
        with ExitStack() as mix3:
            sb("work3", [P, DB, T], F32, mix3)
            sb("wm3", [P, WM_RING, DB, WM_COLS], F32, mix3)
            ftok = sb("ftok", [P, NSEQ, 4, 512], F32, mix3)
            fT = sb("fT", [P, DB, T], F32, mix3)
            kfour = sb("kfour", [P, 2 * P + 1024], F32, mix3)
        with ExitStack() as mix4:
            sb("work4", [P, DB, T], F32, mix4)
            sb("wm4", [P, WM_RING, DB, WM_COLS], F32, mix4)
            xio = sb("xio", [P, NSEQ, D], F32, mix4)
            vrow = sb("vrow", [P, 3, P], F32, mix4)
        with ExitStack() as rt:
            sb("rt_w_hi", [P, RING, D], F32R, rt)
            sb("rt_w_lo", [P, RING, D], F32R, rt)
            r_sc = sb("r_sc", [P, NSEQ, E], F32, rt)
            r_sel = sb("r_sel", [P, NSEQ * NG, GROUP], F32, rt)
            r_pair = sb("r_pair", [P, NSEQ * NG, 6], F32, rt)
            r_gs = sb("r_gs", [P, NSEQ, NG], F32, rt)
            r_ge = sb("r_ge", [P, NSEQ * NG, 16], F32, rt)
            r_gt = sb("r_gt", [P, NSEQ * NG, 16], F32, rt)
            r_best = sb("r_best", [P, NSEQ * NG], F32, rt)
            r_rank = sb("r_rank", [P, NSEQ * NG, GROUP], F32, rt)
            r_mask = sb("r_mask", [P, NSEQ, E], F32, rt)
            r_w = sb("r_w", [P, NSEQ, E], F32, rt)
            r_den = sb("r_den", [P, NSEQ], F32, rt)
            r_pm = sb("r_pm", [P, NSEQ, NG, GROUP], F32, rt)
            r_cnt = sb("r_cnt", [P, 8], F32, rt)
        ps = ctx.enter_context(nc.psum_tensor("ps", [P, 8, 512], F32))
        B_G, B_U, B_Y, B_T, B_A, B_M = 0, 1, 2, 4, 5, 7
        bias_dram = nc.dram_tensor("bias_rows", [HEADS, 3, P], F32, kind="Internal").ap()

        s_load = sem("s_load")
        s_rows = sem("s_rows")
        s_vecs = sem("s_vecs")
        s_cact = sem("s_cact")
        s_xt = sem("s_xt")
        s_xq = sem("s_xq")
        s_sq = sem("s_sq")
        s_ss = sem("s_ss")
        s_ms = sem("s_ms")
        s_rt = sem("s_rt")
        s_n1 = sem("s_n1")
        s_n2 = sem("s_n2")
        s_hq = sem("s_hq")
        s_link = sem("s_link")
        s_lg = sem("s_lg")
        s_sig = sem("s_sig")
        s_mask = sem("s_mask")
        s_pos = sem("s_pos")
        s_tok = sem("s_tok")
        s_thi = sem("s_thi")
        s_tlo = sem("s_tlo")
        s_rounds = sem("s_rounds")
        s_acc0 = sem("s_acc0")
        s_raw = [sem(f"s_raw{k}") for k in range(RAW)]
        s_issue = sem("s_issue")
        s_hi = sem("s_hi")
        s_lo = sem("s_lo")
        s_unit = sem("s_unit")
        s_oh = sem("s_oh")
        s_ga = sem("s_ga")
        s_gev = sem("s_gev")
        s_god = sem("s_god")
        s_oht = sem("s_oht")
        s_ohs = sem("s_ohs")
        s_gc = sem("s_gc")
        s_gcs = sem("s_gcs")
        s_gus = sem("s_gus")
        s_turn = sem("s_turn")
        s_silu = sem("s_silu")
        s_prod = sem("s_prod")
        s_ahi = sem("s_ahi")
        s_alo = sem("s_alo")
        s_yhi = sem("s_yhi")
        s_ylo = sem("s_ylo")
        s_comb = sem("s_comb")
        s_acc = sem("s_acc")
        s_ada_in = [sem(f"s_ada_in{k}") for k in range(2)]
        s_ada = sem("s_ada")
        s_adas = sem("s_adas")
        s_kc = sem("s_kc")
        s_pz = sem("s_pz")
        s_pt = sem("s_pt")
        s_mix = sem("s_mix")
        s_wm = [sem(f"s_wm{k}") for k in range(WM_RING)]
        s_wmu = sem("s_wmu")
        s_qkve = sem("s_qkve")
        s_qkvo = sem("s_qkvo")
        s_bias = sem("s_bias")
        s_pad = sem("s_pad")
        s_flip = sem("s_flip")
        s_biass = sem("s_biass")
        s_kt = sem("s_kt")
        s_kts = sem("s_kts")
        s_sc = sem("s_sc")
        s_max = sem("s_max")
        s_exp = sem("s_exp")
        s_prob = sem("s_prob")
        s_pt2 = sem("s_pt2")
        s_pts = sem("s_pts")
        s_o = sem("s_o")
        s_os = sem("s_os")
        s_f1 = sem("s_f1")
        s_f1e = sem("s_f1e")
        s_f1o = sem("s_f1o")
        s_f2 = sem("s_f2")
        s_f2s = sem("s_f2s")
        s_yt = sem("s_yt")
        s_yts = sem("s_yts")
        s_out = sem("s_out")
        s_kv = sem("s_kv")

        KINDS = [l % 3 for l in range(DEPTH)]
        N_FIRST_LOADS = 13
        WM_TILES = [("qkv", i) for i in range(12)] + [("wo", i) for i in range(4)] + [("four", i) for i in range(4)]
        WM_AT = {t: n for n, t in enumerate(WM_TILES)}
        KC_AFTER = [32, 80, 96, 128]

        def quarter(t, q):
            return t[:, 2 * q:2 * q + 2, :]

        def per_token(v, q):
            return v[:, 2 * q:2 * q + 2, :].unsqueeze(3).to_broadcast([P, 2, NSEQ, SEQ])

        def by_seq(t):
            return t.rearrange("p d (s t) -> p d s t", s=NSEQ)

        def mod(l, n):
            return mods[:, l, n * DB:(n + 1) * DB, :]

        block = ctx.enter_context(nc.Block())

        @block.sync
        def _(sp):
            def load_ada(layer, chunk, slot):
                sp.dma_start(ada_in[:, slot, :, :],
                             ada_w[layer].rearrange("(b p) n -> p b n", p=P)[:, :, bass.ds(chunk * ADA_COLS, ADA_COLS)]
                             ).then_inc(s_ada_in[slot], 16)

            def load_units(l, e, q):
                kind, _, i = UNITS[2 * q]
                slot = q % RAW
                if kind == "gu":
                    rows = slice(i * P, (i + 2) * P)
                    for n, w in enumerate((moe_w_gate, moe_w_up)):
                        sp.dma_start(raw[:, slot, :, n * F:(n + 1) * F],
                                     w[l, e, rows, :].rearrange("(b p) f -> p b f", p=P)).then_inc(s_raw[slot], 16)
                else:
                    for n in range(2):
                        sp.dma_start(raw[:, slot, n, :],
                                     moe_w_down[l, e, (i + n) * P:(i + n + 1) * P, :]).then_inc(s_raw[slot], 16)

            for chunk in range(ADA_CHUNKS):
                if chunk >= 2:
                    sp.wait_ge(s_ada, chunk - 1)
                load_ada(0, chunk, chunk % 2)

            base = 0
            for l in range(DEPTH):
                def group(k):
                    it = base + k
                    g = k & (NG - 1)

                    def ada_chunk(j):
                        if l == DEPTH - 1:
                            return
                        sp.wait_ge(s_ada, ADA_CHUNKS - 1 + 4 * it + j)
                        sp.sem_inc(s_issue, 1)
                        load_ada(l + 1, g * 4 + j, j % 2)

                    ada_chunk(0)
                    ada_chunk(1)
                    for q in range(PAIR_LOADS):
                        if q == 14:
                            ada_chunk(2)
                        if q == 18:
                            ada_chunk(3)
                        sp.wait_ge(s_lo, it * NU + 2 * q + 2)
                        sp.sem_inc(s_issue, 1)
                        load_units(l, g * GROUP + UNITS[2 * q][1], q)

                with sp.Fori(0, NG) as k:
                    group(k)
                sp.wait_ge(s_rounds, l + 1)
                n = sp.value_load(rounds[0:1, l:l + 1], min_val=1, max_val=MAX_ROUNDS)
                with sp.If(n > 1):
                    with sp.Fori(NG, n * NG) as k:
                        group(k)
                base = sp.snap(base + n * NG)
            sp.wait_ge(s_yts, 4)
            sp.dma_start(y_prompt[0], xio[:, 0, :]).then_inc(s_out, 16)
            sp.dma_start(y_sample[0], xio[:, 1, :]).then_inc(s_out, 16)
            sp.wait_ge(s_out, 32)

        @block.gpsimd
        def _(pool):
            nc.gpsimd.memset(credit[:, 0:1], 0.0).then_inc(s_lo, RAW_CREDIT)
            nc.gpsimd.memset(credit[:, 1:2], 0.0).then_inc(s_unit, RING)
            for n, s in enumerate((s_turn, s_prod, s_gus, s_acc, s_ylo, s_gc)):
                nc.gpsimd.memset(credit[:, 2 + n:3 + n], 0.0).then_inc(s, GRANT)
            loads = [
                (const[:, :], k_base),
                (vrow[0:8, 0, :], c_ctx.rearrange("(b p) -> b p", p=P)),
                (vrow[8:16, 0, :], c.rearrange("a (b p) -> (a b) p", p=P)),
                (vrow[16:48, 0, :], norm1_g.rearrange("l (b p) -> (l b) p", p=P)),
                (vrow[48:80, 0, :], norm2_g.rearrange("l (b p) -> (l b) p", p=P)),
                (vrow[80:88, 0, :], final_norm_g.rearrange("(b p) -> b p", p=P)),
                (vrow[88:104, 0, :], pool_scale.rearrange("l (b p) -> (l b) p", p=P)),
                (vrow[0:96, 1, :], ada_b[0:2].rearrange("l (b p) -> (l b) p", p=P)),
                (vrow[0:96, 2, :], ada_b[2:4].rearrange("l (b p) -> (l b) p", p=P)),
                (xio[:, 0, :], x_prompt[0]),
                (xio[:, 1, :], x_sample[0]),
                (rw[:, :, :], router_w.rearrange("(b p) e -> p b e", p=P)),
                (rb[:, :], router_b.partition_broadcast(P)),
            ]
            assert len(loads) == N_FIRST_LOADS
            for dst, src in loads:
                pool.dma_start(dst, src).then_inc(s_load, 16)

            def weight_tile(name, i):
                n = WM_AT[(name, i)]
                if n >= WM_RING:
                    pool.wait_ge(s_wmu, n - WM_RING + 1)
                src = {"qkv": attn_wqkv, "wo": attn_wo, "four": fourier_w}[name][0]
                pool.dma_start(wm[:, n % WM_RING, :, :],
                               src.rearrange("(b p) n -> p b n", p=P)[:, :, i * WM_COLS:(i + 1) * WM_COLS]
                               ).then_inc(s_wm[n % WM_RING], 16)

            for l in range(DEPTH):
                pool.wait_ge(s_xq, 4 * (2 * l) + 4)
                if KINDS[l] == 0:
                    j = l // 3
                    if l == 0:
                        pool.wait_ge(s_vecs, 2)
                    pool.dma_start(kpool[:, :, :], k_pool).then_inc(s_kc, 16)
                    pool.dma_start(wp[:, :, :, :], pool_w[j].rearrange("g (b p) d -> p g b d", p=P)).then_inc(s_kc, 16)
                    nc.gpsimd.memset(zpad[:, :, :, 0:8], 0.0).then_inc(s_pz, 1)
                    nc.gpsimd.memset(zpad[:, :, :, 136:144], 0.0).then_inc(s_pz, 1)
                elif KINDS[l] == 1:
                    for i in range(3):
                        weight_tile("qkv", i)
                    pool.dma_start(kattn[:, :, :], k_attn).then_inc(s_kc, 16)
                    pool.dma_start(ck[:, :], cache_k[0, 0].rearrange("m h d -> m (h d)")).then_inc(s_kc, 16)
                    pool.dma_start(cv[:, :], cache_v[0, 0].rearrange("m h d -> m (h d)")).then_inc(s_kc, 16)
                    nc.gpsimd.memset(rpad[:, :, :], 0.0).then_inc(s_pad, 1)
                    pool.wait_ge(s_pad, 1)
                    pool.dma_start(rpad[:, :, 48:79], attn_rpb[0, :, WIN_ROWS - 2:WIN_ROWS + 1, :]).then_inc(s_bias, 16)
                    pool.wait_ge(s_bias, 16)
                    pool.dma_start(bias_dram, rpad[:, :, :]).then_inc(s_bias, 16)
                    pool.wait_ge(s_bias, 32)
                    for r in range(2):
                        for kr in range(2):
                            src = bass.AP(tensor=bias_dram.tensor, offset=(kr - r + 1) * P,
                                          ap=[[1, GRID_W], [3 * P, HEADS], [1, GRID_W]])
                            dst = oT[r * GRID_W:(r + 1) * GRID_W, :, :].rearrange("p d t -> p (d t)").rearrange(
                                "p (h k) -> p h k", h=HEADS)[:, :, kr * GRID_W:(kr + 1) * GRID_W]
                            pool.dma_start(dst, src).then_inc(s_bias, 16)
                    for i in range(3, 12):
                        weight_tile("qkv", i)
                    for i in range(4):
                        weight_tile("wo", i)
                    pool.wait_ge(s_kts, 4)
                    pool.dma_start(new_cache_k[0, 0].rearrange("m h d -> m (h d)"), knew[:, :]).then_inc(s_kv, 16)
                    pool.wait_ge(s_qkve, 6)
                    pool.wait_ge(s_qkvo, 6)
                    pool.dma_start(new_cache_v[0, 0].rearrange("m h d -> m (h d)"), vtok[:, 0, :]).then_inc(s_kv, 16)
                    pool.wait_ge(s_kv, 32)
                else:
                    pool.dma_start(kfour[:, :], k_four).then_inc(s_kc, 16)
                    for i in range(4):
                        weight_tile("four", i)
                pool.wait_ge(s_tok, 4 * (l + 1))
                nc.gpsimd.memset(hT[:, :, :], 0.0).then_inc(s_acc0, 1)

        @block.scalar
        def _(ac):
            ac.wait_ge(s_vecs, 1)
            nc.scalar.activation(cact[:, :, :], cond.rearrange("p (s b) -> p s b", s=NSEQ), ACT.Silu).then_inc(s_cact, 1)

            def norm(n):
                for q in range(4):
                    ac.wait_ge(s_xq, 4 * n + q + 1)
                    if n == 0 and q == 0:
                        ac.wait_ge(s_xt, 4)
                    nc.scalar.activation(quarter(work, q), quarter(xT, q), ACT.Square).then_inc(s_sq, 1)
                ac.wait_ge(s_ms, n + 1)
                nc.scalar.activation(rstd[:, :], ms[:, :], ACT.Sqrt).then_inc(s_rt, 1)

            def router(l):
                if KINDS[l] == 1:
                    ac.wait_ge(s_kv, 32)
                ac.wait_ge(s_lg, l + 1)
                nc.scalar.activation(r_sc[:, :, :], ps[:, B_M, 0:2 * E].rearrange("p (s e) -> p s e", s=NSEQ),
                                     ACT.Sigmoid).then_inc(s_sig, 1)
                for b in range(4):
                    ac.wait_ge(s_tok, 4 * l + b + 1)
                    nc.scalar.activation(h_hi[:, b // 2, (b % 2) * 512:(b % 2 + 1) * 512], ps[:, b, :],
                                         ACT.Copy).then_inc(s_thi, 1)

            def mixer_attention():
                for t in range(0, 12, 2):
                    ac.wait_ge(s_wmu, t + 1)
                    bank = ps[:, t % 4, :]
                    if t < 8:
                        dst = quarter(work if t < 4 else kT, t % 4)
                        nc.scalar.activation(dst, bank.rearrange("p (d t) -> p d t", d=2), ACT.Copy).then_inc(s_qkve, 1)
                    else:
                        nc.scalar.activation(vtok[:, :, (t - 8) * 256:(t - 7) * 256],
                                             bank.rearrange("p (s n) -> p s n", s=NSEQ), ACT.Copy).then_inc(s_qkve, 1)
                for b in range(4):
                    ac.wait_ge(s_kt, b + 1)
                    dst = (ckT[:, (b % 2) * 4:(b % 2) * 4 + 4, :].rearrange("p d t -> p (d t)") if b < 2
                           else knew[:, (b % 2) * 512:(b % 2 + 1) * 512])
                    nc.scalar.activation(dst, ps[:, 4 + b, :], ACT.Copy).then_inc(s_kts, 1)

                def exps(hp):
                    ac.wait_ge(s_max, hp + 1)
                    for e in range(2):
                        for part, (a, b) in enumerate(((0, P), (P, 3 * P))):
                            v = soft[:, hp % 2, e, a:b]
                            nc.scalar.activation(v, v, ACT.Exp, bias=mstat[:, hp % 2, 1, 2 * e + part:2 * e + part + 1],
                                                 accum_out=mstat[:, hp % 2, 2, 2 * e + part:2 * e + part + 1]
                                                 ).then_inc(s_exp, 1)

                def copy_turned(hp):
                    ac.wait_ge(s_pt2, hp + 1)
                    if hp >= 2:
                        ac.wait_ge(s_o, hp - 1)
                    nc.scalar.activation(pT[:, hp % 2, :, :], ps[:, 4:6, 0:3 * P], ACT.Copy).then_inc(s_pts, 1)

                exps(0)
                for hp in range(PAIRS):
                    if hp + 1 < PAIRS:
                        exps(hp + 1)
                    copy_turned(hp)

            def mixer_fourier():
                for b in range(0, 8, 2):
                    ac.wait_ge(s_f1, b + 1)
                    nc.scalar.activation(ftok[:, b // 4, b % 4, :], ps[:, b, :], ACT.Copy).then_inc(s_f1e, 1)
                for g in range(4):
                    ac.wait_ge(s_f2, g + 1)
                    nc.scalar.activation(quarter(fT, g), ps[:, g, :].rearrange("p (d t) -> p d t", d=2),
                                         ACT.Copy).then_inc(s_f2s, 1)

            base = 0
            for l in range(DEPTH):
                norm(2 * l)
                if KINDS[l] == 1:
                    mixer_attention()
                if KINDS[l] == 2:
                    mixer_fourier()
                norm(2 * l + 1)
                router(l)
                ac.wait_ge(s_rounds, l + 1)
                n = ac.value_load(rounds[0:1, l:l + 1], min_val=1, max_val=MAX_ROUNDS)
                with ac.Fori(0, n * NG) as k:
                    it = ac.snap(base + k)
                    it8 = ac.snap(it * 8)
                    it48 = ac.snap(it * NU)

                    def split_hi(u):
                        slot = (u // 2) % RAW
                        if u % 2 == 0:
                            ac.wait_ge(s_raw[slot], it * (32 * PAIR_LOADS // RAW) + 32 * (u // 2 // RAW + 1))
                        ac.wait_ge(s_unit, it48 + (u + 1))
                        nc.scalar.activation(w_hi[:, u % RING, :], raw[:, slot, u % 2, :], ACT.Copy).then_inc(s_hi, 1)

                    def output_hi(e):
                        for b in range(2):
                            if b == 0:
                                ac.wait_ge(s_unit, it48 + (RING + END[("dn", e)] + 1))
                                if e == 0:
                                    ac.wait_ge(s_gcs, it + 1)
                                if e >= 2:
                                    ac.wait_ge(s_comb, it8 + 4)
                            nc.scalar.activation(y_hi[:, e % 2, b * 512:(b + 1) * 512], ps[:, B_Y + b, :], ACT.Copy,
                                                 scale=gcol[:, e:e + 1]).then_inc(s_yhi, 1)

                    for db in range(0, DB, 2):
                        ac.wait_ge(s_ga, it8 + (db + 1))
                        nc.scalar.activation(
                            xg[:, db, :, :].rearrange("p e (h s) -> p h e s", h=2),
                            ps[:, B_A, :].rearrange("p (h e s) -> p h e s", h=2, e=GROUP), ACT.Copy).then_inc(s_gev, 1)
                    for b in range(2):
                        ac.wait_ge(s_oht, it * 2 + (b + 1))
                        nc.scalar.activation(onehotT[:, 2 * b:2 * b + 2, :], ps[:, B_A + b, :].rearrange(
                            "p (e t) -> p e t", e=2), ACT.Copy).then_inc(s_ohs, 1)
                    for u in range(NU):
                        split_hi(u)
                        if u in AFTER_GATE_UP:
                            e = AFTER_GATE_UP[u]
                            ac.wait_ge(s_unit, it48 + (RING + END[("gu", e)] + 1))
                            ac.wait_ge(s_turn, it * GROUP + e + GRANT)
                            for b in range(2):
                                nc.scalar.activation(gu[:, b * F:(b + 1) * F], ps[:, B_G + b, :], ACT.Copy).then_inc(s_gus, 1)
                        if u in AFTER_HIDDEN:
                            e = AFTER_HIDDEN[u]
                            ac.wait_ge(s_turn, it * GROUP + (e + 1) + GRANT)
                            ac.wait_ge(s_prod, it * GROUP + e + GRANT)
                            nc.scalar.activation(sg[:, :], ps[:, B_T, 0:FB * SLOTS], ACT.Silu).then_inc(s_silu, 1)
                        if u in AFTER_DOWN:
                            output_hi(AFTER_DOWN[u])
                    output_hi(GROUP - 1)
                base = ac.snap(base + n * NG)
            norm(2 * DEPTH)
            for b in range(4):
                ac.wait_ge(s_yt, b + 1)
                nc.scalar.activation(xio[:, b // 2, (b % 2) * 512:(b % 2 + 1) * 512], ps[:, b, :], ACT.Copy).then_inc(s_yts, 1)

        @block.vector
        def _(v):
            links = [0]

            def link(ins):
                links[0] += 1
                ins.then_inc(s_link, 1)
                v.wait_ge(s_link, links[0])

            v.wait_ge(s_rows, 1)
            v.tensor_copy(vecs[:, :], ps[:, 4, 0:104]).then_inc(s_vecs, 1)
            v.wait_ge(s_rows, 3)
            v.tensor_copy(adab[:, :], ps[:, 5, 0:192]).then_inc(s_vecs, 1)
            for q in range(4):
                v.wait_ge(s_xt, q + 1)
                v.tensor_copy(quarter(xT, q), ps[:, q, :].rearrange("p (d t) -> p d t", d=2)).then_inc(s_xq, 1)
            v.wait_ge(s_vecs, 2)

            def store_ada(layer, nb, count):
                m = mods[:, layer, :, :].rearrange("p n s -> p (n s)")[:, bass.ds(nb * 2, ADA_NB * 2)]
                bb = adab[:, layer * NB_MOD:(layer + 1) * NB_MOD][:, bass.ds(nb, ADA_NB)]
                v.wait_ge(s_ada, count)
                v.tensor_tensor(m.rearrange("p (n s) -> p n s", s=NSEQ),
                                ps[:, B_M, 0:2 * ADA_NB].rearrange("p (n s) -> p n s", s=NSEQ),
                                bb.unsqueeze(2).to_broadcast([P, ADA_NB, NSEQ]), ALU.add).then_inc(s_adas, 1)

            for chunk in range(ADA_CHUNKS):
                store_ada(0, chunk * ADA_NB, chunk + 1)

            def norm(n, gain, scale, shift):
                v.wait_ge(s_ss, n + 1)
                v.tensor_scalar(ms[:, :], ps[:, B_M, 0:T], 1.0 / D, EPS, ALU.mult, ALU.add).then_inc(s_ms, 1)
                g2 = gain.unsqueeze(2).to_broadcast([P, DB, NSEQ])
                if scale is None:
                    link(v.tensor_copy(amul[:, :, :], g2))
                else:
                    link(v.scalar_tensor_tensor(amul[:, :, :], scale, 1.0, g2, ALU.add, ALU.mult))
                v.wait_ge(s_rt, n + 1)
                link(v.reciprocal(rstd[:, :], rstd[:, :]))
                link(v.tensor_tensor(newton[:, :], rstd[:, :], rstd[:, :], ALU.mult))
                link(v.tensor_tensor(newton[:, :], newton[:, :], ms[:, :], ALU.mult))
                link(v.tensor_scalar(newton[:, :], newton[:, :], -0.5, 1.5, ALU.mult, ALU.add))
                link(v.tensor_tensor(rstd[:, :], rstd[:, :], newton[:, :], ALU.mult))
                r2 = rstd[:, :].unsqueeze(1).to_broadcast([P, 2, T])
                for q in range(4):
                    v.tensor_tensor(quarter(hT, q), quarter(xT, q), r2, ALU.mult).then_inc(s_n1, 1)
                last = s_hq if shift is None else s_n2
                for q in range(4):
                    h = by_seq(quarter(hT, q))
                    v.wait_ge(s_n1, 4 * n + q + 1)
                    v.tensor_tensor(h, h, per_token(amul, q), ALU.mult).then_inc(last, 1)
                if shift is not None:
                    for q in range(4):
                        h = by_seq(quarter(hT, q))
                        v.wait_ge(s_n2, 4 * n + q + 1)
                        v.tensor_tensor(h, h, per_token(shift, q), ALU.add).then_inc(s_hq, 1)

            def residual(src, coef, q):
                for d in range(2):
                    for s in range(NSEQ):
                        x = xT[:, 2 * q + d, s * SEQ:(s + 1) * SEQ]
                        ins = v.scalar_tensor_tensor(x, src(d, s), coef[:, 2 * q + d, s:s + 1], x, ALU.mult, ALU.add)
                ins.then_inc(s_xq, 1)

            def residual_from_banks(done, before, coef, first_bank):
                for q in range(4):
                    v.wait_ge(done, before + q + 1)
                    bank = ps[:, first_bank + q, :]
                    residual(lambda d, s: bank[:, (2 * d + s) * SEQ:(2 * d + s + 1) * SEQ], coef, q)

            def mixer_pool(l):
                j = l // 3
                gain = pscale[:, j * DB:(j + 1) * DB].unsqueeze(2).to_broadcast([P, DB, NSEQ])
                link(v.tensor_tensor(pcoef[:, :, :], mod(l, 2), gain, ALU.mult))
                v.wait_ge(s_pz, 2 * j + 2)
                for q in range(4):
                    link(v.tensor_copy(zpad[:, 2 * q:2 * q + 2, :, 8:136], by_seq(quarter(hT, q))))
                v.wait_ge(s_kc, KC_AFTER[l])
                link(v.tensor_tensor(wsum[:, :, :, 0:143], zpad[:, :, :, 0:143], zpad[:, :, :, 1:144], ALU.add))
                width, n = 2, 143
                sums, spare = wsum, zpad
                for g in range(4):
                    out = by_seq(quarter(poolT, g))
                    a = 8 - width // 2
                    inv = kpool[:, g, :].unsqueeze(1).unsqueeze(1).to_broadcast([P, 2, NSEQ, SEQ])
                    link(v.tensor_tensor(out, sums[:, 2 * g:2 * g + 2, :, a:a + SEQ], inv, ALU.mult))
                    v.tensor_tensor(out, out, by_seq(quarter(hT, g)), ALU.subtract).then_inc(s_pt, 1)
                    if g < 3:
                        n -= width
                        rest = slice(2 * g + 2, DB)
                        link(v.tensor_tensor(spare[:, rest, :, 0:n], sums[:, rest, :, 0:n],
                                             sums[:, rest, :, width:width + n], ALU.add))
                        sums, spare = spare, sums
                        width *= 2
                residual_from_banks(s_mix, 4 * j, pcoef, 0)

            def mixer_attention(l):
                v.wait_ge(s_kc, KC_AFTER[l])
                mask = kattn[:, 0, :].unsqueeze(1).to_broadcast([P, 4, P])
                for b in range(4):
                    v.wait_ge(s_flip, b + 1)
                    v.tensor_tensor(bias[:, 4 * b:4 * b + 4, :], ps[:, 4 + b, :].rearrange("p (h k) -> p h k", h=4),
                                    mask, ALU.add).then_inc(s_biass, 1)
                for t in range(1, 12, 2):
                    v.wait_ge(s_wmu, t + 1)
                    bank = ps[:, t % 4, :]
                    if t < 8:
                        dst = quarter(work if t < 4 else kT, t % 4)
                        v.tensor_copy(dst, bank.rearrange("p (d t) -> p d t", d=2)).then_inc(s_qkvo, 1)
                    else:
                        v.tensor_copy(vtok[:, :, (t - 8) * 256:(t - 7) * 256],
                                      bank.rearrange("p (s n) -> p s n", s=NSEQ)).then_inc(s_qkvo, 1)

                def scale_bias_max(hp):
                    par = hp % 2
                    v.wait_ge(s_sc, hp + 1)
                    if hp >= 2:
                        v.wait_ge(s_pt2, hp - 1)
                    else:
                        v.wait_ge(s_biass, 4)
                    banks = ps[:, 2 * par:2 * par + 2, 0:3 * P]
                    v.tensor_scalar(soft[:, par, :, 0:P], banks[:, :, 0:P], SCALE, None, ALU.mult)
                    v.tensor_scalar(soft[:, par, :, 2 * P:3 * P], banks[:, :, 2 * P:3 * P], SCALE, None, ALU.mult)
                    link(v.scalar_tensor_tensor(soft[:, par, :, P:2 * P], banks[:, :, P:2 * P], SCALE,
                                                bias[:, 2 * hp:2 * hp + 2, :], ALU.mult, ALU.add))
                    v.tensor_reduce(mstat[:, par, 0, 0:4:2], soft[:, par, :, 0:P], AX_X, ALU.max)
                    link(v.tensor_reduce(mstat[:, par, 0, 1:4:2], soft[:, par, :, P:3 * P], AX_X, ALU.max))
                    v.tensor_scalar(mstat[:, par, 1, :], mstat[:, par, 0, :], -1.0, None, ALU.mult).then_inc(s_max, 1)

                def normalise(hp):
                    par = hp % 2
                    v.wait_ge(s_exp, 4 * hp + 4)
                    link(v.reciprocal(mstat[:, par, 0, :], mstat[:, par, 2, :]))
                    for part, (a, b) in enumerate(((0, P), (P, 3 * P))):
                        r = mstat[:, par, 0, part:4:2].unsqueeze(2).to_broadcast([P, 2, b - a])
                        ins = v.tensor_tensor(soft[:, par, :, a:b], soft[:, par, :, a:b], r, ALU.mult)
                    ins.then_inc(s_prob, 1)

                def copy_output(hp):
                    v.wait_ge(s_o, hp + 1)
                    v.tensor_copy(oT[:, hp, :], ps[:, 6 + hp % 2, 0:T]).then_inc(s_os, 1)

                scale_bias_max(0)
                for hp in range(PAIRS):
                    if hp + 1 < PAIRS:
                        scale_bias_max(hp + 1)
                    normalise(hp)
                    if hp >= 1:
                        copy_output(hp - 1)
                copy_output(PAIRS - 1)
                residual_from_banks(s_wmu, WM_AT[("wo", 0)], mod(l, 2), 0)

            def mixer_fourier(l):
                for b in range(1, 8, 2):
                    v.wait_ge(s_f1, b + 1)
                    v.tensor_copy(ftok[:, b // 4, b % 4, :], ps[:, b, :]).then_inc(s_f1o, 1)
                residual_from_banks(s_wmu, WM_AT[("four", 0)], mod(l, 2), 0)

            def router(l):
                v.wait_ge(s_sig, l + 1)
                sc = r_sc[:, :, :]
                link(v.tensor_tensor(r_sel[:, :, :].rearrange("p (s g) e -> p s (g e)", s=NSEQ), sc,
                                     rb[:, :].unsqueeze(1).to_broadcast([P, NSEQ, E]), ALU.add))
                sel = r_sel[:, :, :]
                at = 0
                for i in range(3):
                    m = 3 - i
                    ins = v.tensor_tensor(r_pair[:, :, at:at + m], sel[:, :, i:i + 1].to_broadcast([P, NSEQ * NG, m]),
                                          sel[:, :, i + 1:4], ALU.add)
                    at += m
                link(ins)
                gs = r_gs[:, :, :].rearrange("p s g -> p (s g)")
                link(v.tensor_reduce(gs, r_pair[:, :, :], AX_X, ALU.max))

                def rank(out, val, n):
                    vi = val.unsqueeze(3).to_broadcast([P, n, 4, 4])
                    vj = val.unsqueeze(2).to_broadcast([P, n, 4, 4])
                    ge = r_ge[:, 0:n, :].rearrange("p n (i j) -> p n i j", i=4)
                    gt = r_gt[:, 0:n, :].rearrange("p n (i j) -> p n i j", i=4)
                    v.tensor_tensor(ge, vj, vi, ALU.is_ge)
                    link(v.tensor_tensor(gt, vj, vi, ALU.is_gt))
                    v.tensor_tensor(r_ge[:, 0:n, :], r_ge[:, 0:n, :], before.unsqueeze(1).to_broadcast([P, n, 16]), ALU.mult)
                    link(v.tensor_tensor(r_gt[:, 0:n, :], r_gt[:, 0:n, :], after.unsqueeze(1).to_broadcast([P, n, 16]), ALU.mult))
                    link(v.tensor_tensor(r_ge[:, 0:n, :], r_ge[:, 0:n, :], r_gt[:, 0:n, :], ALU.add))
                    link(v.tensor_reduce(out, ge, AX_X, ALU.add))

                best = r_best[:, :]
                rank(best.rearrange("p (s g) -> p s g", s=NSEQ), r_gs[:, :, :], NSEQ)
                link(v.tensor_scalar(best, best, 0.0, None, ALU.is_equal))
                rank(r_rank[:, :, :], sel, NSEQ * NG)
                link(v.tensor_scalar(r_rank[:, :, :], r_rank[:, :, :], 2.0, None, ALU.is_lt))
                mask = r_mask[:, :, :]
                v.tensor_tensor(mask.rearrange("p s (g e) -> p (s g) e", e=GROUP), r_rank[:, :, :],
                                best.unsqueeze(2).to_broadcast([P, NSEQ * NG, GROUP]), ALU.mult).then_inc(s_mask, 1)
                v.wait_ge(s_mask, l + 1)
                link(v.tensor_tensor(r_w[:, :, :], sc, mask, ALU.mult))
                link(v.tensor_reduce(r_den[:, :], r_w[:, :, :], AX_X, ALU.add))
                link(v.reciprocal(r_den[:, :], r_den[:, :]))
                for s in range(NSEQ):
                    v.tensor_scalar(gx[:, :, s, :], r_w[:, s, :].rearrange("p (g e) -> p g e", g=NG),
                                    r_den[:, s:s + 1], None, ALU.mult)
                for b in range(4):
                    v.wait_ge(s_thi, 4 * l + b + 1)
                    piece = (slice(None), b // 2, slice((b % 2) * 512, (b % 2 + 1) * 512))
                    v.tensor_tensor(h_lo[piece], ps[:, b, :], h_hi[piece].bitcast(F32), ALU.subtract).then_inc(s_tlo, 1)
                v.wait_ge(s_pos, l + 1)
                pm = r_pm[:, :, :, :]
                link(v.scalar_tensor_tensor(pm.rearrange("p s g e -> p s (g e)"),
                                            ps[:, B_M, 0:2 * E].rearrange("p (s e) -> p s e", s=NSEQ),
                                            1.0, mask, ALU.add, ALU.mult))
                for r in range(MAX_ROUNDS):
                    v.tensor_scalar(posx[:, r * NG:(r + 1) * NG, :, :], pm.rearrange("p s g e -> p g s e"),
                                    -1.0 - SLOTS * r, None, ALU.add)
                link(v.tensor_reduce(r_cnt[:, 0:1], ps[:, B_M, 2 * E:3 * E], AX_X, ALU.max))
                link(v.tensor_tensor(r_cnt[:, 1:4], r_cnt[:, 0:1].to_broadcast([P, 3]), limits, ALU.is_gt))
                link(v.tensor_reduce(r_cnt[:, 4:5], r_cnt[:, 1:4], AX_X, ALU.add))
                v.tensor_scalar(rounds[:, l:l + 1], r_cnt[:, 4:5], 1.0, None, ALU.add).then_inc(s_rounds, 1)
                v.wait_ge(s_rounds, l + 1)

            base = 0
            for l in range(DEPTH):
                norm(2 * l, n1g[:, l * DB:(l + 1) * DB], mod(l, 1), mod(l, 0))
                (mixer_pool, mixer_attention, mixer_fourier)[KINDS[l]](l)
                norm(2 * l + 1, n2g[:, l * DB:(l + 1) * DB], mod(l, 4), mod(l, 3))
                router(l)
                n = v.value_load(rounds[0:1, l:l + 1], min_val=1, max_val=MAX_ROUNDS)
                v.wait_ge(s_acc0, l + 1)
                with v.Fori(0, n * NG) as k:
                    it = v.snap(base + k)
                    it8 = v.snap(it * 8)
                    it48 = v.snap(it * NU)
                    g = v.snap(k & (NG - 1))

                    v.wait_ge(s_gc, it + GRANT)
                    pos = posx[:, :, :, :].rearrange("p k s e -> p (k s e)")[:, bass.ds(k * 8, 8)]
                    v.tensor_tensor(onehot[:, :, :, :].rearrange("p s e c -> p (s e) c"),
                                    iota.unsqueeze(1).to_broadcast([P, 8, P]),
                                    pos.unsqueeze(2).to_broadcast([P, 8, P]), ALU.is_equal).then_inc(s_oh, 1)
                    v.tensor_copy(gsel[:, :, :].rearrange("p s e -> p (s e)"),
                                  gx[:, :, :, :].rearrange("p g s e -> p (g s e)")[:, bass.ds(g * 8, 8)]).then_inc(s_oh, 1)

                    def ada(j):
                        if l < DEPTH - 1:
                            store_ada(l + 1, g * (4 * ADA_NB) + j * ADA_NB, it * 4 + (ADA_CHUNKS + j + 1))

                    def split_lo(u):
                        v.wait_ge(s_hi, it48 + (u + 1))
                        v.tensor_tensor(w_lo[:, u % RING, :], raw[:, (u // 2) % RAW, u % 2, :],
                                        w_hi[:, u % RING, :].bitcast(F32), ALU.subtract).then_inc(s_lo, 1)

                    def output_lo(e):
                        for b in range(2):
                            v.wait_ge(s_yhi, it8 + (2 * e + b + 1))
                            piece = (slice(None), e % 2, slice(b * 512, (b + 1) * 512))
                            v.scalar_tensor_tensor(y_lo[piece], ps[:, B_Y + b, :], gcol[:, e:e + 1],
                                                   y_hi[piece].bitcast(F32), ALU.mult, ALU.subtract).then_inc(s_ylo, 1)

                    def add_up(pair):
                        for q in range(4):
                            v.wait_ge(s_comb, it8 + (4 * pair + q + 1))
                            h = quarter(hT, q)
                            v.tensor_tensor(h, h, ps[:, B_A + q % 2, :].rearrange("p (d t) -> p d t", d=2),
                                            ALU.add).then_inc(s_acc, 1)

                    ada(0)
                    for db in range(1, DB, 2):
                        v.wait_ge(s_ga, it8 + (db + 1))
                        v.tensor_copy(xg[:, db, :, :].rearrange("p e (h s) -> p h e s", h=2),
                                      ps[:, B_A + 1, :].rearrange("p (h e s) -> p h e s", h=2, e=GROUP)).then_inc(s_god, 1)
                    v.wait_ge(s_gc, it + 1 + GRANT)
                    v.tensor_copy(gcol[:, :], ps[:, B_Y, 0:GROUP]).then_inc(s_gcs, 1)
                    for u in range(NU):
                        split_lo(u)
                        if u == END[("gu", 0)] + 1:
                            ada(1)
                        if u in AFTER_HIDDEN:
                            e = AFTER_HIDDEN[u]
                            v.wait_ge(s_silu, it * GROUP + (e + 1))
                            v.tensor_tensor(act[:, :], sg[:, :], ps[:, B_T, FB * SLOTS:2 * FB * SLOTS],
                                            ALU.mult).then_inc(s_prod, 1)
                            v.wait_ge(s_prod, it * GROUP + (e + 1) + GRANT)
                            v.wait_ge(s_unit, it48 + (RING + (END[("dn", e - 1)] + 1 if e else 0)))
                            a3 = act[:, :].rearrange("p (b s) -> p b s", b=FB)
                            v.tensor_copy(a_hl[:, :, 0:SLOTS], a3).then_inc(s_ahi, 1)
                            v.wait_ge(s_ahi, it * GROUP + (e + 1))
                            v.tensor_tensor(a_hl[:, :, SLOTS:2 * SLOTS], a3, a_hl[:, :, 0:SLOTS].bitcast(F32),
                                            ALU.subtract).then_inc(s_alo, 1)
                        if u in AFTER_DOWN:
                            output_lo(AFTER_DOWN[u])
                        if u == END[("gu", 3)] + 1:
                            add_up(0)
                        if u == NU - 2:
                            ada(2)
                    output_lo(GROUP - 1)
                    ada(3)
                    add_up(1)
                base = v.snap(base + n * NG)
                v.wait_ge(s_acc, base * 8 + GRANT)
                for q in range(4):
                    residual(lambda d, s: hT[:, 2 * q + d, s * SEQ:(s + 1) * SEQ], mod(l, 5), q)
            norm(2 * DEPTH, fing, None, None)

        @block.tensor
        def _(pe):
            pe.wait_ge(s_load, 16 * N_FIRST_LOADS)
            pe.transpose(ps[:, 4, 0:104], vrow[0:104, 0, :], ident[0:104, 0:104]).then_inc(s_rows, 1)
            for i in range(2):
                pe.transpose(ps[:, 5, 96 * i:96 * (i + 1)], vrow[0:96, 1 + i, :], ident[0:96, 0:96]).then_inc(s_rows, 1)
            for q in range(4):
                for d in range(2):
                    for s in range(NSEQ):
                        mm = pe.transpose(ps[:, q, (2 * d + s) * SEQ:(2 * d + s + 1) * SEQ],
                                          xio[:, s, (2 * q + d) * P:(2 * q + d + 1) * P], ident)
                mm.then_inc(s_xt, 1)

            def ada_chunk(slot, landed, stored):
                pe.wait_ge(s_ada_in[slot], landed)
                pe.wait_ge(s_adas, stored)
                for n in range(ADA_NB):
                    for b in range(DB):
                        mm = pe.matmul(ps[:, B_M, 2 * n:2 * n + 2], ada_in[:, slot, b, n * P:(n + 1) * P],
                                       cact[:, :, b], start=(b == 0), stop=(b == DB - 1))
                mm.then_inc(s_ada, 1)

            pe.wait_ge(s_cact, 1)
            for chunk in range(ADA_CHUNKS):
                ada_chunk(chunk % 2, 16 * (chunk // 2 + 1), chunk)

            def norm(n):
                for b in range(DB):
                    if b % 2 == 0:
                        pe.wait_ge(s_sq, 4 * n + b // 2 + 1)
                    mm = pe.matmul(ps[:, B_M, 0:T], ones, work[:, b, :], start=(b == 0), stop=(b == DB - 1))
                mm.then_inc(s_ss, 1)

            def router(l):
                n = 2 * l + 1
                for s in range(NSEQ):
                    for b in range(DB):
                        if s == 0 and b % 2 == 0:
                            pe.wait_ge(s_hq, 4 * n + b // 2 + 1)
                        mm = pe.matmul(ps[:, B_M, s * E:(s + 1) * E], hT[:, b, s * SEQ:(s + 1) * SEQ], rw[:, b, :],
                                       start=(b == 0), stop=(b == DB - 1))
                mm.then_inc(s_lg, 1)
                for b in range(4):
                    s, half = b // 2, b % 2
                    for i in range(4):
                        mm = pe.transpose(ps[:, b, i * P:(i + 1) * P], hT[:, 4 * half + i, s * SEQ:(s + 1) * SEQ], ident)
                    mm.then_inc(s_tok, 1)
                pe.wait_ge(s_mask, l + 1)
                pe.matmul(ps[:, B_M, 0:E], tri, r_mask[:, 0, :], start=True, stop=True)
                pe.matmul(ps[:, B_M, E:2 * E], ones, r_mask[:, 0, :], start=True, stop=False)
                pe.matmul(ps[:, B_M, E:2 * E], tri, r_mask[:, 1, :], start=False, stop=True)
                pe.matmul(ps[:, B_M, 2 * E:3 * E], ones, r_mask[:, 0, :], start=True, stop=False)
                pe.matmul(ps[:, B_M, 2 * E:3 * E], ones, r_mask[:, 1, :], start=False, stop=True).then_inc(s_pos, 1)

            def mixer_pool(l):
                pe.wait_ge(s_kc, KC_AFTER[l])
                for g in range(4):
                    pe.wait_ge(s_pt, 4 * (l // 3) + g + 1)
                    for d in range(2):
                        for b in range(2):
                            mm = pe.matmul(ps[:, g, d * T:(d + 1) * T], wp[:, g, b, d * P:(d + 1) * P],
                                           poolT[:, 2 * g + b, :], start=(b == 0), stop=(b == 1))
                    mm.then_inc(s_mix, 1)

            def mixer_attention(l):
                pe.wait_ge(s_kc, KC_AFTER[l])
                pe.wait_ge(s_ms, 2 * l + 1)
                pe.wait_ge(s_bias, 16 * 6)
                rows = oT[:, :, :].rearrange("p d t -> p (d t)")
                for b in range(4):
                    pe.matmul(ps[:, 4 + b, :], kattn[:, 1, :], rows[:, b * 512:(b + 1) * 512],
                              start=True, stop=True).then_inc(s_flip, 1)
                for t in range(12):
                    n = WM_AT[("qkv", t)]
                    if t == 0:
                        pe.wait_ge(s_hq, 4 * (2 * l) + 4)
                    pe.wait_ge(s_wm[n % WM_RING], 16 * (n // WM_RING + 1))
                    if t >= 4:
                        if t % 2 == 0:
                            pe.wait_ge(s_qkve, (t - 4) // 2 + 1)
                        else:
                            pe.wait_ge(s_qkvo, (t - 5) // 2 + 1)
                    for d in range(2):
                        for b in range(DB):
                            if t < 8:
                                lhs, rhs = wm[:, n % WM_RING, b, d * P:(d + 1) * P], hT[:, b, :]
                            else:
                                lhs, rhs = hT[:, b, d * SEQ:(d + 1) * SEQ], wm[:, n % WM_RING, b, :]
                            mm = pe.matmul(ps[:, t % 4, d * T:(d + 1) * T], lhs, rhs, start=(b == 0), stop=(b == DB - 1))
                    mm.then_inc(s_wmu, 1)
                pe.wait_ge(s_biass, 4)
                for b in range(4):
                    for i in range(4):
                        j = 4 * (b % 2) + i
                        src = ck[:, j * P:(j + 1) * P] if b < 2 else kT[:, j, 0:SEQ]
                        if b == 2 and i == 0:
                            pe.wait_ge(s_qkve, 4)
                            pe.wait_ge(s_qkvo, 4)
                        mm = pe.transpose(ps[:, 4 + b, i * P:(i + 1) * P], src, ident)
                    mm.then_inc(s_kt, 1)
                pe.wait_ge(s_kts, 4)
                pe.wait_ge(s_qkve, 6)
                pe.wait_ge(s_qkvo, 6)

                def scores(hp):
                    if hp >= 2:
                        pe.wait_ge(s_max, hp - 1)
                    for e in range(2):
                        rows = slice(e * HD, (e + 1) * HD)
                        bank = ps[:, 2 * (hp % 2) + e, :]
                        q_ctx, q_lat = work[rows, hp, 0:SEQ], work[rows, hp, SEQ:T]
                        pe.matmul(bank[:, 0:P], q_ctx, kT[rows, hp, 0:SEQ], start=True, stop=True)
                        pe.matmul(bank[:, P:2 * P], q_lat, kT[rows, hp, SEQ:T], start=True, stop=True)
                        mm = pe.matmul(bank[:, 2 * P:3 * P], q_lat, ckT[rows, hp, :], start=True, stop=True)
                    mm.then_inc(s_sc, 1)

                def turn(hp):
                    pe.wait_ge(s_prob, hp + 1)
                    if hp >= 1:
                        pe.wait_ge(s_pts, hp)
                    for e in range(2):
                        for i in range(3):
                            mm = pe.transpose(ps[:, 4 + e, i * P:(i + 1) * P], soft[:, hp % 2, e, i * P:(i + 1) * P], ident)
                    mm.then_inc(s_pt2, 1)

                def attend(hp):
                    pe.wait_ge(s_pts, hp + 1)
                    if hp >= 2:
                        pe.wait_ge(s_os, hp - 1)
                    for e in range(2):
                        cols = slice((2 * hp + e) * HD, (2 * hp + e + 1) * HD)
                        out = ps[e * HD:(e + 1) * HD, 6 + hp % 2, :]
                        p = pT[:, hp % 2, e, :]
                        pe.matmul(out[:, 0:SEQ], vtok[:, 0, cols], p[:, 0:P], start=True, stop=True)
                        pe.matmul(out[:, SEQ:T], vtok[:, 1, cols], p[:, P:2 * P], start=True, stop=False)
                        mm = pe.matmul(out[:, SEQ:T], cv[:, cols], p[:, 2 * P:3 * P], start=False, stop=True)
                    mm.then_inc(s_o, 1)

                scores(0)
                scores(1)
                for hp in range(PAIRS):
                    turn(hp)
                    if hp + 2 < PAIRS:
                        scores(hp + 2)
                    attend(hp)
                pe.wait_ge(s_os, PAIRS)
                out_project("wo", oT, 0)

            def out_project(name, src, first_bank):
                for i in range(4):
                    n = WM_AT[(name, i)]
                    pe.wait_ge(s_wm[n % WM_RING], 16 * (n // WM_RING + 1))
                    for d in range(2):
                        for b in range(DB):
                            mm = pe.matmul(ps[:, first_bank + i, d * T:(d + 1) * T], wm[:, n % WM_RING, b, d * P:(d + 1) * P],
                                           src[:, b, :], start=(b == 0), stop=(b == DB - 1))
                    mm.then_inc(s_wmu, 1)

            def mixer_fourier(l):
                pe.wait_ge(s_kc, KC_AFTER[l])
                chan = kfour[:, 2 * P:].rearrange("p (b n) -> p b n", b=2)
                for b8 in range(8):
                    s, g = b8 // 4, b8 % 4
                    pe.wait_ge(s_hq, 4 * (2 * l) + g + 1)
                    for b in range(2):
                        mm = pe.matmul(ps[:, b8, :], hT[:, 2 * g + b, s * SEQ:(s + 1) * SEQ], chan[:, b, :],
                                       start=(b == 0), stop=(b == 1))
                    mm.then_inc(s_f1, 1)
                pe.wait_ge(s_f1e, 4)
                pe.wait_ge(s_f1o, 4)
                for g in range(4):
                    for d in range(2):
                        for s in range(NSEQ):
                            out = ps[:, g, (2 * d + s) * SEQ:(2 * d + s + 1) * SEQ]
                            pe.matmul(out, ftok[:, s, g, d * P:(d + 1) * P], kfour[:, 0:P], start=True, stop=False)
                            mm = pe.matmul(out, ftok[:, s, g, 256 + d * P:256 + (d + 1) * P], kfour[:, P:2 * P],
                                           start=False, stop=True)
                    mm.then_inc(s_f2, 1)
                pe.wait_ge(s_f2s, 4)
                out_project("four", fT, 0)

            base = 0
            for l in range(DEPTH):
                if l > 0:
                    pe.wait_ge(s_adas, base * 4 + ADA_CHUNKS)
                else:
                    pe.wait_ge(s_adas, ADA_CHUNKS)
                norm(2 * l)
                (mixer_pool, mixer_attention, mixer_fourier)[KINDS[l]](l)
                norm(2 * l + 1)
                pe.wait_ge(s_ms, 2 * l + 2)
                router(l)
                pe.wait_ge(s_rounds, l + 1)
                pe.wait_ge(s_tlo, 4 * l + 4)
                n = pe.value_load(rounds[0:1, l:l + 1], min_val=1, max_val=MAX_ROUNDS)
                with pe.Fori(0, n * NG) as k:
                    it = pe.snap(base + k)
                    it4 = pe.snap(it * 4)
                    it8 = pe.snap(it * 8)
                    it48 = pe.snap(it * NU)

                    def ada(j):
                        if l < DEPTH - 1:
                            ada_chunk(j % 2, it * 32 + 16 * (ADA_CHUNKS // 2 + j // 2 + 1), it4 + (ADA_CHUNKS + j))

                    def gather():
                        pe.wait_ge(s_oh, it * 2 + 2)
                        for db in range(DB):
                            if db < 2:
                                pe.wait_ge(s_acc, it8 + GRANT)
                            elif db % 2 == 0:
                                pe.wait_ge(s_gev, it4 + db // 2)
                            else:
                                pe.wait_ge(s_god, it4 + db // 2)
                            for half, h in enumerate((h_hi, h_lo)):
                                for s in range(NSEQ):
                                    mm = pe.matmul(ps[:, B_A + db % 2, half * 256:(half + 1) * 256],
                                                   h[:, s, db * P:(db + 1) * P], onehot[:, s, :, 0:SLOTS],
                                                   start=(s == 0), stop=(s == NSEQ - 1))
                            mm.then_inc(s_ga, 1)
                        for e in range(GROUP):
                            if e == 0:
                                pe.wait_ge(s_gev, it4 + 4)
                            if e == 2:
                                pe.wait_ge(s_god, it4 + 4)
                            for s in range(NSEQ):
                                at = (e % 2) * T + s * SEQ
                                mm = pe.transpose(ps[:, B_A + e // 2, at:at + SEQ], onehot[:, s, e, :].bitcast(F32), ident)
                            if e % 2:
                                mm.then_inc(s_oht, 1)
                        pe.wait_ge(s_ylo, it8 + GRANT)
                        for e in range(GROUP):
                            for s in range(NSEQ):
                                mm = pe.matmul(ps[:, B_Y, e:e + 1], onehot[:, s, e, :].bitcast(F32), gsel[:, s, e:e + 1],
                                               start=(s == 0), stop=(s == NSEQ - 1))
                        mm.then_inc(s_gc, 1)

                    def gate_up(e):
                        if e == 0:
                            pe.wait_ge(s_gev, it4 + 4)
                            pe.wait_ge(s_god, it4 + 4)
                        pe.wait_ge(s_gus, it8 + 2 * e + GRANT)
                        for b in range(DB):
                            u = FIRST[("gu", e)] + b
                            pe.wait_ge(s_lo, it48 + (u + 1 + RAW_CREDIT))
                            for w, first in ((w_hi, True), (w_lo, False)):
                                for n2 in range(2):
                                    mm = pe.matmul(ps[:, B_G + n2, :], xg[:, b, e, :], w[:, u % RING, n2 * F:(n2 + 1) * F],
                                                   start=(b == 0 and first), stop=(b == DB - 1 and not first))
                            mm.then_inc(s_unit, 1)

                    def turn(e):
                        pe.wait_ge(s_gus, it8 + (2 * e + 2) + GRANT)
                        pe.wait_ge(s_prod, it4 + e + GRANT)
                        for i in range(2 * FB):
                            mm = pe.matmul(ps[:, B_T, i * SLOTS:(i + 1) * SLOTS], gu[:, i * P:(i + 1) * P], halves,
                                           start=True, stop=True)
                        mm.then_inc(s_turn, 1)

                    def down(e):
                        pe.wait_ge(s_alo, it4 + (e + 1))
                        pe.wait_ge(s_ylo, it8 + 2 * e + GRANT)
                        if e == 0:
                            pe.wait_ge(s_gcs, it + 1)
                        for b in range(FB):
                            u = FIRST[("dn", e)] + b
                            pe.wait_ge(s_lo, it48 + (u + 1 + RAW_CREDIT))
                            for w, first in ((w_hi, True), (w_lo, False)):
                                for n2 in range(2):
                                    mm = pe.matmul(ps[:, B_Y + n2, :], a_hl[:, b, :], w[:, u % RING, n2 * 512:(n2 + 1) * 512],
                                                   start=(b == 0 and first), stop=(b == FB - 1 and not first))
                            mm.then_inc(s_unit, 1)

                    def combine(pair):
                        pe.wait_ge(s_ylo, it8 + (4 * pair + 4) + GRANT)
                        if pair == 0:
                            pe.wait_ge(s_ohs, it * 2 + 2)
                        for q in range(4):
                            c = 4 * pair + q
                            if c >= 2:
                                pe.wait_ge(s_acc, it8 + (c - 1) + GRANT)
                            for d in range(2):
                                n2 = 0
                                for e in range(2):
                                    for y in (y_hi, y_lo):
                                        mm = pe.matmul(ps[:, B_A + q % 2, d * T:(d + 1) * T],
                                                       y[:, e, (2 * q + d) * P:(2 * q + d + 1) * P],
                                                       onehotT[:, 2 * pair + e, :], start=(n2 == 0), stop=(n2 == 3))
                                        n2 += 1
                            mm.then_inc(s_comb, 1)

                    ada(0)
                    gather()
                    gate_up(0)
                    ada(1)
                    turn(0)
                    gate_up(1)
                    down(0)
                    turn(1)
                    gate_up(2)
                    down(1)
                    turn(2)
                    gate_up(3)
                    combine(0)
                    down(2)
                    turn(3)
                    ada(2)
                    down(3)
                    ada(3)
                    combine(1)
                base = pe.snap(base + n * NG)
            norm(2 * DEPTH)
            for b in range(4):
                s, half = b // 2, b % 2
                for i in range(4):
                    if s == 0:
                        pe.wait_ge(s_hq, 4 * 2 * DEPTH + (4 * half + i) // 2 + 1)
                    mm = pe.transpose(ps[:, b, i * P:(i + 1) * P], hT[:, 4 * half + i, s * SEQ:(s + 1) * SEQ], ident)
                mm.then_inc(s_yt, 1)


_INS = ["x_prompt", "x_sample", "cache_k", "cache_v", "c", "c_ctx", "ada_w", "ada_b", "norm1_g", "norm2_g", "pool_w",
        "pool_scale", "attn_wqkv", "attn_wo", "attn_rpb", "fourier_w", "router_w", "router_b", "moe_w_gate", "moe_w_up",
        "moe_w_down", "final_norm_g"]
_OUTS = [((1, 128, 1024), "float32"), ((1, 128, 1024), "float32"),
         ((1, 1, 128, 16, 64), "float32"), ((1, 1, 128, 16, 64), "float32")]


def kernel(**inputs):
    import numpy as _np
    import concourse.bacc as _bacc
    from concourse import mybir as _mybir
    from concourse.bass_utils import run_bass_kernel_spmd as _run

    nc = _bacc.Bacc("TRN2", target_bir_lowering=False, num_devices=1)
    arrays, args = {}, []
    given = {name: _np.ascontiguousarray(inputs[name]) for name in _INS}
    given.update(host_constants())
    for name, a in given.items():
        arrays[f"in_{name}_dram"] = a
        args.append(nc.dram_tensor(f"in_{name}_dram", a.shape, _mybir.dt.from_np(a.dtype), kind="ExternalInput").ap())
    for i, (shape, dtype) in enumerate(_OUTS):
        dt = _mybir.dt.from_np(_np.dtype(dtype))
        args.append(nc.dram_tensor(f"out_{i}_dram", shape, dt, kind="ExternalOutput").ap())
    build(nc, *args)
    r = _run(nc, [arrays], core_ids=[0])
    return tuple(r.results[0][f"out_{i}_dram"] for i in range(len(_OUTS)))
```

```python
from contextlib import ExitStack

import numpy as np

import concourse.bass as bass
from concourse import mybir

F32 = mybir.dt.float32
F32R = mybir.dt.float32r
I32 = mybir.dt.int32
ALU = mybir.AluOpType
ACT = mybir.ActivationFunctionType
AX_X = mybir.AxisListType.X

P = 128
D = 1024
DB = D // P
SEQ = 128
NSEQ = 2
T = NSEQ * SEQ
DEPTH = 4
HEADS = 16
HD = 64
PAIRS = HEADS // 2
E = 16
GROUP = 4
NG = E // GROUP
F = 512
FB = F // P
SLOTS = 64
MAX_ROUNDS = T // SLOTS
EPS = 1e-6
SCALE = HD ** -0.5
GRID_W = 64
WIN_ROWS, WIN_COLS = 8, 16
MASKED = -1e30

BLOCKS = [("gu", 0), ("gu", 1), ("dn", 0), ("gu", 2), ("dn", 1), ("gu", 3), ("dn", 2), ("dn", 3)]
UNITS = [(kind, e, i) for kind, e in BLOCKS for i in range(DB if kind == "gu" else FB)]
NU = len(UNITS)
FIRST = {b: UNITS.index((b[0], b[1], 0)) for b in BLOCKS}
END = {b: FIRST[b] + (DB if b[0] == "gu" else FB) - 1 for b in BLOCKS}
RAW = 6
PAIR_LOADS = NU // 2
RING = 6
GRANT = 1
RAW_CREDIT = 2 * RAW

END_GU = [END[("gu", e)] for e in range(GROUP)]
END_DN = [END[("dn", e)] for e in range(GROUP)]
GU_COPIED = {END_GU[e] + 4: e for e in range(GROUP)}
PE_TURN = {END_GU[0] + 3: 0, END_GU[1] + 2: 1, END_GU[2] + 2: 2, END_GU[3] + 2: 3}
SILU = {END_GU[0] + 7: 0, END_GU[1] + 6: 1, END_GU[2] + 6: 2, END_GU[3] + 6: 3}
HIDDEN = {END_GU[0] + 6: 0, END_GU[1] + 5: 1, END_GU[2] + 5: 2, END_GU[3] + 5: 3}
LAST_HI, LAST_LO = 4, 3
OUTPUT_HI = {END_DN[0] + 4: 0, END_DN[1] + 4: 1, END_DN[2] + 3: 2}
OUTPUT_LO = {END_DN[0] + 3: 0, END_DN[1] + 3: 1, END_DN[2] + 2: 2}
PE_COMBINE_LAST = {5 + q: q for q in range(4)}
ADD_LAST = {7 + q: q for q in range(4)}
PE_COMBINE_FIRST = {END_DN[1] + 4 + q: q for q in range(4)}
ADD_FIRST = {END_DN[1] + 6 + q: q for q in range(4)}
PE_ONEHOT_TURN, PE_GATES = 12, 13
ONEHOT_COPIED, GATES_COPIED = 16, 15
NEXT_ONEHOT = 24
PE_GATHER = {NU - 7: [0], NU - 6: [1], NU - 5: [2, 3], NU - 4: [4], NU - 3: [5], NU - 2: [6], NU - 1: [7]}
GATHERED = {NU - 3: [0], NU - 2: [1], NU - 1: [2, 3]}
GATHERED_LATE = {0: 4, 1: 5, 2: 6, 3: 7}
FIRST_GATHER_BANKS = [2, 3, 4, 7, 5, 6, 5, 6]

ADA_COLS = 256
ADA_NB = ADA_COLS // P
ADA_CHUNKS = 6 * D // ADA_COLS
ADA_PER = ADA_CHUNKS // NG
ADA_SLOTS = 2
PE_ADA = {7: 0, 15: 1, 22: 2, 28: 3, 34: 4, 40: 5}
PE_ADA_TURN = {11: 0, 18: 1, 25: 2, 31: 3, 37: 4, 43: 5}
ADA_COPIED = {11: 0, 18: 1, 25: 2, 31: 3, 37: 4, 43: 5}
ADA_STORED = {13: 0, 20: 1, 27: 2, 33: 3, 39: 4, 45: 5}
ADA_LOADED = {0: 0, 4: 1, 12: 2, 15: 3, 19: 4, 22: 5}
MOD_CHUNKS = D // ADA_COLS
MOD_BANK = [4, 5, 6, 5, 6, 4]
NB_MOD = 6 * DB

C_IDENT, C_TRI, C_ONES, C_HALVES, C_IOTA = 0, 128, 256, 384, 448
C_LIMITS, C_BEFORE, C_AFTER, C_END = 576, 579, 595, 611
WM_COLS = 256
WM_RING = 3


def host_constants():
    i = np.arange(P)
    base = np.zeros((P, C_END), np.float32)
    base[:, C_IDENT:C_IDENT + P] = np.eye(P)
    base[:, C_TRI:C_TRI + P] = i[:, None] < i[None, :]
    base[:, C_ONES:C_ONES + P] = 1.0
    base[:, C_HALVES:C_HALVES + SLOTS] = (i[:, None] % SLOTS) == np.arange(SLOTS)[None, :]
    base[:, C_IOTA:C_IOTA + P] = (i % SLOTS)[None, :]
    base[:, C_LIMITS:C_LIMITS + 3] = SLOTS * np.arange(1, 4)[None, :]
    j = np.arange(GROUP)
    base[:, C_BEFORE:C_BEFORE + 16] = (j[None, :] < j[:, None]).reshape(1, 16)
    base[:, C_AFTER:C_AFTER + 16] = (j[None, :] > j[:, None]).reshape(1, 16)
    pool = np.zeros((P, 4, P), np.float32)
    for g, win in enumerate((2, 4, 8, 16)):
        lo = np.clip(i - win // 2, 0, SEQ)
        hi = np.clip(i - win // 2 + win, 0, SEQ)
        inside = (i[:, None] >= lo[None, :]) & (i[:, None] < hi[None, :])
        pool[:, g, :] = inside / (hi - lo)[None, :] - np.eye(P)
    attn = np.zeros((P, 2, P), np.float32)
    cq = i % GRID_W
    start = np.clip(cq - WIN_COLS // 2, 0, GRID_W - WIN_COLS)
    ok = (cq[None, :] >= start[:, None]) & (cq[None, :] < start[:, None] + WIN_COLS)
    attn[:, 0, :] = np.where(ok, 0.0, MASKED)
    attn[i, 1, (i // GRID_W) * GRID_W + GRID_W - 1 - cq] = 1.0
    four = np.zeros((P, 2 * P + 2 * 512), np.float32)
    wn = 2 * np.pi * np.outer(i, i) / SEQ
    four[:, 0:P] = np.cos(wn) / np.sqrt(SEQ)
    four[:, P:2 * P] = -np.sin(wn) / np.sqrt(SEQ)
    c = np.arange(256)
    wc = 2 * np.pi * np.outer(c, c) / 256
    both = np.concatenate([np.cos(wc), np.sin(wc)], axis=1) / 16.0
    four[:, 2 * P:] = both.reshape(2, P, 512).transpose(1, 0, 2).reshape(P, 1024)
    return {"k_base": base, "k_pool": pool.reshape(P, 512), "k_attn": attn.reshape(P, 256), "k_four": four}


def build(nc, x_prompt, x_sample, cache_k, cache_v, c, c_ctx, ada_w, ada_b, norm1_g, norm2_g, pool_w,
          pool_scale, attn_wqkv, attn_wo, attn_rpb, fourier_w, router_w, router_b, moe_w_gate, moe_w_up,
          moe_w_down, final_norm_g, k_base, k_pool, k_attn, k_four,
          y_prompt, y_sample, new_cache_k, new_cache_v):
    ctx = ExitStack()
    with ctx:
        def sb(name, shape, dt=F32, stack=ctx):
            return stack.enter_context(nc.sbuf_tensor(name, shape, dt))

        def sem(name):
            return ctx.enter_context(nc.semaphore(name))

        xT = sb("xT", [P, DB, T])
        hT = sb("hT", [P, DB, T])
        raw = sb("raw", [P, RAW, 2, D])
        ada_in = sb("ada_in", [P, ADA_SLOTS, DB, ADA_COLS])
        const = sb("const", [P, C_END])
        mods = sb("mods", [P, DEPTH, NB_MOD, NSEQ])
        vecs = sb("vecs", [P, 104])
        adab = sb("adab", [P, DEPTH * NB_MOD])
        ada_row = sb("ada_row", [P, ADA_COLS])
        cact = sb("cact", [P, NSEQ, DB])
        rw = sb("rw", [P, DB, E])
        rb = sb("rb", [P, E])
        amul = sb("amul", [P, DB, NSEQ])
        pcoef = sb("pcoef", [P, DB, NSEQ])
        ms = sb("ms", [P, T])
        rstd = sb("rstd", [P, T])
        newton = sb("newton", [P, T])
        posx = sb("posx", [P, MAX_ROUNDS * NG + 1, NSEQ, GROUP])
        gx = sb("gx", [P, NG, NSEQ, GROUP])
        rounds = sb("rounds", [P, DEPTH], I32)
        credit = sb("credit", [P, 8])

        ident = const[:, C_IDENT:C_IDENT + P]
        tri = const[:, C_TRI:C_TRI + P]
        ones = const[:, C_ONES:C_ONES + P]
        halves = const[:, C_HALVES:C_HALVES + SLOTS]
        iota = const[:, C_IOTA:C_IOTA + P]
        limits = const[:, C_LIMITS:C_LIMITS + 3]
        before = const[:, C_BEFORE:C_BEFORE + 16]
        after = const[:, C_AFTER:C_AFTER + 16]
        cond = vecs[:, 0:16]
        n1g, n2g = vecs[:, 16:48], vecs[:, 48:80]
        fing, pscale = vecs[:, 80:88], vecs[:, 88:104]

        with ExitStack() as moe:
            w_hi = sb("w_hi", [P, RING, D], F32R, moe)
            w_lo = sb("w_lo", [P, RING, D], F32R, moe)
            xg = sb("xg", [P, DB, GROUP, 2 * SLOTS], F32R, moe)
            h_hi = sb("h_hi", [P, NSEQ, D], F32R, moe)
            h_lo = sb("h_lo", [P, NSEQ, D], F32R, moe)
            y_hi = sb("y_hi", [P, 2, D], F32R, moe)
            y_lo = sb("y_lo", [P, 2, D], F32R, moe)
            onehot = sb("onehot", [P, NSEQ, GROUP, 2 * SLOTS], F32R, moe)
            onehotT = sb("onehotT", [P, GROUP, T], F32R, moe)
            gsel = sb("gsel", [P, NSEQ, GROUP], F32, moe)
            gcol = sb("gcol", [P, GROUP], F32, moe)
            gu = sb("gu", [P, 2 * F], F32, moe)
            sg = sb("sg", [P, FB * SLOTS], F32, moe)
            act = sb("act", [P, FB * SLOTS], F32, moe)
            a_hl = sb("a_hl", [P, FB, 2 * SLOTS], F32R, moe)
        with ExitStack() as mix:
            work = sb("work", [P, DB, T], F32, mix)
            wm = sb("wm", [P, WM_RING, DB, WM_COLS], F32, mix)
            kT = sb("kT", [P, DB, T], F32, mix)
            vtok = sb("vtok", [P, NSEQ, D], F32, mix)
            ck = sb("ck", [P, D], F32, mix)
            cv = sb("cv", [P, D], F32, mix)
            ckT = sb("ckT", [P, DB, SEQ], F32, mix)
            knew = sb("knew", [P, D], F32, mix)
            bias = sb("bias", [P, HEADS, P], F32, mix)
            oT = sb("oT", [P, DB, T], F32, mix)
            soft = sb("soft", [P, 2, 2, 3 * P], F32, mix)
            pT = sb("pT", [P, 2, 2, 3 * P], F32, mix)
            kattn = sb("kattn", [P, 2, P], F32, mix)
            mstat = sb("mstat", [P, 2, 3, 4], F32, mix)
            rpad = sb("rpad", [HEADS, 3, P], F32, mix)
        with ExitStack() as mix2:
            work2 = sb("work2", [P, DB, T], F32, mix2)
            ada_rows = sb("ada_rows", [NSEQ, 6 * D], F32, mix2)
            ztok = sb("ztok", [P, 4, NSEQ, 256], F32, mix2)
            kpool = sb("kpool", [P, 4, P], F32, mix2)
            wp = sb("wp", [P, 4, 2, 256], F32, mix2)
        with ExitStack() as mix3:
            sb("work3", [P, DB, T], F32, mix3)
            sb("wm3", [P, WM_RING, DB, WM_COLS], F32, mix3)
            ftok = sb("ftok", [P, NSEQ, 4, 512], F32, mix3)
            fT = sb("fT", [P, DB, T], F32, mix3)
            kfour = sb("kfour", [P, 2 * P + 1024], F32, mix3)
        with ExitStack() as mix4:
            sb("work4", [P, DB, T], F32, mix4)
            sb("wm4", [P, WM_RING, DB, WM_COLS], F32, mix4)
            xio = sb("xio", [P, NSEQ, D], F32, mix4)
            vrow = sb("vrow", [P, 3, P], F32, mix4)
        with ExitStack() as rt:
            sb("rt_w_hi", [P, RING, D], F32R, rt)
            sb("rt_w_lo", [P, RING, D], F32R, rt)
            r_sc = sb("r_sc", [P, NSEQ, E], F32, rt)
            r_sel = sb("r_sel", [P, NSEQ * NG, GROUP], F32, rt)
            r_pair = sb("r_pair", [P, NSEQ * NG, 6], F32, rt)
            r_gs = sb("r_gs", [P, NSEQ, NG], F32, rt)
            r_ge = sb("r_ge", [P, NSEQ * NG, 16], F32, rt)
            r_gt = sb("r_gt", [P, NSEQ * NG, 16], F32, rt)
            r_best = sb("r_best", [P, NSEQ * NG], F32, rt)
            r_rank = sb("r_rank", [P, NSEQ * NG, GROUP], F32, rt)
            r_mask = sb("r_mask", [P, NSEQ, E], F32, rt)
            r_w = sb("r_w", [P, NSEQ, E], F32, rt)
            r_den = sb("r_den", [P, NSEQ], F32, rt)
            r_pm = sb("r_pm", [P, NSEQ, NG, GROUP], F32, rt)
            r_cnt = sb("r_cnt", [P, 8], F32, rt)
        ps = ctx.enter_context(nc.psum_tensor("ps", [P, 8, 512], F32))
        B_G, B_U, B_Y, B_T, B_A, B_M = 0, 1, 2, 4, 5, 7
        bias_dram = nc.dram_tensor("bias_rows", [HEADS, 3, P], F32, kind="Internal").ap()

        s_load = sem("s_load")
        s_rows = sem("s_rows")
        s_vecs = sem("s_vecs")
        s_cact = sem("s_cact")
        s_xt = sem("s_xt")
        s_xq = sem("s_xq")
        s_sq = sem("s_sq")
        s_ss = sem("s_ss")
        s_ms = sem("s_ms")
        s_rt = sem("s_rt")
        s_n1 = sem("s_n1")
        s_n2 = sem("s_n2")
        s_hq = sem("s_hq")
        s_link = sem("s_link")
        s_lg = sem("s_lg")
        s_sig = sem("s_sig")
        s_mask = sem("s_mask")
        s_pos = sem("s_pos")
        s_tok = sem("s_tok")
        s_thi = sem("s_thi")
        s_tlo = sem("s_tlo")
        s_rounds = sem("s_rounds")
        s_acc0 = sem("s_acc0")
        s_raw = [sem(f"s_raw{k}") for k in range(RAW)]
        s_issue = sem("s_issue")
        s_hi = sem("s_hi")
        s_lo = sem("s_lo")
        s_unit = sem("s_unit")
        s_oh = sem("s_oh")
        s_ga = sem("s_ga")
        s_gev = sem("s_gev")
        s_oht = sem("s_oht")
        s_ohs = sem("s_ohs")
        s_gc = sem("s_gc")
        s_gcs = sem("s_gcs")
        s_gus = sem("s_gus")
        s_turn = sem("s_turn")
        s_silu = sem("s_silu")
        s_prod = sem("s_prod")
        s_ahi = sem("s_ahi")
        s_alo = sem("s_alo")
        s_yhi = sem("s_yhi")
        s_ylo = sem("s_ylo")
        s_comb = sem("s_comb")
        s_acc = sem("s_acc")
        s_ada_in = [sem(f"s_ada_in{k}") for k in range(2)]
        s_ada = sem("s_ada")
        s_adac = sem("s_adac")
        s_adat = sem("s_adat")
        s_posx = sem("s_posx")
        s_adas = sem("s_adas")
        s_kc = sem("s_kc")
        s_z = sem("s_z")
        s_ze = sem("s_ze")
        s_zo = sem("s_zo")
        s_mix = sem("s_mix")
        s_wm = [sem(f"s_wm{k}") for k in range(WM_RING)]
        s_wmu = sem("s_wmu")
        s_qkve = sem("s_qkve")
        s_qkvo = sem("s_qkvo")
        s_bias = sem("s_bias")
        s_pad = sem("s_pad")
        s_flip = sem("s_flip")
        s_biass = sem("s_biass")
        s_kt = sem("s_kt")
        s_kts = sem("s_kts")
        s_sc = sem("s_sc")
        s_max = sem("s_max")
        s_exp = sem("s_exp")
        s_prob = sem("s_prob")
        s_pt2 = sem("s_pt2")
        s_pts = sem("s_pts")
        s_o = sem("s_o")
        s_os = sem("s_os")
        s_f1 = sem("s_f1")
        s_f1e = sem("s_f1e")
        s_f1o = sem("s_f1o")
        s_f2 = sem("s_f2")
        s_f2s = sem("s_f2s")
        s_yt = sem("s_yt")
        s_yts = sem("s_yts")
        s_out = sem("s_out")
        s_kv = sem("s_kv")

        KINDS = [l % 3 for l in range(DEPTH)]
        N_FIRST_LOADS = 13
        WM_TILES = [("qkv", i) for i in range(12)] + [("wo", i) for i in range(4)] + [("four", i) for i in range(4)]
        WM_AT = {t: n for n, t in enumerate(WM_TILES)}
        KC_AFTER = [32, 80, 96, 128]

        def quarter(t, q):
            return t[:, 2 * q:2 * q + 2, :]

        def per_token(v, q):
            return v[:, 2 * q:2 * q + 2, :].unsqueeze(3).to_broadcast([P, 2, NSEQ, SEQ])

        def by_seq(t):
            return t.rearrange("p d (s t) -> p d s t", s=NSEQ)

        def mod(l, n):
            return mods[:, l, n * DB:(n + 1) * DB, :]

        block = ctx.enter_context(nc.Block())

        @block.sync
        def _(sp):
            def load_ada(layer, chunk, slot):
                sp.dma_start(ada_in[:, slot, :, :],
                             ada_w[layer].rearrange("(b p) n -> p b n", p=P)[:, :, bass.ds(chunk * ADA_COLS, ADA_COLS)]
                             ).then_inc(s_ada_in[slot], 16)

            def load_units(l, e, q):
                kind, _, i = UNITS[2 * q]
                slot = q % RAW
                if kind == "gu":
                    rows = slice(i * P, (i + 2) * P)
                    for n, w in enumerate((moe_w_gate, moe_w_up)):
                        sp.dma_start(raw[:, slot, :, n * F:(n + 1) * F],
                                     w[l, e, rows, :].rearrange("(b p) f -> p b f", p=P)).then_inc(s_raw[slot], 16)
                else:
                    for n in range(2):
                        sp.dma_start(raw[:, slot, n, :],
                                     moe_w_down[l, e, (i + n) * P:(i + n + 1) * P, :]).then_inc(s_raw[slot], 16)

            for chunk in range(ADA_CHUNKS):
                if chunk >= 2:
                    sp.wait_ge(s_ada, chunk - 1)
                load_ada(0, chunk, chunk % 2)

            base = 0
            for l in range(DEPTH):
                def group(k):
                    it = base + k
                    g = k & (NG - 1)

                    def ada_chunk(j):
                        if l == DEPTH - 1:
                            return
                        sp.wait_ge(s_ada, ADA_CHUNKS - 1 + ADA_PER * it + j)
                        sp.sem_inc(s_issue, 1)
                        load_ada(l + 1, g * ADA_PER + j, j % ADA_SLOTS)

                    for q in range(PAIR_LOADS):
                        if q in ADA_LOADED:
                            ada_chunk(ADA_LOADED[q])
                        sp.wait_ge(s_lo, it * NU + 2 * q + 2)
                        sp.sem_inc(s_issue, 1)
                        load_units(l, g * GROUP + UNITS[2 * q][1], q)

                with sp.Fori(0, NG) as k:
                    group(k)
                sp.wait_ge(s_rounds, l + 1)
                n = sp.value_load(rounds[0:1, l:l + 1], min_val=1, max_val=MAX_ROUNDS)
                with sp.If(n > 1):
                    with sp.Fori(NG, n * NG) as k:
                        group(k)
                base = sp.snap(base + n * NG)
            sp.wait_ge(s_yts, 4)
            sp.dma_start(y_prompt[0], xio[:, 0, :]).then_inc(s_out, 16)
            sp.dma_start(y_sample[0], xio[:, 1, :]).then_inc(s_out, 16)
            sp.wait_ge(s_out, 32)

        @block.gpsimd
        def _(pool):
            nc.gpsimd.memset(credit[:, 0:1], 0.0).then_inc(s_lo, RAW_CREDIT)
            nc.gpsimd.memset(credit[:, 1:2], 0.0).then_inc(s_unit, RING)
            for n, s in enumerate((s_turn, s_prod, s_gus, s_acc, s_ylo)):
                nc.gpsimd.memset(credit[:, 2 + n:3 + n], 0.0).then_inc(s, GRANT)
            loads = [
                (const[:, :], k_base),
                (vrow[0:8, 0, :], c_ctx.rearrange("(b p) -> b p", p=P)),
                (vrow[8:16, 0, :], c.rearrange("a (b p) -> (a b) p", p=P)),
                (vrow[16:48, 0, :], norm1_g.rearrange("l (b p) -> (l b) p", p=P)),
                (vrow[48:80, 0, :], norm2_g.rearrange("l (b p) -> (l b) p", p=P)),
                (vrow[80:88, 0, :], final_norm_g.rearrange("(b p) -> b p", p=P)),
                (vrow[88:104, 0, :], pool_scale.rearrange("l (b p) -> (l b) p", p=P)),
                (vrow[0:96, 1, :], ada_b[0:2].rearrange("l (b p) -> (l b) p", p=P)),
                (vrow[0:96, 2, :], ada_b[2:4].rearrange("l (b p) -> (l b) p", p=P)),
                (xio[:, 0, :], x_prompt[0]),
                (xio[:, 1, :], x_sample[0]),
                (rw[:, :, :], router_w.rearrange("(b p) e -> p b e", p=P)),
                (rb[:, :], router_b.partition_broadcast(P)),
            ]
            assert len(loads) == N_FIRST_LOADS
            for dst, src in loads:
                pool.dma_start(dst, src).then_inc(s_load, 16)

            def weight_tile(name, i):
                n = WM_AT[(name, i)]
                if n >= WM_RING:
                    pool.wait_ge(s_wmu, n - WM_RING + 1)
                src = {"qkv": attn_wqkv, "wo": attn_wo, "four": fourier_w}[name][0]
                pool.dma_start(wm[:, n % WM_RING, :, :],
                               src.rearrange("(b p) n -> p b n", p=P)[:, :, i * WM_COLS:(i + 1) * WM_COLS]
                               ).then_inc(s_wm[n % WM_RING], 16)

            for l in range(DEPTH):
                pool.wait_ge(s_xq, 4 * (2 * l) + 4)
                if KINDS[l] == 0:
                    j = l // 3
                    if l == 0:
                        pool.wait_ge(s_vecs, 2)
                    pool.dma_start(kpool[:, :, :], k_pool).then_inc(s_kc, 16)
                    pool.dma_start(wp[:, :, :, :], pool_w[j].rearrange("g (b p) d -> p g b d", p=P)).then_inc(s_kc, 16)
                elif KINDS[l] == 1:
                    for i in range(3):
                        weight_tile("qkv", i)
                    pool.dma_start(kattn[:, :, :], k_attn).then_inc(s_kc, 16)
                    pool.dma_start(ck[:, :], cache_k[0, 0].rearrange("m h d -> m (h d)")).then_inc(s_kc, 16)
                    pool.dma_start(cv[:, :], cache_v[0, 0].rearrange("m h d -> m (h d)")).then_inc(s_kc, 16)
                    nc.gpsimd.memset(rpad[:, :, :], 0.0).then_inc(s_pad, 1)
                    pool.wait_ge(s_pad, 1)
                    pool.dma_start(rpad[:, :, 48:79], attn_rpb[0, :, WIN_ROWS - 2:WIN_ROWS + 1, :]).then_inc(s_bias, 16)
                    pool.wait_ge(s_bias, 16)
                    pool.dma_start(bias_dram, rpad[:, :, :]).then_inc(s_bias, 16)
                    pool.wait_ge(s_bias, 32)
                    for r in range(2):
                        for kr in range(2):
                            src = bass.AP(tensor=bias_dram.tensor, offset=(kr - r + 1) * P,
                                          ap=[[1, GRID_W], [3 * P, HEADS], [1, GRID_W]])
                            dst = oT[r * GRID_W:(r + 1) * GRID_W, :, :].rearrange("p d t -> p (d t)").rearrange(
                                "p (h k) -> p h k", h=HEADS)[:, :, kr * GRID_W:(kr + 1) * GRID_W]
                            pool.dma_start(dst, src).then_inc(s_bias, 16)
                    for i in range(3, 12):
                        weight_tile("qkv", i)
                    for i in range(4):
                        weight_tile("wo", i)
                    pool.wait_ge(s_kts, 4)
                    pool.dma_start(new_cache_k[0, 0].rearrange("m h d -> m (h d)"), knew[:, :]).then_inc(s_kv, 16)
                    pool.wait_ge(s_qkve, 6)
                    pool.wait_ge(s_qkvo, 6)
                    pool.dma_start(new_cache_v[0, 0].rearrange("m h d -> m (h d)"), vtok[:, 0, :]).then_inc(s_kv, 16)
                    pool.wait_ge(s_kv, 32)
                else:
                    pool.dma_start(kfour[:, :], k_four).then_inc(s_kc, 16)
                    for i in range(4):
                        weight_tile("four", i)
                pool.wait_ge(s_tok, 4 * (l + 1))
                nc.gpsimd.memset(hT[:, :, :], 0.0).then_inc(s_acc0, 1)
                nc.gpsimd.memset(y_hi[:, 0, :].bitcast(F32), 0.0).then_inc(s_acc0, 1)
                nc.gpsimd.memset(y_lo[:, 0, :].bitcast(F32), 0.0).then_inc(s_acc0, 1)
                nc.gpsimd.memset(onehotT[:, 2:4, :].bitcast(F32), 0.0).then_inc(s_acc0, 1)

        @block.scalar
        def _(ac):
            ac.wait_ge(s_vecs, 1)
            nc.scalar.activation(cact[:, :, :], cond.rearrange("p (s b) -> p s b", s=NSEQ), ACT.Silu).then_inc(s_cact, 1)

            def ada_copy(count):
                ac.wait_ge(s_ada, count + 1)
                ac.wait_ge(s_adat, count - (ADA_CHUNKS - 6))
                nc.scalar.activation(ada_row[0:NSEQ, :], ps[0:NSEQ, B_M, T:T + ADA_COLS], ACT.Copy).then_inc(s_adac, 1)

            def copy_first(a, b):
                for chunk in range(a * MOD_CHUNKS, b * MOD_CHUNKS):
                    ac.wait_ge(s_ada, chunk + 1)
                    nc.scalar.activation(ada_rows[:, chunk * ADA_COLS:(chunk + 1) * ADA_COLS],
                                         ps[0:NSEQ, B_M, T:T + ADA_COLS], ACT.Copy).then_inc(s_adac, 1)

            def norm(n):
                for q in range(4):
                    ac.wait_ge(s_xq, 4 * n + q + 1)
                    if n == 0 and q == 0:
                        ac.wait_ge(s_xt, 4)
                    nc.scalar.activation(quarter(work, q), quarter(xT, q), ACT.Square).then_inc(s_sq, 1)
                ac.wait_ge(s_ms, n + 1)
                nc.scalar.activation(rstd[:, :], ms[:, :], ACT.Sqrt).then_inc(s_rt, 1)

            def router(l):
                if KINDS[l] == 1:
                    ac.wait_ge(s_kv, 32)
                ac.wait_ge(s_lg, l + 1)
                nc.scalar.activation(r_sc[:, :, :], ps[:, B_M, 0:2 * E].rearrange("p (s e) -> p s e", s=NSEQ),
                                     ACT.Sigmoid).then_inc(s_sig, 1)
                for b in range(4):
                    ac.wait_ge(s_tok, 4 * l + b + 1)
                    nc.scalar.activation(h_hi[:, b // 2, (b % 2) * 512:(b % 2 + 1) * 512], ps[:, b, :],
                                         ACT.Copy).then_inc(s_thi, 1)

            def mixer_attention():
                for t in range(0, 12, 2):
                    ac.wait_ge(s_wmu, t + 1)
                    bank = ps[:, t % 4, :]
                    if t < 8:
                        dst = quarter(work if t < 4 else kT, t % 4)
                        nc.scalar.activation(dst, bank.rearrange("p (d t) -> p d t", d=2), ACT.Copy).then_inc(s_qkve, 1)
                    else:
                        nc.scalar.activation(vtok[:, :, (t - 8) * 256:(t - 7) * 256],
                                             bank.rearrange("p (s n) -> p s n", s=NSEQ), ACT.Copy).then_inc(s_qkve, 1)
                for b in range(4):
                    ac.wait_ge(s_kt, b + 1)
                    dst = (ckT[:, (b % 2) * 4:(b % 2) * 4 + 4, :].rearrange("p d t -> p (d t)") if b < 2
                           else knew[:, (b % 2) * 512:(b % 2 + 1) * 512])
                    nc.scalar.activation(dst, ps[:, 4 + b, :], ACT.Copy).then_inc(s_kts, 1)

                def exps(hp):
                    ac.wait_ge(s_max, hp + 1)
                    for e in range(2):
                        for part, (a, b) in enumerate(((0, P), (P, 3 * P))):
                            v = soft[:, hp % 2, e, a:b]
                            nc.scalar.activation(v, v, ACT.Exp, bias=mstat[:, hp % 2, 1, 2 * e + part:2 * e + part + 1],
                                                 accum_out=mstat[:, hp % 2, 2, 2 * e + part:2 * e + part + 1]
                                                 ).then_inc(s_exp, 1)

                def copy_turned(hp):
                    ac.wait_ge(s_pt2, hp + 1)
                    if hp >= 2:
                        ac.wait_ge(s_o, hp - 1)
                    nc.scalar.activation(pT[:, hp % 2, :, :], ps[:, 4:6, 0:3 * P], ACT.Copy).then_inc(s_pts, 1)

                exps(0)
                exps(1)
                for hp in range(PAIRS):
                    copy_turned(hp)
                    if hp + 2 < PAIRS:
                        exps(hp + 2)

            def mixer_pool(l):
                j = l // 3
                for g in range(0, 4, 2):
                    ac.wait_ge(s_z, 4 * j + g + 1)
                    nc.scalar.activation(ztok[:, g, :, :].rearrange("p s n -> p (s n)"), ps[:, g, :],
                                         ACT.Copy).then_inc(s_ze, 1)

            def mixer_fourier():
                for b in range(0, 8, 2):
                    ac.wait_ge(s_f1, b + 1)
                    nc.scalar.activation(ftok[:, b // 4, b % 4, :], ps[:, b, :], ACT.Copy).then_inc(s_f1e, 1)
                for g in range(4):
                    ac.wait_ge(s_f2, g + 1)
                    nc.scalar.activation(quarter(fT, g), ps[:, g, :].rearrange("p (d t) -> p d t", d=2),
                                         ACT.Copy).then_inc(s_f2s, 1)

            base = 0
            for l in range(DEPTH):
                norm(2 * l)
                if l == 0:
                    copy_first(0, 3)
                if KINDS[l] == 0:
                    mixer_pool(l)
                if l == 0:
                    copy_first(3, 4)
                if KINDS[l] == 1:
                    mixer_attention()
                if KINDS[l] == 2:
                    mixer_fourier()
                norm(2 * l + 1)
                if l == 0:
                    copy_first(4, 5)
                router(l)
                if l == 0:
                    copy_first(5, 6)

                def gathered(gi, db, bank=None):
                    ac.wait_ge(s_ga, gi * 8 + (db + 1))
                    nc.scalar.activation(
                        xg[:, db, :, :].rearrange("p e (h s) -> p h e s", h=2),
                        ps[:, B_A + db % 2 if bank is None else bank, :].rearrange("p (h e s) -> p h e s", h=2, e=GROUP),
                        ACT.Copy).then_inc(s_gev, 1)

                def output_hi(e, it48, it8, it):
                    if e == 3:
                        ac.wait_ge(s_unit, it48 + RING)
                    else:
                        ac.wait_ge(s_unit, it48 + (RING + END_DN[e] + 1))
                        if e == 0:
                            ac.wait_ge(s_gcs, it + 1)
                        if e % 2 == 0:
                            ac.wait_ge(s_comb, it8 + (4 * l + 4 + 2 * e))
                    for b in range(2):
                        nc.scalar.activation(y_hi[:, e % 2, b * 512:(b + 1) * 512], ps[:, B_Y + b, :], ACT.Copy,
                                             scale=gcol[:, e:e + 1]).then_inc(s_yhi, 1)

                first = ac.snap(base + l)
                for db in range(4):
                    gathered(first, db, FIRST_GATHER_BANKS[db])
                ac.wait_ge(s_rounds, l + 1)
                n = ac.value_load(rounds[0:1, l:l + 1], min_val=1, max_val=MAX_ROUNDS)
                with ac.Fori(0, n * NG) as k:
                    it = ac.snap(base + k)
                    it8 = ac.snap(it * 8)
                    it48 = ac.snap(it * NU)
                    gi = ac.snap(it + l)
                    following = ac.snap(it + (l + 1))

                    def split_hi(u):
                        slot = (u // 2) % RAW
                        if u % 2 == 0:
                            ac.wait_ge(s_raw[slot], it * (32 * PAIR_LOADS // RAW) + 32 * (u // 2 // RAW + 1))
                        ac.wait_ge(s_unit, it48 + (u + 1))
                        nc.scalar.activation(w_hi[:, u % RING, :], raw[:, slot, u % 2, :], ACT.Copy).then_inc(s_hi, 1)

                    for u in range(NU):
                        split_hi(u)
                        if u in GU_COPIED:
                            e = GU_COPIED[u]
                            ac.wait_ge(s_unit, it48 + (RING + END_GU[e] + 1))
                            ac.wait_ge(s_turn, it * GROUP + e + GRANT)
                            for b in range(2):
                                nc.scalar.activation(gu[:, b * F:(b + 1) * F], ps[:, B_G + b, :], ACT.Copy).then_inc(s_gus, 1)
                        if u == ONEHOT_COPIED:
                            for b in range(2):
                                ac.wait_ge(s_oht, it * 2 + (b + 1))
                                nc.scalar.activation(onehotT[:, 2 * b:2 * b + 2, :], ps[:, B_A + b, :].rearrange(
                                    "p (e t) -> p e t", e=2), ACT.Copy).then_inc(s_ohs, 1)
                        if u in SILU:
                            e = SILU[u]
                            ac.wait_ge(s_turn, it * GROUP + (e + 1) + GRANT)
                            ac.wait_ge(s_prod, it * GROUP + e + GRANT)
                            nc.scalar.activation(sg[:, :], ps[:, B_T, 0:FB * SLOTS], ACT.Silu).then_inc(s_silu, 1)
                        if u == LAST_HI:
                            output_hi(3, it48, it8, it)
                        if u in GATHERED_LATE:
                            gathered(gi, GATHERED_LATE[u])
                        if u in OUTPUT_HI:
                            output_hi(OUTPUT_HI[u], it48, it8, it)
                        for db in GATHERED.get(u, []):
                            gathered(following, db)
                        if u in ADA_COPIED and l < DEPTH - 1:
                            ada_copy(it * ADA_PER + (ADA_CHUNKS + ADA_COPIED[u]))
                base = ac.snap(base + n * NG)
                for db in range(4, DB):
                    gathered(base + l, db)
                output_hi(3, base * NU, None, None)
            norm(2 * DEPTH)
            for b in range(4):
                ac.wait_ge(s_yt, b + 1)
                nc.scalar.activation(xio[:, b // 2, (b % 2) * 512:(b % 2 + 1) * 512], ps[:, b, :], ACT.Copy).then_inc(s_yts, 1)

        @block.vector
        def _(v):
            links = [0]

            def link(ins):
                links[0] += 1
                ins.then_inc(s_link, 1)
                v.wait_ge(s_link, links[0])

            v.wait_ge(s_rows, 1)
            v.tensor_copy(vecs[:, :], ps[:, 4, 0:104]).then_inc(s_vecs, 1)
            v.wait_ge(s_rows, 3)
            v.tensor_copy(adab[:, :], ps[:, 5, 0:192]).then_inc(s_vecs, 1)
            for q in range(4):
                v.wait_ge(s_xt, q + 1)
                v.tensor_copy(quarter(xT, q), ps[:, q, :].rearrange("p (d t) -> p d t", d=2)).then_inc(s_xq, 1)
            v.wait_ge(s_vecs, 2)

            def store_ada(layer, chunk, count):
                m = mods[:, layer, :, :].rearrange("p n s -> p (n s)")[:, bass.ds(chunk * (ADA_NB * 2), ADA_NB * 2)]
                bb = adab[:, layer * NB_MOD:(layer + 1) * NB_MOD][:, bass.ds(chunk * ADA_NB, ADA_NB)]
                v.wait_ge(s_adat, count)
                v.tensor_tensor(m.rearrange("p (n s) -> p n s", s=NSEQ),
                                ps[:, B_M, 0:2 * ADA_NB].rearrange("p (n s) -> p n s", s=NSEQ),
                                bb.unsqueeze(2).to_broadcast([P, ADA_NB, NSEQ]), ALU.add).then_inc(s_adas, 1)

            def store_first(a, b):
                for n in range(a, b):
                    v.wait_ge(s_adat, n + 1)
                    v.tensor_tensor(mod(0, n), ps[:, MOD_BANK[n], 0:2 * DB].rearrange("p (n s) -> p n s", s=NSEQ),
                                    adab[:, n * DB:(n + 1) * DB].unsqueeze(2).to_broadcast([P, DB, NSEQ]),
                                    ALU.add).then_inc(s_adas, 1)
                v.wait_ge(s_adas, b)

            v.memset(posx[:, MAX_ROUNDS * NG, :, :], -1.0).then_inc(s_posx, 1)
            v.memset(ada_row[:, :], 0.0).then_inc(s_posx, 1)

            def norm(n, gain, scale, shift, stores=None):
                g2 = gain.unsqueeze(2).to_broadcast([P, DB, NSEQ])

                def gain_and_scale():
                    if scale is None:
                        link(v.tensor_copy(amul[:, :, :], g2))
                    else:
                        link(v.scalar_tensor_tensor(amul[:, :, :], scale, 1.0, g2, ALU.add, ALU.mult))

                def times_gain(q, src, done):
                    v.tensor_tensor(by_seq(quarter(hT, q)), by_seq(quarter(src, q)), per_token(amul, q),
                                    ALU.mult).then_inc(done, 1)

                def times_rstd(q, src, done):
                    v.tensor_tensor(quarter(hT, q), quarter(src, q), rstd[:, :].unsqueeze(1).to_broadcast([P, 2, T]),
                                    ALU.mult).then_inc(done, 1)

                if stores is None:
                    gain_and_scale()
                    for q in range(4):
                        v.wait_ge(s_xq, 4 * n + q + 1)
                        times_gain(q, xT, s_n1)
                v.wait_ge(s_ss, n + 1)
                v.tensor_scalar(ms[:, :], ps[:, B_M, 0:T], 1.0 / D, EPS, ALU.mult, ALU.add).then_inc(s_ms, 1)
                v.wait_ge(s_rt, n + 1)
                link(v.reciprocal(rstd[:, :], rstd[:, :]))
                link(v.scalar_tensor_tensor(newton[:, :], rstd[:, :], -0.5, rstd[:, :], ALU.mult, ALU.mult))
                link(v.tensor_tensor(newton[:, :], newton[:, :], ms[:, :], ALU.mult))
                link(v.scalar_tensor_tensor(rstd[:, :], newton[:, :], 1.5, rstd[:, :], ALU.add, ALU.mult))
                if stores is not None:
                    for q in range(4):
                        times_rstd(q, xT, s_n1)
                    store_first(*stores)
                    gain_and_scale()
                last = s_hq if shift is None else s_n2
                for q in range(4):
                    v.wait_ge(s_n1, 4 * n + q + 1)
                    if stores is None:
                        times_rstd(q, hT, last)
                    else:
                        times_gain(q, hT, last)
                if shift is not None:
                    for q in range(4):
                        h = by_seq(quarter(hT, q))
                        v.wait_ge(s_n2, 4 * n + q + 1)
                        v.tensor_tensor(h, h, per_token(shift, q), ALU.add).then_inc(s_hq, 1)

            def residual(src, coef, q):
                for d in range(2):
                    for s in range(NSEQ):
                        x = xT[:, 2 * q + d, s * SEQ:(s + 1) * SEQ]
                        ins = v.scalar_tensor_tensor(x, src(d, s), coef[:, 2 * q + d, s:s + 1], x, ALU.mult, ALU.add)
                ins.then_inc(s_xq, 1)

            def residual_from_banks(done, before, coef, first_bank):
                for q in range(4):
                    v.wait_ge(done, before + q + 1)
                    bank = ps[:, first_bank + q, :]
                    residual(lambda d, s: bank[:, (2 * d + s) * SEQ:(2 * d + s + 1) * SEQ], coef, q)

            def mixer_pool(l):
                j = l // 3
                for g in range(1, 4, 2):
                    v.wait_ge(s_z, 4 * j + g + 1)
                    v.tensor_copy(ztok[:, g, :, :].rearrange("p s n -> p (s n)"), ps[:, g, :]).then_inc(s_zo, 1)
                if l == 0:
                    store_first(2, 3)
                gain = pscale[:, j * DB:(j + 1) * DB].unsqueeze(2).to_broadcast([P, DB, NSEQ])
                link(v.tensor_tensor(pcoef[:, :, :], mod(l, 2), gain, ALU.mult))
                residual_from_banks(s_mix, 4 * j, pcoef, 0)

            def mixer_attention(l):
                for t in range(1, 12, 2):
                    v.wait_ge(s_wmu, t + 1)
                    bank = ps[:, t % 4, :]
                    if t < 8:
                        dst = quarter(work if t < 4 else kT, t % 4)
                        v.tensor_copy(dst, bank.rearrange("p (d t) -> p d t", d=2)).then_inc(s_qkvo, 1)
                    else:
                        v.tensor_copy(vtok[:, :, (t - 8) * 256:(t - 7) * 256],
                                      bank.rearrange("p (s n) -> p s n", s=NSEQ)).then_inc(s_qkvo, 1)

                v.wait_ge(s_kc, KC_AFTER[l])
                mask = kattn[:, 0, :].unsqueeze(1).to_broadcast([P, 4, P])
                for b in range(4):
                    v.wait_ge(s_flip, b + 1)
                    v.tensor_tensor(bias[:, 4 * b:4 * b + 4, :], ps[:, 4 + b, :].rearrange("p (h k) -> p h k", h=4),
                                    mask, ALU.add).then_inc(s_biass, 1)

                def scale_bias_max(hp):
                    par = hp % 2
                    v.wait_ge(s_sc, hp + 1)
                    if hp >= 2:
                        v.wait_ge(s_pt2, hp - 1)
                    else:
                        v.wait_ge(s_biass, 4)
                    banks = ps[:, 2 * par:2 * par + 2, 0:3 * P]
                    v.tensor_scalar(soft[:, par, :, 0:P], banks[:, :, 0:P], SCALE, None, ALU.mult)
                    v.tensor_scalar(soft[:, par, :, 2 * P:3 * P], banks[:, :, 2 * P:3 * P], SCALE, None, ALU.mult)
                    link(v.scalar_tensor_tensor(soft[:, par, :, P:2 * P], banks[:, :, P:2 * P], SCALE,
                                                bias[:, 2 * hp:2 * hp + 2, :], ALU.mult, ALU.add))
                    v.tensor_reduce(mstat[:, par, 0, 0:4:2], soft[:, par, :, 0:P], AX_X, ALU.max)
                    link(v.tensor_reduce(mstat[:, par, 0, 1:4:2], soft[:, par, :, P:3 * P], AX_X, ALU.max))
                    v.tensor_scalar(mstat[:, par, 1, :], mstat[:, par, 0, :], -1.0, None, ALU.mult).then_inc(s_max, 1)

                def normalise(hp):
                    par = hp % 2
                    v.wait_ge(s_exp, 4 * hp + 4)
                    link(v.reciprocal(mstat[:, par, 0, :], mstat[:, par, 2, :]))
                    for part, (a, b) in enumerate(((0, P), (P, 3 * P))):
                        r = mstat[:, par, 0, part:4:2].unsqueeze(2).to_broadcast([P, 2, b - a])
                        ins = v.tensor_tensor(soft[:, par, :, a:b], soft[:, par, :, a:b], r, ALU.mult)
                    ins.then_inc(s_prob, 1)

                def copy_output(hp):
                    v.wait_ge(s_o, hp + 1)
                    v.tensor_copy(oT[:, hp, :], ps[:, 6 + hp % 2, 0:T]).then_inc(s_os, 1)

                scale_bias_max(0)
                scale_bias_max(1)
                normalise(0)
                for hp in range(PAIRS):
                    if hp + 1 < PAIRS:
                        normalise(hp + 1)
                    if hp >= 1:
                        copy_output(hp - 1)
                    if hp + 2 < PAIRS:
                        scale_bias_max(hp + 2)
                copy_output(PAIRS - 1)
                residual_from_banks(s_wmu, WM_AT[("wo", 0)], mod(l, 2), 0)

            def mixer_fourier(l):
                for b in range(1, 8, 2):
                    v.wait_ge(s_f1, b + 1)
                    v.tensor_copy(ftok[:, b // 4, b % 4, :], ps[:, b, :]).then_inc(s_f1o, 1)
                residual_from_banks(s_wmu, WM_AT[("four", 0)], mod(l, 2), 0)

            def router(l):
                v.wait_ge(s_sig, l + 1)
                sc = r_sc[:, :, :]
                link(v.tensor_tensor(r_sel[:, :, :].rearrange("p (s g) e -> p s (g e)", s=NSEQ), sc,
                                     rb[:, :].unsqueeze(1).to_broadcast([P, NSEQ, E]), ALU.add))
                sel = r_sel[:, :, :]
                at = 0
                for i in range(3):
                    m = 3 - i
                    ins = v.tensor_tensor(r_pair[:, :, at:at + m], sel[:, :, i:i + 1].to_broadcast([P, NSEQ * NG, m]),
                                          sel[:, :, i + 1:4], ALU.add)
                    at += m
                link(ins)
                gs = r_gs[:, :, :].rearrange("p s g -> p (s g)")
                link(v.tensor_reduce(gs, r_pair[:, :, :], AX_X, ALU.max))

                def rank(out, val, n):
                    vi = val.unsqueeze(3).to_broadcast([P, n, 4, 4])
                    vj = val.unsqueeze(2).to_broadcast([P, n, 4, 4])
                    ge = r_ge[:, 0:n, :].rearrange("p n (i j) -> p n i j", i=4)
                    gt = r_gt[:, 0:n, :].rearrange("p n (i j) -> p n i j", i=4)
                    v.tensor_tensor(ge, vj, vi, ALU.is_ge)
                    link(v.tensor_tensor(gt, vj, vi, ALU.is_gt))
                    v.tensor_tensor(r_ge[:, 0:n, :], r_ge[:, 0:n, :], before.unsqueeze(1).to_broadcast([P, n, 16]), ALU.mult)
                    link(v.tensor_tensor(r_gt[:, 0:n, :], r_gt[:, 0:n, :], after.unsqueeze(1).to_broadcast([P, n, 16]), ALU.mult))
                    link(v.tensor_tensor(r_ge[:, 0:n, :], r_ge[:, 0:n, :], r_gt[:, 0:n, :], ALU.add))
                    link(v.tensor_reduce(out, ge, AX_X, ALU.add))

                best = r_best[:, :]
                rank(best.rearrange("p (s g) -> p s g", s=NSEQ), r_gs[:, :, :], NSEQ)
                link(v.tensor_scalar(best, best, 0.0, None, ALU.is_equal))
                rank(r_rank[:, :, :], sel, NSEQ * NG)
                link(v.tensor_scalar(r_rank[:, :, :], r_rank[:, :, :], 2.0, None, ALU.is_lt))
                mask = r_mask[:, :, :]
                v.tensor_tensor(mask.rearrange("p s (g e) -> p (s g) e", e=GROUP), r_rank[:, :, :],
                                best.unsqueeze(2).to_broadcast([P, NSEQ * NG, GROUP]), ALU.mult).then_inc(s_mask, 1)
                v.wait_ge(s_mask, l + 1)
                link(v.tensor_tensor(r_w[:, :, :], sc, mask, ALU.mult))
                link(v.tensor_reduce(r_den[:, :], r_w[:, :, :], AX_X, ALU.add))
                link(v.reciprocal(r_den[:, :], r_den[:, :]))
                for s in range(NSEQ):
                    v.tensor_scalar(gx[:, :, s, :], r_w[:, s, :].rearrange("p (g e) -> p g e", g=NG),
                                    r_den[:, s:s + 1], None, ALU.mult)
                for b in range(4):
                    v.wait_ge(s_thi, 4 * l + b + 1)
                    piece = (slice(None), b // 2, slice((b % 2) * 512, (b % 2 + 1) * 512))
                    v.tensor_tensor(h_lo[piece], ps[:, b, :], h_hi[piece].bitcast(F32), ALU.subtract).then_inc(s_tlo, 1)
                v.wait_ge(s_pos, l + 1)
                pm = r_pm[:, :, :, :]
                link(v.scalar_tensor_tensor(pm.rearrange("p s g e -> p s (g e)"),
                                            ps[:, B_M, 0:2 * E].rearrange("p (s e) -> p s e", s=NSEQ),
                                            1.0, mask, ALU.add, ALU.mult))
                for r in range(MAX_ROUNDS):
                    v.tensor_scalar(posx[:, r * NG:(r + 1) * NG, :, :], pm.rearrange("p s g e -> p g s e"),
                                    -1.0 - SLOTS * r, None, ALU.add)
                link(v.memset(gcol[:, :], 0.0))
                link(v.tensor_reduce(r_cnt[:, 0:1], ps[:, B_M, 2 * E:3 * E], AX_X, ALU.max))
                link(v.tensor_tensor(r_cnt[:, 1:4], r_cnt[:, 0:1].to_broadcast([P, 3]), limits, ALU.is_gt))
                link(v.tensor_reduce(r_cnt[:, 4:5], r_cnt[:, 1:4], AX_X, ALU.add))
                v.tensor_scalar(rounds[:, l:l + 1], r_cnt[:, 4:5], 1.0, None, ALU.add).then_inc(s_rounds, 1)
                v.wait_ge(s_rounds, l + 1)

            base = 0
            for l in range(DEPTH):
                norm(2 * l, n1g[:, l * DB:(l + 1) * DB], mod(l, 1), mod(l, 0), (0, 2) if l == 0 else None)
                (mixer_pool, mixer_attention, mixer_fourier)[KINDS[l]](l)
                norm(2 * l + 1, n2g[:, l * DB:(l + 1) * DB], mod(l, 4), mod(l, 3), (3, 5) if l == 0 else None)
                router(l)
                if l == 0:
                    store_first(5, 6)

                def onehots(group, g):
                    pos = posx[:, :, :, :].rearrange("p k s e -> p (k s e)")[:, bass.ds(group * 8, 8)]
                    v.tensor_tensor(onehot[:, :, :, :].rearrange("p s e c -> p (s e) c"),
                                    iota.unsqueeze(1).to_broadcast([P, 8, P]),
                                    pos.unsqueeze(2).to_broadcast([P, 8, P]), ALU.is_equal).then_inc(s_oh, 1)
                    v.tensor_copy(gsel[:, :, :].rearrange("p s e -> p (s e)"),
                                  gx[:, :, :, :].rearrange("p g s e -> p (g s e)")[:, bass.ds(g * 8, 8)]).then_inc(s_oh, 1)

                def output_lo(e, count):
                    for b in range(2):
                        v.wait_ge(s_yhi, count + (b + 1))
                        piece = (slice(None), e % 2, slice(b * 512, (b + 1) * 512))
                        v.scalar_tensor_tensor(y_lo[piece], ps[:, B_Y + b, :], gcol[:, e:e + 1],
                                               y_hi[piece].bitcast(F32), ALU.mult, ALU.subtract).then_inc(s_ylo, 1)

                def add_up(q, count):
                    v.wait_ge(s_comb, count)
                    h = quarter(hT, q)
                    v.tensor_tensor(h, h, ps[:, B_A + q % 2, :].rearrange("p (d t) -> p d t", d=2),
                                    ALU.add).then_inc(s_acc, 1)

                v.wait_ge(s_posx, 2)
                onehots(0, 0)
                n = v.value_load(rounds[0:1, l:l + 1], min_val=1, max_val=MAX_ROUNDS)
                v.wait_ge(s_acc0, 4 * (l + 1))
                with v.Fori(0, n * NG) as k:
                    it = v.snap(base + k)
                    it8 = v.snap(it * 8)
                    it48 = v.snap(it * NU)
                    g = v.snap(k & (NG - 1))
                    g_next = v.snap((k + 1) & (NG - 1))
                    k_next = v.snap(k + 1)

                    def split_lo(u):
                        v.wait_ge(s_hi, it48 + (u + 1))
                        v.tensor_tensor(w_lo[:, u % RING, :], raw[:, (u // 2) % RAW, u % 2, :],
                                        w_hi[:, u % RING, :].bitcast(F32), ALU.subtract).then_inc(s_lo, 1)

                    for u in range(NU):
                        split_lo(u)
                        if u in ADD_LAST:
                            add_up(ADD_LAST[u], it8 + (4 * l + ADD_LAST[u] + 1))
                        if u == GATES_COPIED:
                            v.wait_ge(s_gc, it + 1)
                            v.tensor_copy(gcol[:, :], ps[:, B_Y, 0:GROUP]).then_inc(s_gcs, 1)
                        if u in HIDDEN:
                            e = HIDDEN[u]
                            v.wait_ge(s_silu, it * GROUP + (e + 1))
                            v.tensor_tensor(act[:, :], sg[:, :], ps[:, B_T, FB * SLOTS:2 * FB * SLOTS],
                                            ALU.mult).then_inc(s_prod, 1)
                            v.wait_ge(s_prod, it * GROUP + (e + 1) + GRANT)
                            v.wait_ge(s_unit, it48 + (RING + (END_DN[e - 1] + 1 if e else 0)))
                            a3 = act[:, :].rearrange("p (b s) -> p b s", b=FB)
                            v.tensor_copy(a_hl[:, :, 0:SLOTS], a3).then_inc(s_ahi, 1)
                            v.wait_ge(s_ahi, it * GROUP + (e + 1))
                            v.tensor_tensor(a_hl[:, :, SLOTS:2 * SLOTS], a3, a_hl[:, :, 0:SLOTS].bitcast(F32),
                                            ALU.subtract).then_inc(s_alo, 1)
                        if u == NEXT_ONEHOT:
                            onehots(k_next, g_next)
                        if u == LAST_LO:
                            output_lo(3, it8 + 2 * l)
                        if u in OUTPUT_LO:
                            e = OUTPUT_LO[u]
                            output_lo(e, it8 + (2 * l + 2 + 2 * e))
                        if u in ADD_FIRST:
                            add_up(ADD_FIRST[u], it8 + (4 * l + 4 + ADD_FIRST[u] + 1))
                        if u in ADA_STORED and l < DEPTH - 1:
                            j = ADA_STORED[u]
                            store_ada(l + 1, g * ADA_PER + j, it * ADA_PER + (6 + j + 1))
                base = v.snap(base + n * NG)
                output_lo(3, base * 8 + 2 * l)
                for q in range(4):
                    add_up(q, base * 8 + (4 * l + q + 1))
                v.wait_ge(s_acc, base * 8 + (4 * l + 4 + GRANT))
                for q in range(4):
                    residual(lambda d, s: hT[:, 2 * q + d, s * SEQ:(s + 1) * SEQ], mod(l, 5), q)
            norm(2 * DEPTH, fing, None, None)

        @block.tensor
        def _(pe):
            pe.wait_ge(s_load, 16 * N_FIRST_LOADS)
            pe.transpose(ps[:, 4, 0:104], vrow[0:104, 0, :], ident[0:104, 0:104]).then_inc(s_rows, 1)
            for i in range(2):
                pe.transpose(ps[:, 5, 96 * i:96 * (i + 1)], vrow[0:96, 1 + i, :], ident[0:96, 0:96]).then_inc(s_rows, 1)
            for q in range(4):
                for d in range(2):
                    for s in range(NSEQ):
                        mm = pe.transpose(ps[:, q, (2 * d + s) * SEQ:(2 * d + s + 1) * SEQ],
                                          xio[:, s, (2 * q + d) * P:(2 * q + d + 1) * P], ident)
                mm.then_inc(s_xt, 1)

            def ada_product(slot, landed, count):
                pe.wait_ge(s_ada_in[slot], landed)
                if not (isinstance(count, int) and count == 0):
                    pe.wait_ge(s_adac, count)
                for b in range(DB):
                    mm = pe.matmul(ps[0:NSEQ, B_M, T:T + ADA_COLS], cact[:, :, b], ada_in[:, slot, b, :],
                                   start=(b == 0), stop=(b == DB - 1))
                mm.then_inc(s_ada, 1)

            def ada_turn(count):
                pe.wait_ge(s_adac, count + 1)
                for n in range(ADA_NB):
                    mm = pe.matmul(ps[:, B_M, NSEQ * n:NSEQ * (n + 1)], ada_row[:, n * P:(n + 1) * P],
                                   ident[:, 0:NSEQ], start=True, stop=True)
                mm.then_inc(s_adat, 1)

            def ada_first(a, b):
                for n in range(a, b):
                    for chunk in range(n * MOD_CHUNKS, (n + 1) * MOD_CHUNKS):
                        ada_product(chunk % ADA_SLOTS, 16 * (chunk // ADA_SLOTS + 1), chunk)
                    pe.wait_ge(s_adac, (n + 1) * MOD_CHUNKS)
                    if n >= 3:
                        pe.wait_ge(s_adas, n - 1)
                    for j in range(DB):
                        mm = pe.transpose(ps[:, MOD_BANK[n], NSEQ * j:NSEQ * (j + 1)],
                                          ada_rows[:, n * D + j * P:n * D + (j + 1) * P], ident[0:NSEQ, 0:NSEQ])
                    mm.then_inc(s_adat, 1)

            def norm(n):
                for b in range(DB):
                    if b % 2 == 0:
                        pe.wait_ge(s_sq, 4 * n + b // 2 + 1)
                    mm = pe.matmul(ps[:, B_M, 0:T], ones, work[:, b, :], start=(b == 0), stop=(b == DB - 1))
                mm.then_inc(s_ss, 1)

            def router(l):
                n = 2 * l + 1
                for s in range(NSEQ):
                    for b in range(DB):
                        if s == 0 and b % 2 == 0:
                            pe.wait_ge(s_hq, 4 * n + b // 2 + 1)
                        mm = pe.matmul(ps[:, B_M, s * E:(s + 1) * E], hT[:, b, s * SEQ:(s + 1) * SEQ], rw[:, b, :],
                                       start=(b == 0), stop=(b == DB - 1))
                mm.then_inc(s_lg, 1)
                for b in range(4):
                    s, half = b // 2, b % 2
                    for i in range(4):
                        mm = pe.transpose(ps[:, b, i * P:(i + 1) * P], hT[:, 4 * half + i, s * SEQ:(s + 1) * SEQ], ident)
                    mm.then_inc(s_tok, 1)
                if l == 0:
                    pe.wait_ge(s_sig, 1)
                    ada_first(5, 6)
                    pe.wait_ge(s_adac, 6 * MOD_CHUNKS)
                pe.wait_ge(s_mask, l + 1)
                pe.matmul(ps[:, B_M, 0:E], tri, r_mask[:, 0, :], start=True, stop=True)
                pe.matmul(ps[:, B_M, E:2 * E], ones, r_mask[:, 0, :], start=True, stop=False)
                pe.matmul(ps[:, B_M, E:2 * E], tri, r_mask[:, 1, :], start=False, stop=True)
                pe.matmul(ps[:, B_M, 2 * E:3 * E], ones, r_mask[:, 0, :], start=True, stop=False)
                pe.matmul(ps[:, B_M, 2 * E:3 * E], ones, r_mask[:, 1, :], start=False, stop=True).then_inc(s_pos, 1)

            def mixer_pool(l):
                if l == 0:
                    pe.wait_ge(s_ms, 1)
                    ada_first(0, 3)
                pe.wait_ge(s_kc, KC_AFTER[l])
                j = l // 3
                for g in range(4):
                    pe.wait_ge(s_hq, 4 * (2 * l) + g + 1)
                    for s in range(NSEQ):
                        for b in range(2):
                            mm = pe.matmul(ps[:, g, s * T:(s + 1) * T], hT[:, 2 * g + b, s * SEQ:(s + 1) * SEQ],
                                           wp[:, g, b, :], start=(b == 0), stop=(b == 1))
                    mm.then_inc(s_z, 1)
                for g in range(4):
                    pe.wait_ge(s_zo if g % 2 else s_ze, 2 * j + g // 2 + 1)
                    for d in range(2):
                        for s in range(NSEQ):
                            mm = pe.matmul(ps[:, g, (2 * d + s) * SEQ:(2 * d + s + 1) * SEQ],
                                           ztok[:, g, s, d * P:(d + 1) * P], kpool[:, g, :], start=True, stop=True)
                    mm.then_inc(s_mix, 1)

            def mixer_attention(l):
                for t in range(12):
                    n = WM_AT[("qkv", t)]
                    if t == 0:
                        pe.wait_ge(s_hq, 4 * (2 * l) + 4)
                    pe.wait_ge(s_wm[n % WM_RING], 16 * (n // WM_RING + 1))
                    if t >= 4:
                        if t % 2 == 0:
                            pe.wait_ge(s_qkve, (t - 4) // 2 + 1)
                        else:
                            pe.wait_ge(s_qkvo, (t - 5) // 2 + 1)
                    for d in range(2):
                        for b in range(DB):
                            if t < 8:
                                lhs, rhs = wm[:, n % WM_RING, b, d * P:(d + 1) * P], hT[:, b, :]
                            else:
                                lhs, rhs = hT[:, b, d * SEQ:(d + 1) * SEQ], wm[:, n % WM_RING, b, :]
                            mm = pe.matmul(ps[:, t % 4, d * T:(d + 1) * T], lhs, rhs, start=(b == 0), stop=(b == DB - 1))
                    mm.then_inc(s_wmu, 1)
                pe.wait_ge(s_kc, KC_AFTER[l])
                pe.wait_ge(s_ms, 2 * l + 1)
                pe.wait_ge(s_bias, 16 * 6)
                rows = oT[:, :, :].rearrange("p d t -> p (d t)")
                for b in range(4):
                    pe.matmul(ps[:, 4 + b, :], kattn[:, 1, :], rows[:, b * 512:(b + 1) * 512],
                              start=True, stop=True).then_inc(s_flip, 1)
                pe.wait_ge(s_biass, 4)
                for b in range(4):
                    for i in range(4):
                        j = 4 * (b % 2) + i
                        src = ck[:, j * P:(j + 1) * P] if b < 2 else kT[:, j, 0:SEQ]
                        if b == 2 and i == 0:
                            pe.wait_ge(s_qkve, 4)
                            pe.wait_ge(s_qkvo, 4)
                        mm = pe.transpose(ps[:, 4 + b, i * P:(i + 1) * P], src, ident)
                    mm.then_inc(s_kt, 1)
                pe.wait_ge(s_kts, 4)
                pe.wait_ge(s_qkve, 6)
                pe.wait_ge(s_qkvo, 6)

                def scores(hp):
                    if hp >= 2:
                        pe.wait_ge(s_max, hp - 1)
                    for e in range(2):
                        rows = slice(e * HD, (e + 1) * HD)
                        bank = ps[:, 2 * (hp % 2) + e, :]
                        q_ctx, q_lat = work[rows, hp, 0:SEQ], work[rows, hp, SEQ:T]
                        pe.matmul(bank[:, 0:P], q_ctx, kT[rows, hp, 0:SEQ], start=True, stop=True)
                        pe.matmul(bank[:, P:2 * P], q_lat, kT[rows, hp, SEQ:T], start=True, stop=True)
                        mm = pe.matmul(bank[:, 2 * P:3 * P], q_lat, ckT[rows, hp, :], start=True, stop=True)
                    mm.then_inc(s_sc, 1)

                def turn(hp):
                    pe.wait_ge(s_prob, hp + 1)
                    if hp >= 1:
                        pe.wait_ge(s_pts, hp)
                    for e in range(2):
                        for i in range(3):
                            mm = pe.transpose(ps[:, 4 + e, i * P:(i + 1) * P], soft[:, hp % 2, e, i * P:(i + 1) * P], ident)
                    mm.then_inc(s_pt2, 1)

                def attend(hp):
                    pe.wait_ge(s_pts, hp + 1)
                    if hp >= 2:
                        pe.wait_ge(s_os, hp - 1)
                    for e in range(2):
                        cols = slice((2 * hp + e) * HD, (2 * hp + e + 1) * HD)
                        out = ps[e * HD:(e + 1) * HD, 6 + hp % 2, :]
                        p = pT[:, hp % 2, e, :]
                        pe.matmul(out[:, 0:SEQ], vtok[:, 0, cols], p[:, 0:P], start=True, stop=True)
                        pe.matmul(out[:, SEQ:T], vtok[:, 1, cols], p[:, P:2 * P], start=True, stop=False)
                        mm = pe.matmul(out[:, SEQ:T], cv[:, cols], p[:, 2 * P:3 * P], start=False, stop=True)
                    mm.then_inc(s_o, 1)

                scores(0)
                scores(1)
                for hp in range(PAIRS):
                    turn(hp)
                    if hp + 2 < PAIRS:
                        scores(hp + 2)
                    attend(hp)
                pe.wait_ge(s_os, PAIRS)
                out_project("wo", oT, 0)

            def out_project(name, src, first_bank):
                for i in range(4):
                    n = WM_AT[(name, i)]
                    pe.wait_ge(s_wm[n % WM_RING], 16 * (n // WM_RING + 1))
                    for d in range(2):
                        for b in range(DB):
                            mm = pe.matmul(ps[:, first_bank + i, d * T:(d + 1) * T], wm[:, n % WM_RING, b, d * P:(d + 1) * P],
                                           src[:, b, :], start=(b == 0), stop=(b == DB - 1))
                    mm.then_inc(s_wmu, 1)

            def mixer_fourier(l):
                pe.wait_ge(s_kc, KC_AFTER[l])
                chan = kfour[:, 2 * P:].rearrange("p (b n) -> p b n", b=2)
                for b8 in range(8):
                    s, g = b8 // 4, b8 % 4
                    pe.wait_ge(s_hq, 4 * (2 * l) + g + 1)
                    for b in range(2):
                        mm = pe.matmul(ps[:, b8, :], hT[:, 2 * g + b, s * SEQ:(s + 1) * SEQ], chan[:, b, :],
                                       start=(b == 0), stop=(b == 1))
                    mm.then_inc(s_f1, 1)
                pe.wait_ge(s_f1e, 4)
                pe.wait_ge(s_f1o, 4)
                for g in range(4):
                    for d in range(2):
                        for s in range(NSEQ):
                            out = ps[:, g, (2 * d + s) * SEQ:(2 * d + s + 1) * SEQ]
                            pe.matmul(out, ftok[:, s, g, d * P:(d + 1) * P], kfour[:, 0:P], start=True, stop=False)
                            mm = pe.matmul(out, ftok[:, s, g, 256 + d * P:256 + (d + 1) * P], kfour[:, P:2 * P],
                                           start=False, stop=True)
                    mm.then_inc(s_f2, 1)
                pe.wait_ge(s_f2s, 4)
                out_project("four", fT, 0)

            base = 0
            for l in range(DEPTH):
                if l > 0:
                    pe.wait_ge(s_adas, base * ADA_PER + 6)
                else:
                    pe.wait_ge(s_cact, 1)
                    pe.wait_ge(s_vecs, 2)
                norm(2 * l)
                (mixer_pool, mixer_attention, mixer_fourier)[KINDS[l]](l)
                if l == 0:
                    ada_first(3, 4)
                if l == 0:
                    pe.wait_ge(s_adac, 4 * MOD_CHUNKS)
                norm(2 * l + 1)
                pe.wait_ge(s_ms, 2 * l + 2)
                if l == 0:
                    ada_first(4, 5)
                    pe.wait_ge(s_adac, 5 * MOD_CHUNKS)
                router(l)

                def gather(gi, db, bank=None):
                    if db >= (2 if bank is None else 6):
                        pe.wait_ge(s_gev, gi * 8 + (db - 1))
                    for half, h in enumerate((h_hi, h_lo)):
                        for s in range(NSEQ):
                            mm = pe.matmul(ps[:, B_A + db % 2 if bank is None else bank, half * 256:(half + 1) * 256],
                                           h[:, s, db * P:(db + 1) * P], onehot[:, s, :, 0:SLOTS],
                                           start=(s == 0), stop=(s == NSEQ - 1))
                    mm.then_inc(s_ga, 1)

                def combine(pair, q):
                    for d in range(2):
                        n2 = 0
                        for e in range(2):
                            for y in (y_hi, y_lo):
                                mm = pe.matmul(ps[:, B_A + q % 2, d * T:(d + 1) * T],
                                               y[:, e, (2 * q + d) * P:(2 * q + d + 1) * P],
                                               onehotT[:, 2 * pair + e, :], start=(n2 == 0), stop=(n2 == 3))
                                n2 += 1
                    mm.then_inc(s_comb, 1)

                def combine_last(q, it8, gi):
                    if q == 0:
                        pe.wait_ge(s_ylo, it8 + (2 * l + 2 + GRANT))
                    if q < 2:
                        pe.wait_ge(s_gev, gi * 8 + (7 + q))
                    else:
                        pe.wait_ge(s_acc, it8 + (4 * l + q - 1 + GRANT))
                    combine(1, q)

                pe.wait_ge(s_rounds, l + 1)
                pe.wait_ge(s_tlo, 4 * l + 4)
                first = pe.snap(base + l)
                pe.wait_ge(s_oh, first * 2 + 2)
                for db in range(DB):
                    gather(first, db, FIRST_GATHER_BANKS[db])
                n = pe.value_load(rounds[0:1, l:l + 1], min_val=1, max_val=MAX_ROUNDS)
                pe.wait_ge(s_acc0, 4 * (l + 1))
                with pe.Fori(0, n * NG) as k:
                    it = pe.snap(base + k)
                    it4 = pe.snap(it * 4)
                    it8 = pe.snap(it * 8)
                    it48 = pe.snap(it * NU)
                    gi = pe.snap(it + l)
                    following = pe.snap(it + (l + 1))

                    def gate_up_unit(e, b):
                        u = FIRST[("gu", e)] + b
                        if e == 0:
                            pe.wait_ge(s_gev, gi * 8 + (b + 1))
                        if b == 0:
                            pe.wait_ge(s_gus, it8 + 2 * e + GRANT)
                        pe.wait_ge(s_lo, it48 + (u + 1 + RAW_CREDIT))
                        for w, first_half in ((w_hi, True), (w_lo, False)):
                            for n2 in range(2):
                                mm = pe.matmul(ps[:, B_G + n2, :], xg[:, b, e, :], w[:, u % RING, n2 * F:(n2 + 1) * F],
                                               start=(b == 0 and first_half), stop=(b == DB - 1 and not first_half))
                        mm.then_inc(s_unit, 1)

                    def down_unit(e, b):
                        u = FIRST[("dn", e)] + b
                        if b == 0:
                            pe.wait_ge(s_alo, it4 + (e + 1))
                            pe.wait_ge(s_ylo, it8 + (2 * l + 2 + 2 * e + GRANT))
                            if e == 0:
                                pe.wait_ge(s_gcs, it + 1)
                        pe.wait_ge(s_lo, it48 + (u + 1 + RAW_CREDIT))
                        for w, first_half in ((w_hi, True), (w_lo, False)):
                            for n2 in range(2):
                                mm = pe.matmul(ps[:, B_Y + n2, :], a_hl[:, b, :], w[:, u % RING, n2 * 512:(n2 + 1) * 512],
                                               start=(b == 0 and first_half), stop=(b == FB - 1 and not first_half))
                        mm.then_inc(s_unit, 1)

                    def turn(e):
                        pe.wait_ge(s_gus, it8 + (2 * e + 2) + GRANT)
                        pe.wait_ge(s_prod, it4 + e + GRANT)
                        for i in range(2 * FB):
                            mm = pe.matmul(ps[:, B_T, i * SLOTS:(i + 1) * SLOTS], gu[:, i * P:(i + 1) * P], halves,
                                           start=True, stop=True)
                        mm.then_inc(s_turn, 1)

                    def turn_onehots():
                        pe.wait_ge(s_acc, it8 + (4 * l + 4 + GRANT))
                        for e in range(GROUP):
                            for s in range(NSEQ):
                                at = (e % 2) * T + s * SEQ
                                mm = pe.transpose(ps[:, B_A + e // 2, at:at + SEQ], onehot[:, s, e, :].bitcast(F32), ident)
                            if e % 2:
                                mm.then_inc(s_oht, 1)

                    def slot_gates():
                        for e in range(GROUP):
                            for s in range(NSEQ):
                                mm = pe.matmul(ps[:, B_Y, e:e + 1], onehot[:, s, e, :].bitcast(F32), gsel[:, s, e:e + 1],
                                               start=(s == 0), stop=(s == NSEQ - 1))
                        mm.then_inc(s_gc, 1)

                    def combine_first(q):
                        if q == 0:
                            pe.wait_ge(s_ylo, it8 + (2 * l + 6 + GRANT))
                        if q < 2:
                            pe.wait_ge(s_ohs, it * 2 + 2)
                        else:
                            pe.wait_ge(s_acc, it8 + (4 * l + 4 + q - 1 + GRANT))
                        combine(0, q)

                    for u, (kind, e, i) in enumerate(UNITS):
                        (gate_up_unit if kind == "gu" else down_unit)(e, i)
                        if u in PE_COMBINE_LAST:
                            combine_last(PE_COMBINE_LAST[u], it8, gi)
                        if u == PE_ONEHOT_TURN:
                            turn_onehots()
                        if u == PE_GATES:
                            slot_gates()
                        if u in PE_TURN:
                            turn(PE_TURN[u])
                        if u in PE_COMBINE_FIRST:
                            combine_first(PE_COMBINE_FIRST[u])
                        for db in PE_GATHER.get(u, []):
                            if db == 0:
                                pe.wait_ge(s_oh, following * 2 + 2)
                                pe.wait_ge(s_acc, it8 + (4 * l + 8 + GRANT))
                            gather(following, db)
                        if u in PE_ADA and l < DEPTH - 1:
                            j = PE_ADA[u]
                            per_slot = ADA_PER // ADA_SLOTS
                            pe.wait_ge(s_adas, it * ADA_PER + (6 + j))
                            ada_product(j % ADA_SLOTS, it * (16 * per_slot) +
                                        16 * (ADA_CHUNKS // ADA_SLOTS + j // ADA_SLOTS + 1),
                                        it * ADA_PER + (ADA_CHUNKS + j))
                        if u in PE_ADA_TURN and l < DEPTH - 1:
                            ada_turn(it * ADA_PER + (ADA_CHUNKS + PE_ADA_TURN[u]))
                base = pe.snap(base + n * NG)
                for q in range(4):
                    combine_last(q, base * 8, base + l)
            norm(2 * DEPTH)
            for b in range(4):
                s, half = b // 2, b % 2
                for i in range(4):
                    if s == 0:
                        pe.wait_ge(s_hq, 4 * 2 * DEPTH + (4 * half + i) // 2 + 1)
                    mm = pe.transpose(ps[:, b, i * P:(i + 1) * P], hT[:, 4 * half + i, s * SEQ:(s + 1) * SEQ], ident)
                mm.then_inc(s_yt, 1)


_INS = ["x_prompt", "x_sample", "cache_k", "cache_v", "c", "c_ctx", "ada_w", "ada_b", "norm1_g", "norm2_g", "pool_w",
        "pool_scale", "attn_wqkv", "attn_wo", "attn_rpb", "fourier_w", "router_w", "router_b", "moe_w_gate", "moe_w_up",
        "moe_w_down", "final_norm_g"]
_OUTS = [((1, 128, 1024), "float32"), ((1, 128, 1024), "float32"),
         ((1, 1, 128, 16, 64), "float32"), ((1, 1, 128, 16, 64), "float32")]


def kernel(**inputs):
    import numpy as _np
    import concourse.bacc as _bacc
    from concourse import mybir as _mybir
    from concourse.bass_utils import run_bass_kernel_spmd as _run

    nc = _bacc.Bacc("TRN2", target_bir_lowering=False, num_devices=1)
    arrays, args = {}, []
    given = {name: _np.ascontiguousarray(inputs[name]) for name in _INS}
    given.update(host_constants())
    for name, a in given.items():
        arrays[f"in_{name}_dram"] = a
        args.append(nc.dram_tensor(f"in_{name}_dram", a.shape, _mybir.dt.from_np(a.dtype), kind="ExternalInput").ap())
    for i, (shape, dtype) in enumerate(_OUTS):
        dt = _mybir.dt.from_np(_np.dtype(dtype))
        args.append(nc.dram_tensor(f"out_{i}_dram", shape, dt, kind="ExternalOutput").ap())
    build(nc, *args)
    r = _run(nc, [arrays], core_ids=[0])
    return tuple(r.results[0][f"out_{i}_dram"] for i in range(len(_OUTS)))
```

```python
from contextlib import ExitStack

import numpy as np

import concourse.bass as bass
from concourse import mybir

F32 = mybir.dt.float32
F32R = mybir.dt.float32r
I32 = mybir.dt.int32
ALU = mybir.AluOpType
ACT = mybir.ActivationFunctionType
AX_X = mybir.AxisListType.X

P = 128
D = 1024
DB = D // P
SEQ = 128
NSEQ = 2
T = NSEQ * SEQ
DEPTH = 4
HEADS = 16
HD = 64
PAIRS = HEADS // 2
E = 16
GROUP = 4
NG = E // GROUP
F = 512
FB = F // P
SLOTS = 64
MAX_ROUNDS = T // SLOTS
EPS = 1e-6
SCALE = HD ** -0.5
GRID_W = 64
WIN_ROWS, WIN_COLS = 8, 16
MASKED = -1e30

BLOCKS = [("gu", 0), ("gu", 1), ("dn", 0), ("gu", 2), ("dn", 1), ("gu", 3), ("dn", 2), ("dn", 3)]
UNITS = [(kind, e, i) for kind, e in BLOCKS for i in range(DB if kind == "gu" else FB)]
NU = len(UNITS)
FIRST = {b: UNITS.index((b[0], b[1], 0)) for b in BLOCKS}
END = {b: FIRST[b] + (DB if b[0] == "gu" else FB) - 1 for b in BLOCKS}
RAW = 6
PAIR_LOADS = NU // 2
RING = 6
GRANT = 1
RAW_CREDIT = 2 * RAW

END_GU = [END[("gu", e)] for e in range(GROUP)]
END_DN = [END[("dn", e)] for e in range(GROUP)]
GU_COPIED = {END_GU[e] + 4: e for e in range(GROUP)}
PE_TURN = {END_GU[0] + 3: 0, END_GU[1] + 2: 1, END_GU[2] + 2: 2, END_GU[3] + 2: 3}
SILU = {END_GU[0] + 7: 0, END_GU[1] + 6: 1, END_GU[2] + 6: 2, END_GU[3] + 6: 3}
HIDDEN = {END_GU[0] + 6: 0, END_GU[1] + 5: 1, END_GU[2] + 5: 2, END_GU[3] + 5: 3}
LAST_HI, LAST_LO = 4, 3
OUTPUT_HI = {END_DN[0] + 4: 0, END_DN[1] + 4: 1, END_DN[2] + 3: 2}
OUTPUT_LO = {END_DN[0] + 3: 0, END_DN[1] + 3: 1, END_DN[2] + 2: 2}
PE_COMBINE_LAST = {5 + q: q for q in range(4)}
ADD_LAST = {8 + q: q for q in range(4)}
PE_COMBINE_FIRST = {END_DN[1] + 4 + q: q for q in range(4)}
ADD_FIRST = {END_DN[1] + 6 + q: q for q in range(4)}
PE_GATES, PE_ONEHOT_TURN = 9, 12
GATES_COPIED, ONEHOT_COPIED = 13, 16
NEXT_ONEHOT = 24
PE_GATHER = {NU - 7: [0], NU - 6: [1], NU - 5: [2, 3], NU - 4: [4], NU - 3: [5], NU - 2: [6], NU - 1: [7]}
GATHERED = {NU - 3: [0], NU - 2: [1], NU - 1: [2, 3]}
GATHERED_LATE = {0: 4, 1: 5, 2: 6, 3: 7}
FIRST_GATHER_BANKS = [2, 3, 4, 7, 5, 6, 5, 6]

ADA_COLS = 256
ADA_NB = ADA_COLS // P
ADA_CHUNKS = 6 * D // ADA_COLS
ADA_SLOTS = 2
MIX_CHUNKS = 8
MIX_LAYERS = (0, 1, 2)
ADA_PER = [(ADA_CHUNKS - (MIX_CHUNKS if l in MIX_LAYERS else 0)) // NG if l < DEPTH - 1 else 0 for l in range(DEPTH)]
MIX_BANKS = {0: [6, 6, 4, 5, 4, 5, 4, 5], 1: [4, 5, 4, 7, 4, 5, 4, 5], 2: [4, 5, 4, 5, 4, 5, 4, 5]}
MIX_SECOND = {0: 2, 1: 4, 2: 3}
ADA_STEP = 11
PE_ADA = [{1 + ADA_STEP * j: j for j in range(n)} for n in ADA_PER]
PE_ADA_TURN = [{u + 6: j for u, j in at.items()} for at in PE_ADA]
ADA_COPIED = PE_ADA_TURN
ADA_STORED = [{u + 8: j for u, j in at.items()} for at in PE_ADA]
ADA_LOADED = {4: {0: 0, 2: 1, 8: 2, 14: 3}, 0: {}}
MOD_CHUNKS = D // ADA_COLS
FIRST_SLOTS = RAW
FIRST_RING = 4
MIX_LOADED_FIRST = {5: [0, 1], 14: [2], 16: [3], 18: [4], 21: [5], 23: [6, 7]}
MOD_BANK = [4, 5, 6, 5, 6, 4]
NB_MOD = 6 * DB

C_IDENT, C_TRI, C_ONES, C_HALVES, C_IOTA = 0, 128, 256, 384, 448
C_LIMITS, C_BEFORE, C_AFTER, C_FOLD, C_END = 576, 579, 595, 611, 613
WM_COLS = 256
WM_RING = 3


def host_constants():
    i = np.arange(P)
    base = np.zeros((P, C_END), np.float32)
    base[:, C_IDENT:C_IDENT + P] = np.eye(P)
    base[:, C_TRI:C_TRI + P] = i[:, None] < i[None, :]
    base[:, C_ONES:C_ONES + P] = 1.0
    base[:, C_HALVES:C_HALVES + SLOTS] = (i[:, None] % SLOTS) == np.arange(SLOTS)[None, :]
    base[:, C_IOTA:C_IOTA + P] = (i % SLOTS)[None, :]
    base[:, C_LIMITS:C_LIMITS + 3] = SLOTS * np.arange(1, 4)[None, :]
    j = np.arange(GROUP)
    base[:, C_BEFORE:C_BEFORE + 16] = (j[None, :] < j[:, None]).reshape(1, 16)
    base[:, C_AFTER:C_AFTER + 16] = (j[None, :] > j[:, None]).reshape(1, 16)
    base[:4, C_FOLD:C_END] = (i[:4, None] % NSEQ) == np.arange(NSEQ)[None, :]
    pool = np.zeros((P, 4, P), np.float32)
    for g, win in enumerate((2, 4, 8, 16)):
        lo = np.clip(i - win // 2, 0, SEQ)
        hi = np.clip(i - win // 2 + win, 0, SEQ)
        inside = (i[:, None] >= lo[None, :]) & (i[:, None] < hi[None, :])
        pool[:, g, :] = inside / (hi - lo)[None, :] - np.eye(P)
    attn = np.zeros((P, 2, P), np.float32)
    cq = i % GRID_W
    start = np.clip(cq - WIN_COLS // 2, 0, GRID_W - WIN_COLS)
    ok = (cq[None, :] >= start[:, None]) & (cq[None, :] < start[:, None] + WIN_COLS)
    attn[:, 0, :] = np.where(ok, 0.0, MASKED)
    attn[i, 1, (i // GRID_W) * GRID_W + GRID_W - 1 - cq] = 1.0
    four = np.zeros((P, 2 * P + 2 * 512), np.float32)
    wn = 2 * np.pi * np.outer(i, i) / SEQ
    four[:, 0:P] = np.cos(wn) / np.sqrt(SEQ)
    four[:, P:2 * P] = -np.sin(wn) / np.sqrt(SEQ)
    c = np.arange(256)
    wc = 2 * np.pi * np.outer(c, c) / 256
    both = np.concatenate([np.cos(wc), np.sin(wc)], axis=1) / 16.0
    four[:, 2 * P:] = both.reshape(2, P, 512).transpose(1, 0, 2).reshape(P, 1024)
    return {"k_base": base, "k_pool": pool.reshape(P, 512), "k_attn": attn.reshape(P, 256), "k_four": four}


def build(nc, x_prompt, x_sample, cache_k, cache_v, c, c_ctx, ada_w, ada_b, norm1_g, norm2_g, pool_w,
          pool_scale, attn_wqkv, attn_wo, attn_rpb, fourier_w, router_w, router_b, moe_w_gate, moe_w_up,
          moe_w_down, final_norm_g, k_base, k_pool, k_attn, k_four,
          y_prompt, y_sample, new_cache_k, new_cache_v):
    ctx = ExitStack()
    with ctx:
        def sb(name, shape, dt=F32, stack=ctx):
            return stack.enter_context(nc.sbuf_tensor(name, shape, dt))

        def sem(name):
            return ctx.enter_context(nc.semaphore(name))

        xT = sb("xT", [P, DB, T])
        hT = sb("hT", [P, DB, T])
        raw = sb("raw", [P, RAW, 2, D])
        ada_in = sb("ada_in", [P, ADA_SLOTS, DB, ADA_COLS])
        const = sb("const", [P, C_END])
        mods = sb("mods", [P, DEPTH, NB_MOD, NSEQ])
        vecs = sb("vecs", [P, 104])
        adab = sb("adab", [P, DEPTH * NB_MOD])
        ada_row = sb("ada_row", [P, ADA_COLS])
        cond_hl = sb("cond_hl", [P, DB, 2 * NSEQ], F32R)
        cact = sb("cact", [P, NSEQ, DB])
        rw = sb("rw", [P, DB, E])
        rb = sb("rb", [P, E])
        amul = sb("amul", [P, DB, NSEQ])
        pcoef = sb("pcoef", [P, DB, NSEQ])
        ms = sb("ms", [P, T])
        rstd = sb("rstd", [P, T])
        newton = sb("newton", [P, T])
        posx = sb("posx", [P, MAX_ROUNDS * NG + 1, NSEQ, GROUP])
        gx = sb("gx", [P, NG, NSEQ, GROUP])
        rounds = sb("rounds", [P, DEPTH], I32)
        credit = sb("credit", [P, 8])

        ident = const[:, C_IDENT:C_IDENT + P]
        tri = const[:, C_TRI:C_TRI + P]
        ones = const[:, C_ONES:C_ONES + P]
        halves = const[:, C_HALVES:C_HALVES + SLOTS]
        iota = const[:, C_IOTA:C_IOTA + P]
        limits = const[:, C_LIMITS:C_LIMITS + 3]
        before = const[:, C_BEFORE:C_BEFORE + 16]
        after = const[:, C_AFTER:C_AFTER + 16]
        fold = const[0:2 * NSEQ, C_FOLD:C_END]
        cond = vecs[:, 0:16]
        n1g, n2g = vecs[:, 16:48], vecs[:, 48:80]
        fing, pscale = vecs[:, 80:88], vecs[:, 88:104]

        with ExitStack() as moe:
            w_hi = sb("w_hi", [P, RING, D], F32R, moe)
            w_lo = sb("w_lo", [P, RING, D], F32R, moe)
            xg = sb("xg", [P, DB, GROUP, 2 * SLOTS], F32R, moe)
            h_hi = sb("h_hi", [P, NSEQ, D], F32R, moe)
            h_lo = sb("h_lo", [P, NSEQ, D], F32R, moe)
            y_hi = sb("y_hi", [P, 2, D], F32R, moe)
            y_lo = sb("y_lo", [P, 2, D], F32R, moe)
            onehot = sb("onehot", [P, NSEQ, GROUP, 2 * SLOTS], F32R, moe)
            onehotT = sb("onehotT", [P, GROUP, T], F32R, moe)
            gsel = sb("gsel", [P, NSEQ, GROUP], F32, moe)
            gcol = sb("gcol", [P, GROUP], F32, moe)
            gu = sb("gu", [P, 2 * F], F32, moe)
            sg = sb("sg", [P, FB * SLOTS], F32, moe)
            act = sb("act", [P, FB * SLOTS], F32, moe)
            a_hl = sb("a_hl", [P, 2, FB, 2 * SLOTS], F32R, moe)
        with ExitStack() as mix:
            work = sb("work", [P, DB, T], F32, mix)
            wm = sb("wm", [P, WM_RING, DB, WM_COLS], F32, mix)
            mix_rows = sb("mix_rows", [NSEQ, MIX_CHUNKS * ADA_COLS], F32, mix)
            kT = sb("kT", [P, DB, T], F32, mix)
            vtok = sb("vtok", [P, NSEQ, D], F32, mix)
            ck = sb("ck", [P, D], F32, mix)
            cv = sb("cv", [P, D], F32, mix)
            ckT = sb("ckT", [P, DB, SEQ], F32, mix)
            knew = sb("knew", [P, D], F32, mix)
            bias = sb("bias", [P, HEADS, P], F32, mix)
            oT = sb("oT", [P, DB, T], F32, mix)
            soft = sb("soft", [P, 2, 2, 3 * P], F32, mix)
            pT = sb("pT", [P, 2, 2, 3 * P], F32, mix)
            kattn = sb("kattn", [P, 2, P], F32, mix)
            mstat = sb("mstat", [P, 2, 3, 4], F32, mix)
            rpad = sb("rpad", [HEADS, 3, P], F32, mix)
        with ExitStack() as mix2:
            sb("work2", [P, DB, T], F32, mix2)
            ada_rows = sb("ada_rows", [2 * NSEQ, 6 * D], F32, mix2)
            sb("mix_rows2", [NSEQ, MIX_CHUNKS * ADA_COLS], F32, mix2)
            ztok = sb("ztok", [P, 4, NSEQ, 256], F32, mix2)
            kpool = sb("kpool", [P, 4, P], F32, mix2)
            wp = sb("wp", [P, 4, 2, 256], F32, mix2)
            f_hi = sb("f_hi", [P, FIRST_RING, D], F32R, mix2)
            f_lo = sb("f_lo", [P, FIRST_RING, D], F32R, mix2)
        with ExitStack() as mix3:
            sb("work3", [P, DB, T], F32, mix3)
            sb("wm3", [P, WM_RING, DB, WM_COLS], F32, mix3)
            sb("mix_rows3", [NSEQ, MIX_CHUNKS * ADA_COLS], F32, mix3)
            ftok = sb("ftok", [P, NSEQ, 4, 512], F32, mix3)
            fT = sb("fT", [P, DB, T], F32, mix3)
            kfour = sb("kfour", [P, 2 * P + 1024], F32, mix3)
        with ExitStack() as mix4:
            sb("work4", [P, DB, T], F32, mix4)
            sb("wm4", [P, WM_RING, DB, WM_COLS], F32, mix4)
            xio = sb("xio", [P, NSEQ, D], F32, mix4)
            vrow = sb("vrow", [P, 3, P], F32, mix4)
        with ExitStack() as rt:
            sb("rt_w_hi", [P, RING, D], F32R, rt)
            sb("rt_w_lo", [P, RING, D], F32R, rt)
            r_sc = sb("r_sc", [P, NSEQ, E], F32, rt)
            r_sel = sb("r_sel", [P, NSEQ * NG, GROUP], F32, rt)
            r_pair = sb("r_pair", [P, NSEQ * NG, 6], F32, rt)
            r_gs = sb("r_gs", [P, NSEQ, NG], F32, rt)
            r_ge = sb("r_ge", [P, NSEQ * NG, 16], F32, rt)
            r_gt = sb("r_gt", [P, NSEQ * NG, 16], F32, rt)
            r_best = sb("r_best", [P, NSEQ * NG], F32, rt)
            r_rank = sb("r_rank", [P, NSEQ * NG, GROUP], F32, rt)
            r_mask = sb("r_mask", [P, NSEQ, E], F32, rt)
            r_w = sb("r_w", [P, NSEQ, E], F32, rt)
            r_den = sb("r_den", [P, NSEQ], F32, rt)
            r_pm = sb("r_pm", [P, NSEQ, NG, GROUP], F32, rt)
            r_cnt = sb("r_cnt", [P, 8], F32, rt)
        ps = ctx.enter_context(nc.psum_tensor("ps", [P, 8, 512], F32))
        B_G, B_U, B_Y, B_T, B_A, B_M = 0, 1, 2, 4, 5, 7
        bias_dram = nc.dram_tensor("bias_rows", [HEADS, 3, P], F32, kind="Internal").ap()

        s_load = sem("s_load")
        s_load_v = sem("s_load_v")
        s_clo = sem("s_clo")
        s_fhi = sem("s_fhi")
        s_flo = sem("s_flo")
        s_fu = sem("s_fu")
        s_rows = sem("s_rows")
        s_vecs = sem("s_vecs")
        s_cact = sem("s_cact")
        s_xt = sem("s_xt")
        s_xq = sem("s_xq")
        s_sq = sem("s_sq")
        s_ss = sem("s_ss")
        s_ms = sem("s_ms")
        s_rt = sem("s_rt")
        s_n1 = sem("s_n1")
        s_n2 = sem("s_n2")
        s_hq = sem("s_hq")
        s_link = sem("s_link")
        s_lg = sem("s_lg")
        s_sig = sem("s_sig")
        s_mask = sem("s_mask")
        s_pos = sem("s_pos")
        s_tok = sem("s_tok")
        s_thi = sem("s_thi")
        s_tlo = sem("s_tlo")
        s_rounds = sem("s_rounds")
        s_acc0 = sem("s_acc0")
        s_raw = [sem(f"s_raw{k}") for k in range(RAW)]
        s_issue = sem("s_issue")
        s_hi = sem("s_hi")
        s_lo = sem("s_lo")
        s_unit = sem("s_unit")
        s_oh = sem("s_oh")
        s_ga = sem("s_ga")
        s_gev = sem("s_gev")
        s_oht = sem("s_oht")
        s_ohs = sem("s_ohs")
        s_gc = sem("s_gc")
        s_gcs = sem("s_gcs")
        s_gus = sem("s_gus")
        s_turn = sem("s_turn")
        s_silu = sem("s_silu")
        s_prod = sem("s_prod")
        s_ahi = sem("s_ahi")
        s_alo = sem("s_alo")
        s_yhi = sem("s_yhi")
        s_ylo = sem("s_ylo")
        s_comb = sem("s_comb")
        s_acc = sem("s_acc")
        s_ada_in = [sem(f"s_ada_in{k}") for k in range(2)]
        s_ada = sem("s_ada")
        s_adac = sem("s_adac")
        s_adat = sem("s_adat")
        s_posx = sem("s_posx")
        s_adas = sem("s_adas")
        s_mix_in = [sem(f"s_mix_in{k}") for k in range(ADA_SLOTS)]
        s_mixp = sem("s_mixp")
        s_mixr = sem("s_mixr")
        s_mixt = sem("s_mixt")
        s_mixs = sem("s_mixs")
        s_kc = sem("s_kc")
        s_z = sem("s_z")
        s_ze = sem("s_ze")
        s_zo = sem("s_zo")
        s_mix = sem("s_mix")
        s_wm = [sem(f"s_wm{k}") for k in range(WM_RING)]
        s_wmu = sem("s_wmu")
        s_qkve = sem("s_qkve")
        s_qkvo = sem("s_qkvo")
        s_bias = sem("s_bias")
        s_pad = sem("s_pad")
        s_flip = sem("s_flip")
        s_biass = sem("s_biass")
        s_kt = sem("s_kt")
        s_kts = sem("s_kts")
        s_sc = sem("s_sc")
        s_max = sem("s_max")
        s_exp = sem("s_exp")
        s_prob = sem("s_prob")
        s_pt2 = sem("s_pt2")
        s_pts = sem("s_pts")
        s_o = sem("s_o")
        s_os = sem("s_os")
        s_f1 = sem("s_f1")
        s_f1e = sem("s_f1e")
        s_f1o = sem("s_f1o")
        s_f2 = sem("s_f2")
        s_f2s = sem("s_f2s")
        s_yt = sem("s_yt")
        s_yts = sem("s_yts")
        s_out = sem("s_out")
        s_kv = sem("s_kv")

        KINDS = [l % 3 for l in range(DEPTH)]
        N_X_LOADS, N_VECTOR_LOADS = 4, 9
        WM_TILES = [("qkv", i) for i in range(12)] + [("wo", i) for i in range(4)] + [("four", i) for i in range(4)]
        WM_AT = {t: n for n, t in enumerate(WM_TILES)}
        KC_AFTER = [32, 80, 96, 128]

        def first_unit(c, half):
            return raw[:, c % FIRST_SLOTS, half, :]

        FIRST_PER_SLOT = ADA_CHUNKS // FIRST_SLOTS

        def quarter(t, q):
            return t[:, 2 * q:2 * q + 2, :]

        def per_token(v, q):
            return v[:, 2 * q:2 * q + 2, :].unsqueeze(3).to_broadcast([P, 2, NSEQ, SEQ])

        def by_seq(t):
            return t.rearrange("p d (s t) -> p d s t", s=NSEQ)

        def mod(l, n):
            return mods[:, l, n * DB:(n + 1) * DB, :]

        block = ctx.enter_context(nc.Block())

        @block.sync
        def _(sp):
            def load_ada(layer, chunk, slot, landed):
                sp.dma_start(ada_in[:, slot, :, :],
                             ada_w[layer].rearrange("(b p) n -> p b n", p=P)[:, :, bass.ds(chunk * ADA_COLS, ADA_COLS)]
                             ).then_inc(landed[slot], 16)

            def load_units(l, e, q):
                kind, _, i = UNITS[2 * q]
                slot = q % RAW
                if kind == "gu":
                    rows = slice(i * P, (i + 2) * P)
                    for n, w in enumerate((moe_w_gate, moe_w_up)):
                        sp.dma_start(raw[:, slot, :, n * F:(n + 1) * F],
                                     w[l, e, rows, :].rearrange("(b p) f -> p b f", p=P)).then_inc(s_raw[slot], 16)
                else:
                    for n in range(2):
                        sp.dma_start(raw[:, slot, n, :],
                                     moe_w_down[l, e, (i + n) * P:(i + n + 1) * P, :]).then_inc(s_raw[slot], 16)

            sp.wait_ge(s_load_v, 16 * N_VECTOR_LOADS)
            for c in range(ADA_CHUNKS):
                k = c % FIRST_SLOTS
                if c == 2:
                    sp.wait_ge(s_load, 16 * N_X_LOADS)
                if c >= FIRST_SLOTS:
                    sp.wait_ge(s_flo, 2 * (c - FIRST_SLOTS + 1))
                dst = raw[:, k, :, :].rearrange("p t (b n) -> p (t b) n", n=ADA_COLS)
                sp.dma_start(dst, ada_w[0].rearrange("(b p) n -> p b n", p=P)[:, :, c * ADA_COLS:(c + 1) * ADA_COLS]
                             ).then_inc(s_raw[c % FIRST_SLOTS], 16)
                for i in MIX_LOADED_FIRST.get(c, []):
                    if i >= ADA_SLOTS:
                        sp.wait_ge(s_mixp, i - 1)
                    load_ada(1, i, i % ADA_SLOTS, s_mix_in)
            sp.wait_ge(s_flo, 2 * ADA_CHUNKS)

            base = ada_base = 0
            for l in range(DEPTH):
                if l in MIX_LAYERS:
                    for i in range(MIX_CHUNKS if l > 0 else 0):
                        m = MIX_CHUNKS * MIX_LAYERS.index(l) + i
                        if i == 0:
                            sp.wait_ge(s_ada, ada_base + ADA_CHUNKS)
                            sp.sem_inc(s_issue, 1)
                        elif i >= ADA_SLOTS:
                            sp.wait_ge(s_mixp, m - 1)
                        load_ada(l + 1, i, i % ADA_SLOTS, s_mix_in)
                    sp.wait_ge(s_mixp, MIX_CHUNKS * (MIX_LAYERS.index(l) + 1))

                def group(k):
                    it = base + k
                    g = k & (NG - 1)
                    per = ADA_PER[l]

                    def ada_chunk(j):
                        sp.wait_ge(s_ada, ada_base + k * per + (ADA_CHUNKS - 1 + j))
                        sp.sem_inc(s_issue, 1)
                        load_ada(l + 1, g * per + (ADA_CHUNKS - NG * per + j), j % ADA_SLOTS, s_ada_in)

                    for q in range(PAIR_LOADS):
                        if q in ADA_LOADED[per]:
                            ada_chunk(ADA_LOADED[per][q])
                        sp.wait_ge(s_lo, it * NU + 2 * q + 2)
                        sp.sem_inc(s_issue, 1)
                        load_units(l, g * GROUP + UNITS[2 * q][1], q)

                with sp.Fori(0, NG) as k:
                    group(k)
                sp.wait_ge(s_rounds, l + 1)
                n = sp.value_load(rounds[0:1, l:l + 1], min_val=1, max_val=MAX_ROUNDS)
                with sp.If(n > 1):
                    with sp.Fori(NG, n * NG) as k:
                        group(k)
                base = sp.snap(base + n * NG)
                ada_base = sp.snap(ada_base + n * (NG * ADA_PER[l]))
            sp.wait_ge(s_yts, 4)
            sp.dma_start(y_prompt[0], xio[:, 0, :]).then_inc(s_out, 16)
            sp.dma_start(y_sample[0], xio[:, 1, :]).then_inc(s_out, 16)
            sp.wait_ge(s_out, 32)

        @block.gpsimd
        def _(pool):
            nc.gpsimd.memset(credit[:, 0:1], 0.0).then_inc(s_lo, RAW_CREDIT)
            nc.gpsimd.memset(credit[:, 1:2], 0.0).then_inc(s_unit, RING)
            nc.gpsimd.memset(credit[:, 7:8], 0.0).then_inc(s_ada, ADA_CHUNKS)
            for n, s in enumerate((s_turn, s_prod, s_gus, s_acc, s_ylo)):
                nc.gpsimd.memset(credit[:, 2 + n:3 + n], 0.0).then_inc(s, GRANT)
            loads = [
                (xio[:, 0, :], x_prompt[0]),
                (xio[:, 1, :], x_sample[0]),
                (rw[:, :, :], router_w.rearrange("(b p) e -> p b e", p=P)),
                (rb[:, :], router_b.partition_broadcast(P)),
            ]
            assert len(loads) == N_X_LOADS
            for dst, src in loads:
                pool.dma_start(dst, src).then_inc(s_load, 16)

            def weight_tile(name, i):
                n = WM_AT[(name, i)]
                if n >= WM_RING:
                    pool.wait_ge(s_wmu, n - WM_RING + 1)
                src = {"qkv": attn_wqkv, "wo": attn_wo, "four": fourier_w}[name][0]
                pool.dma_start(wm[:, n % WM_RING, :, :],
                               src.rearrange("(b p) n -> p b n", p=P)[:, :, i * WM_COLS:(i + 1) * WM_COLS]
                               ).then_inc(s_wm[n % WM_RING], 16)

            for l in range(DEPTH):
                pool.wait_ge(s_xq, 4 * (2 * l) + 4)
                if KINDS[l] == 0:
                    j = l // 3
                    if l == 0:
                        pool.wait_ge(s_vecs, 2)
                    pool.dma_start(kpool[:, :, :], k_pool).then_inc(s_kc, 16)
                    pool.dma_start(wp[:, :, :, :], pool_w[j].rearrange("g (b p) d -> p g b d", p=P)).then_inc(s_kc, 16)
                elif KINDS[l] == 1:
                    for i in range(3):
                        weight_tile("qkv", i)
                    pool.dma_start(kattn[:, :, :], k_attn).then_inc(s_kc, 16)
                    pool.dma_start(ck[:, :], cache_k[0, 0].rearrange("m h d -> m (h d)")).then_inc(s_kc, 16)
                    pool.dma_start(cv[:, :], cache_v[0, 0].rearrange("m h d -> m (h d)")).then_inc(s_kc, 16)
                    nc.gpsimd.memset(rpad[:, :, :], 0.0).then_inc(s_pad, 1)
                    pool.wait_ge(s_pad, 1)
                    pool.dma_start(rpad[:, :, 48:79], attn_rpb[0, :, WIN_ROWS - 2:WIN_ROWS + 1, :]).then_inc(s_bias, 16)
                    pool.wait_ge(s_bias, 16)
                    pool.dma_start(bias_dram, rpad[:, :, :]).then_inc(s_bias, 16)
                    pool.wait_ge(s_bias, 32)
                    for r in range(2):
                        for kr in range(2):
                            src = bass.AP(tensor=bias_dram.tensor, offset=(kr - r + 1) * P,
                                          ap=[[1, GRID_W], [3 * P, HEADS], [1, GRID_W]])
                            dst = oT[r * GRID_W:(r + 1) * GRID_W, :, :].rearrange("p d t -> p (d t)").rearrange(
                                "p (h k) -> p h k", h=HEADS)[:, :, kr * GRID_W:(kr + 1) * GRID_W]
                            pool.dma_start(dst, src).then_inc(s_bias, 16)
                    for i in range(3, 12):
                        weight_tile("qkv", i)
                    for i in range(4):
                        weight_tile("wo", i)
                    pool.wait_ge(s_kts, 4)
                    pool.dma_start(new_cache_k[0, 0].rearrange("m h d -> m (h d)"), knew[:, :]).then_inc(s_kv, 16)
                    pool.wait_ge(s_qkve, 6)
                    pool.wait_ge(s_qkvo, 6)
                    pool.dma_start(new_cache_v[0, 0].rearrange("m h d -> m (h d)"), vtok[:, 0, :]).then_inc(s_kv, 16)
                    pool.wait_ge(s_kv, 32)
                else:
                    pool.dma_start(kfour[:, :], k_four).then_inc(s_kc, 16)
                    for i in range(4):
                        weight_tile("four", i)
                pool.wait_ge(s_tok, 4 * (l + 1))
                nc.gpsimd.memset(hT[:, :, :], 0.0).then_inc(s_acc0, 1)
                nc.gpsimd.memset(y_hi[:, 0, :].bitcast(F32), 0.0).then_inc(s_acc0, 1)
                nc.gpsimd.memset(y_lo[:, 0, :].bitcast(F32), 0.0).then_inc(s_acc0, 1)
                nc.gpsimd.memset(onehotT[:, 2:4, :].bitcast(F32), 0.0).then_inc(s_acc0, 1)

        @block.scalar
        def _(ac):
            loads = [
                (const[:, :], k_base),
                (vrow[0:8, 0, :], c_ctx.rearrange("(b p) -> b p", p=P)),
                (vrow[8:16, 0, :], c.rearrange("a (b p) -> (a b) p", p=P)),
                (vrow[16:48, 0, :], norm1_g.rearrange("l (b p) -> (l b) p", p=P)),
                (vrow[48:80, 0, :], norm2_g.rearrange("l (b p) -> (l b) p", p=P)),
                (vrow[80:88, 0, :], final_norm_g.rearrange("(b p) -> b p", p=P)),
                (vrow[88:104, 0, :], pool_scale.rearrange("l (b p) -> (l b) p", p=P)),
                (vrow[0:96, 1, :], ada_b[0:2].rearrange("l (b p) -> (l b) p", p=P)),
                (vrow[0:96, 2, :], ada_b[2:4].rearrange("l (b p) -> (l b) p", p=P)),
            ]
            assert len(loads) == N_VECTOR_LOADS
            for dst, src in loads:
                ac.dma_start(dst, src).then_inc(s_load_v, 16)
            ac.wait_ge(s_vecs, 1)
            nc.scalar.activation(cact[:, :, :], cond.rearrange("p (s b) -> p s b", s=NSEQ), ACT.Silu).then_inc(s_cact, 1)
            ac.wait_ge(s_cact, 1)
            nc.scalar.activation(cond_hl[:, :, 0:NSEQ], cact[:, :, :].rearrange("p s b -> p b s"), ACT.Copy).then_inc(s_cact, 1)

            def ada_copy(count):
                ac.wait_ge(s_ada, count + 1)
                ac.wait_ge(s_adat, count - (ADA_CHUNKS - 6))
                nc.scalar.activation(ada_row[0:NSEQ, :], ps[0:NSEQ, B_M, T:T + ADA_COLS], ACT.Copy).then_inc(s_adac, 1)

            def split_first(c):
                if c >= ADA_CHUNKS:
                    return
                ac.wait_ge(s_raw[c % FIRST_SLOTS], 16 * (c // FIRST_SLOTS + 1))
                for half in range(2):
                    u = 2 * c + half
                    if u >= FIRST_RING:
                        ac.wait_ge(s_fu, u - FIRST_RING + 1)
                    nc.scalar.activation(f_hi[:, u % FIRST_RING, :], first_unit(c, half), ACT.Copy).then_inc(s_fhi, 1)

            def first_chunks(a, b):
                for c in range(a, b):
                    ac.wait_ge(s_fu, 2 * c + 2)
                    nc.scalar.activation(ada_rows[:, c * ADA_COLS:(c + 1) * ADA_COLS],
                                         ps[0:2 * NSEQ, B_M, T:T + ADA_COLS], ACT.Copy).then_inc(s_adac, 1)
                    split_first(c + 2)

            def norm(n):
                for q in range(4):
                    ac.wait_ge(s_xq, 4 * n + q + 1)
                    if n == 0 and q == 0:
                        ac.wait_ge(s_xt, 4)
                    nc.scalar.activation(quarter(work, q), quarter(xT, q), ACT.Square).then_inc(s_sq, 1)
                if n == 0:
                    first_chunks(2, 4)
                ac.wait_ge(s_ms, n + 1)
                nc.scalar.activation(rstd[:, :], ms[:, :], ACT.Sqrt).then_inc(s_rt, 1)

            def router(l):
                if KINDS[l] == 1:
                    ac.wait_ge(s_kv, 32)
                ac.wait_ge(s_lg, l + 1)
                nc.scalar.activation(r_sc[:, :, :], ps[:, B_M, 0:2 * E].rearrange("p (s e) -> p s e", s=NSEQ),
                                     ACT.Sigmoid).then_inc(s_sig, 1)
                for b in range(4):
                    ac.wait_ge(s_tok, 4 * l + b + 1)
                    nc.scalar.activation(h_hi[:, b // 2, (b % 2) * 512:(b % 2 + 1) * 512], ps[:, b, :],
                                         ACT.Copy).then_inc(s_thi, 1)
                if l in MIX_LAYERS:
                    mixer_rows(l, MIX_CHUNKS - 1, MIX_CHUNKS)

            def mixer_rows(l, a, b):
                for i in range(a, b):
                    ac.wait_ge(s_mixp, MIX_CHUNKS * MIX_LAYERS.index(l) + i + 1)
                    nc.scalar.activation(mix_rows[:, i * ADA_COLS:(i + 1) * ADA_COLS],
                                         ps[0:NSEQ, MIX_BANKS[l][i], T:T + ADA_COLS], ACT.Copy).then_inc(s_mixr, 1)

            def mixer_attention(l):
                for t in range(0, 12, 2):
                    ac.wait_ge(s_wmu, t + 1)
                    bank = ps[:, t % 4, :]
                    if t < 8:
                        dst = quarter(work if t < 4 else kT, t % 4)
                        nc.scalar.activation(dst, bank.rearrange("p (d t) -> p d t", d=2), ACT.Copy).then_inc(s_qkve, 1)
                    else:
                        nc.scalar.activation(vtok[:, :, (t - 8) * 256:(t - 7) * 256],
                                             bank.rearrange("p (s n) -> p s n", s=NSEQ), ACT.Copy).then_inc(s_qkve, 1)
                for b in range(4):
                    ac.wait_ge(s_kt, b + 1)
                    dst = (ckT[:, (b % 2) * 4:(b % 2) * 4 + 4, :].rearrange("p d t -> p (d t)") if b < 2
                           else knew[:, (b % 2) * 512:(b % 2 + 1) * 512])
                    nc.scalar.activation(dst, ps[:, 4 + b, :], ACT.Copy).then_inc(s_kts, 1)

                def exps(hp):
                    ac.wait_ge(s_max, hp + 1)
                    for e in range(2):
                        for part, (a, b) in enumerate(((0, P), (P, 3 * P))):
                            v = soft[:, hp % 2, e, a:b]
                            nc.scalar.activation(v, v, ACT.Exp, bias=mstat[:, hp % 2, 1, 2 * e + part:2 * e + part + 1],
                                                 accum_out=mstat[:, hp % 2, 2, 2 * e + part:2 * e + part + 1]
                                                 ).then_inc(s_exp, 1)

                def copy_turned(hp):
                    ac.wait_ge(s_pt2, hp + 1)
                    if hp >= 2:
                        ac.wait_ge(s_o, hp - 1)
                    nc.scalar.activation(pT[:, hp % 2, :, :], ps[:, 4:6, 0:3 * P], ACT.Copy).then_inc(s_pts, 1)

                exps(0)
                exps(1)
                mixer_rows(l, 3, 4)
                copy_turned(0)
                for hp in range(PAIRS):
                    if hp + 1 < PAIRS:
                        copy_turned(hp + 1)
                    if hp + 2 < PAIRS:
                        exps(hp + 2)

            def mixer_pool(l):
                j = l // 3
                for g in range(0, 4, 2):
                    ac.wait_ge(s_z, 4 * j + g + 1)
                    nc.scalar.activation(ztok[:, g, :, :].rearrange("p s n -> p (s n)"), ps[:, g, :],
                                         ACT.Copy).then_inc(s_ze, 1)

            def mixer_fourier():
                for b in range(0, 8, 2):
                    ac.wait_ge(s_f1, b + 1)
                    nc.scalar.activation(ftok[:, b // 4, b % 4, :], ps[:, b, :], ACT.Copy).then_inc(s_f1e, 1)
                for g in range(4):
                    ac.wait_ge(s_f2, g + 1)
                    nc.scalar.activation(quarter(fT, g), ps[:, g, :].rearrange("p (d t) -> p d t", d=2),
                                         ACT.Copy).then_inc(s_f2s, 1)

            base = ada_base = 0
            for l in range(DEPTH):
                if l == 0:
                    split_first(0)
                    split_first(1)
                    first_chunks(0, 2)
                norm(2 * l)
                if l == 0:
                    first_chunks(4, 8)
                    mixer_rows(l, 0, 1)
                    first_chunks(8, 10)
                    mixer_rows(l, 1, 2)
                if KINDS[l] == 0:
                    mixer_pool(l)
                if l == 0:
                    first_chunks(10, 12)
                if l in MIX_LAYERS and l > 0:
                    mixer_rows(l, 0, 3)
                if KINDS[l] == 1:
                    mixer_attention(l)
                if KINDS[l] == 2:
                    mixer_fourier()
                norm(2 * l + 1)
                if l in MIX_LAYERS and l > 0:
                    mixer_rows(l, MIX_SECOND[l], MIX_CHUNKS - 1)
                if l == 0:
                    mixer_rows(l, 2, 3)
                    for i in range(4):
                        first_chunks(12 + 3 * i, 15 + 3 * i)
                        mixer_rows(l, 3 + i, 4 + i)
                router(l)

                def gathered(gi, db, bank=None):
                    ac.wait_ge(s_ga, gi * 8 + (db + 1))
                    nc.scalar.activation(
                        xg[:, db, :, :].rearrange("p e (h s) -> p h e s", h=2),
                        ps[:, B_A + db % 2 if bank is None else bank, :].rearrange("p (h e s) -> p h e s", h=2, e=GROUP),
                        ACT.Copy).then_inc(s_gev, 1)

                def output_hi(e, it48, it8, it):
                    if e == 3:
                        ac.wait_ge(s_unit, it48 + RING)
                    else:
                        ac.wait_ge(s_unit, it48 + (RING + END_DN[e] + 1))
                        if e == 0:
                            ac.wait_ge(s_gcs, it + 1)
                        if e % 2 == 0:
                            ac.wait_ge(s_comb, it8 + (4 * l + 4 + 2 * e))
                    for b in range(2):
                        nc.scalar.activation(y_hi[:, e % 2, b * 512:(b + 1) * 512], ps[:, B_Y + b, :], ACT.Copy,
                                             scale=gcol[:, e:e + 1]).then_inc(s_yhi, 1)

                first = ac.snap(base + l)
                for db in range(4):
                    gathered(first, db, FIRST_GATHER_BANKS[db])
                ac.wait_ge(s_rounds, l + 1)
                n = ac.value_load(rounds[0:1, l:l + 1], min_val=1, max_val=MAX_ROUNDS)
                with ac.Fori(0, n * NG) as k:
                    it = ac.snap(base + k)
                    ada_it = ac.snap(ada_base + k * ADA_PER[l])
                    it8 = ac.snap(it * 8)
                    it48 = ac.snap(it * NU)
                    gi = ac.snap(it + l)
                    following = ac.snap(it + (l + 1))

                    def split_hi(u):
                        slot = (u // 2) % RAW
                        if u % 2 == 0:
                            ac.wait_ge(s_raw[slot], it * (32 * PAIR_LOADS // RAW) +
                                       (16 * FIRST_PER_SLOT + 32 * (u // 2 // RAW + 1)))
                        ac.wait_ge(s_unit, it48 + (u + 1))
                        nc.scalar.activation(w_hi[:, u % RING, :], raw[:, slot, u % 2, :], ACT.Copy).then_inc(s_hi, 1)

                    for u in range(NU):
                        split_hi(u)
                        if u in GU_COPIED:
                            e = GU_COPIED[u]
                            ac.wait_ge(s_unit, it48 + (RING + END_GU[e] + 1))
                            ac.wait_ge(s_turn, it * GROUP + e + GRANT)
                            for b in range(2):
                                nc.scalar.activation(gu[:, b * F:(b + 1) * F], ps[:, B_G + b, :], ACT.Copy).then_inc(s_gus, 1)
                        if u == ONEHOT_COPIED:
                            for b in range(2):
                                ac.wait_ge(s_oht, it * 2 + (b + 1))
                                nc.scalar.activation(onehotT[:, 2 * b:2 * b + 2, :], ps[:, B_A + b, :].rearrange(
                                    "p (e t) -> p e t", e=2), ACT.Copy).then_inc(s_ohs, 1)
                        if u in SILU:
                            e = SILU[u]
                            ac.wait_ge(s_turn, it * GROUP + (e + 1) + GRANT)
                            ac.wait_ge(s_prod, it * GROUP + e + GRANT)
                            nc.scalar.activation(sg[:, :], ps[:, B_T, 0:FB * SLOTS], ACT.Silu).then_inc(s_silu, 1)
                        if u == LAST_HI:
                            output_hi(3, it48, it8, it)
                        if u in GATHERED_LATE:
                            gathered(gi, GATHERED_LATE[u])
                        if u in OUTPUT_HI:
                            output_hi(OUTPUT_HI[u], it48, it8, it)
                        for db in GATHERED.get(u, []):
                            gathered(following, db)
                        if u in ADA_COPIED[l]:
                            ada_copy(ada_it + (ADA_CHUNKS + ADA_COPIED[l][u]))
                base = ac.snap(base + n * NG)
                ada_base = ac.snap(ada_base + n * (NG * ADA_PER[l]))
                for db in range(4, DB):
                    gathered(base + l, db)
                output_hi(3, base * NU, None, None)
            norm(2 * DEPTH)
            for b in range(4):
                ac.wait_ge(s_yt, b + 1)
                nc.scalar.activation(xio[:, b // 2, (b % 2) * 512:(b % 2 + 1) * 512], ps[:, b, :], ACT.Copy).then_inc(s_yts, 1)

        @block.vector
        def _(v):
            links = [0]

            def link(ins):
                links[0] += 1
                ins.then_inc(s_link, 1)
                v.wait_ge(s_link, links[0])

            v.wait_ge(s_rows, 1)
            v.tensor_copy(vecs[:, :], ps[:, 4, 0:104]).then_inc(s_vecs, 1)
            v.wait_ge(s_rows, 3)
            v.tensor_copy(adab[:, :], ps[:, 5, 0:192]).then_inc(s_vecs, 1)
            v.wait_ge(s_cact, 2)
            v.tensor_tensor(cond_hl[:, :, NSEQ:2 * NSEQ], cact[:, :, :].rearrange("p s b -> p b s"),
                            cond_hl[:, :, 0:NSEQ].bitcast(F32), ALU.subtract).then_inc(s_clo, 1)

            def split_first(a, b):
                for u in range(2 * a, 2 * b):
                    v.wait_ge(s_fhi, u + 1)
                    v.tensor_tensor(f_lo[:, u % FIRST_RING, :], first_unit(u // 2, u % 2),
                                    f_hi[:, u % FIRST_RING, :].bitcast(F32), ALU.subtract).then_inc(s_flo, 1)

            split_first(0, 2)
            for q in range(4):
                v.wait_ge(s_xt, q + 1)
                v.tensor_copy(quarter(xT, q), ps[:, q, :].rearrange("p (d t) -> p d t", d=2)).then_inc(s_xq, 1)
            split_first(2, 6)
            v.wait_ge(s_vecs, 2)

            def store_ada(layer, chunk, count):
                m = mods[:, layer, :, :].rearrange("p n s -> p (n s)")[:, bass.ds(chunk * (ADA_NB * 2), ADA_NB * 2)]
                bb = adab[:, layer * NB_MOD:(layer + 1) * NB_MOD][:, bass.ds(chunk * ADA_NB, ADA_NB)]
                v.wait_ge(s_adat, count)
                v.tensor_tensor(m.rearrange("p (n s) -> p n s", s=NSEQ),
                                ps[:, B_M, 0:2 * ADA_NB].rearrange("p (n s) -> p n s", s=NSEQ),
                                bb.unsqueeze(2).to_broadcast([P, ADA_NB, NSEQ]), ALU.add).then_inc(s_adas, 1)

            def store_first(a, b):
                for n in range(a, b):
                    v.wait_ge(s_adat, n + 1)
                    v.tensor_tensor(mod(0, n), ps[:, MOD_BANK[n], 0:2 * DB].rearrange("p (n s) -> p n s", s=NSEQ),
                                    adab[:, n * DB:(n + 1) * DB].unsqueeze(2).to_broadcast([P, DB, NSEQ]),
                                    ALU.add).then_inc(s_adas, 1)
                v.wait_ge(s_adas, b)

            v.memset(posx[:, MAX_ROUNDS * NG, :, :], -1.0).then_inc(s_posx, 1)
            v.memset(ada_row[:, :], 0.0).then_inc(s_posx, 1)

            def norm(n, gain, scale, shift, stores=None):
                g2 = gain.unsqueeze(2).to_broadcast([P, DB, NSEQ])

                def gain_and_scale():
                    if scale is None:
                        link(v.tensor_copy(amul[:, :, :], g2))
                    else:
                        link(v.scalar_tensor_tensor(amul[:, :, :], scale, 1.0, g2, ALU.add, ALU.mult))

                def times_gain(q, src, done):
                    v.tensor_tensor(by_seq(quarter(hT, q)), by_seq(quarter(src, q)), per_token(amul, q),
                                    ALU.mult).then_inc(done, 1)

                def times_rstd(q, src, done):
                    v.tensor_tensor(quarter(hT, q), quarter(src, q), rstd[:, :].unsqueeze(1).to_broadcast([P, 2, T]),
                                    ALU.mult).then_inc(done, 1)

                if stores is None:
                    gain_and_scale()
                    for q in range(4):
                        v.wait_ge(s_xq, 4 * n + q + 1)
                        times_gain(q, xT, s_n1)
                v.wait_ge(s_ss, n + 1)
                v.tensor_scalar(ms[:, :], ps[:, B_M, 0:T], 1.0 / D, EPS, ALU.mult, ALU.add).then_inc(s_ms, 1)
                v.wait_ge(s_rt, n + 1)
                link(v.reciprocal(rstd[:, :], rstd[:, :]))
                link(v.scalar_tensor_tensor(newton[:, :], rstd[:, :], -0.5, rstd[:, :], ALU.mult, ALU.mult))
                link(v.tensor_tensor(newton[:, :], newton[:, :], ms[:, :], ALU.mult))
                link(v.scalar_tensor_tensor(rstd[:, :], newton[:, :], 1.5, rstd[:, :], ALU.add, ALU.mult))
                if stores is not None:
                    for q in range(4):
                        times_rstd(q, xT, s_n1)
                    chunks, vectors = stores
                    split_first(*chunks)
                    store_first(*vectors)
                    gain_and_scale()
                last = s_hq if shift is None else s_n2
                for q in range(4):
                    v.wait_ge(s_n1, 4 * n + q + 1)
                    if stores is None:
                        times_rstd(q, hT, last)
                    else:
                        times_gain(q, hT, last)
                if shift is not None:
                    for q in range(4):
                        h = by_seq(quarter(hT, q))
                        v.wait_ge(s_n2, 4 * n + q + 1)
                        v.tensor_tensor(h, h, per_token(shift, q), ALU.add).then_inc(s_hq, 1)

            def residual(src, coef, q):
                for d in range(2):
                    for s in range(NSEQ):
                        x = xT[:, 2 * q + d, s * SEQ:(s + 1) * SEQ]
                        ins = v.scalar_tensor_tensor(x, src(d, s), coef[:, 2 * q + d, s:s + 1], x, ALU.mult, ALU.add)
                ins.then_inc(s_xq, 1)

            def residual_from_banks(done, before, coef, first_bank):
                for q in range(4):
                    v.wait_ge(done, before + q + 1)
                    bank = ps[:, first_bank + q, :]
                    residual(lambda d, s: bank[:, (2 * d + s) * SEQ:(2 * d + s + 1) * SEQ], coef, q)

            def mixer_pool(l):
                j = l // 3
                if l == 0:
                    split_first(8, 10)
                for g in range(1, 4, 2):
                    v.wait_ge(s_z, 4 * j + g + 1)
                    v.tensor_copy(ztok[:, g, :, :].rearrange("p s n -> p (s n)"), ps[:, g, :]).then_inc(s_zo, 1)
                if l == 0:
                    split_first(10, 12)
                    store_first(2, 3)
                gain = pscale[:, j * DB:(j + 1) * DB].unsqueeze(2).to_broadcast([P, DB, NSEQ])
                link(v.tensor_tensor(pcoef[:, :, :], mod(l, 2), gain, ALU.mult))
                residual_from_banks(s_mix, 4 * j, pcoef, 0)
                if l == 0:
                    split_first(12, 14)

            def mixer_attention(l):
                for t in range(1, 12, 2):
                    v.wait_ge(s_wmu, t + 1)
                    bank = ps[:, t % 4, :]
                    if t < 8:
                        dst = quarter(work if t < 4 else kT, t % 4)
                        v.tensor_copy(dst, bank.rearrange("p (d t) -> p d t", d=2)).then_inc(s_qkvo, 1)
                    else:
                        v.tensor_copy(vtok[:, :, (t - 8) * 256:(t - 7) * 256],
                                      bank.rearrange("p (s n) -> p s n", s=NSEQ)).then_inc(s_qkvo, 1)

                v.wait_ge(s_kc, KC_AFTER[l])
                mask = kattn[:, 0, :].unsqueeze(1).to_broadcast([P, 4, P])
                for b in range(4):
                    v.wait_ge(s_flip, b + 1)
                    v.tensor_tensor(bias[:, 4 * b:4 * b + 4, :], ps[:, 4 + b, :].rearrange("p (h k) -> p h k", h=4),
                                    mask, ALU.add).then_inc(s_biass, 1)

                def scale_bias_max(hp):
                    par = hp % 2
                    v.wait_ge(s_sc, hp + 1)
                    if hp >= 2:
                        v.wait_ge(s_pt2, hp - 1)
                    else:
                        v.wait_ge(s_biass, 4)
                    banks = ps[:, 2 * par:2 * par + 2, 0:3 * P]
                    v.tensor_scalar(soft[:, par, :, 0:P], banks[:, :, 0:P], SCALE, None, ALU.mult)
                    v.tensor_scalar(soft[:, par, :, 2 * P:3 * P], banks[:, :, 2 * P:3 * P], SCALE, None, ALU.mult)
                    link(v.scalar_tensor_tensor(soft[:, par, :, P:2 * P], banks[:, :, P:2 * P], SCALE,
                                                bias[:, 2 * hp:2 * hp + 2, :], ALU.mult, ALU.add))
                    v.tensor_reduce(mstat[:, par, 0, 0:4:2], soft[:, par, :, 0:P], AX_X, ALU.max)
                    link(v.tensor_reduce(mstat[:, par, 0, 1:4:2], soft[:, par, :, P:3 * P], AX_X, ALU.max))
                    v.tensor_scalar(mstat[:, par, 1, :], mstat[:, par, 0, :], -1.0, None, ALU.mult).then_inc(s_max, 1)

                def normalise(hp):
                    par = hp % 2
                    v.wait_ge(s_exp, 4 * hp + 4)
                    link(v.reciprocal(mstat[:, par, 0, :], mstat[:, par, 2, :]))
                    for part, (a, b) in enumerate(((0, P), (P, 3 * P))):
                        r = mstat[:, par, 0, part:4:2].unsqueeze(2).to_broadcast([P, 2, b - a])
                        ins = v.tensor_tensor(soft[:, par, :, a:b], soft[:, par, :, a:b], r, ALU.mult)
                    ins.then_inc(s_prob, 1)

                def copy_output(hp):
                    v.wait_ge(s_o, hp + 1)
                    v.tensor_copy(oT[:, hp, :], ps[:, 6 + hp % 2, 0:T]).then_inc(s_os, 1)

                scale_bias_max(0)
                scale_bias_max(1)
                normalise(0)
                for hp in range(PAIRS):
                    if hp + 1 < PAIRS:
                        normalise(hp + 1)
                    if hp >= 1:
                        copy_output(hp - 1)
                    if hp + 2 < PAIRS:
                        scale_bias_max(hp + 2)
                copy_output(PAIRS - 1)
                residual_from_banks(s_wmu, WM_AT[("wo", 0)], mod(l, 2), 0)

            def mixer_fourier(l):
                for b in range(1, 8, 2):
                    v.wait_ge(s_f1, b + 1)
                    v.tensor_copy(ftok[:, b // 4, b % 4, :], ps[:, b, :]).then_inc(s_f1o, 1)
                residual_from_banks(s_wmu, WM_AT[("four", 0)], mod(l, 2), 0)

            def router(l):
                v.wait_ge(s_sig, l + 1)
                sc = r_sc[:, :, :]
                link(v.tensor_tensor(r_sel[:, :, :].rearrange("p (s g) e -> p s (g e)", s=NSEQ), sc,
                                     rb[:, :].unsqueeze(1).to_broadcast([P, NSEQ, E]), ALU.add))
                sel = r_sel[:, :, :]
                at = 0
                for i in range(3):
                    m = 3 - i
                    ins = v.tensor_tensor(r_pair[:, :, at:at + m], sel[:, :, i:i + 1].to_broadcast([P, NSEQ * NG, m]),
                                          sel[:, :, i + 1:4], ALU.add)
                    at += m
                link(ins)
                gs = r_gs[:, :, :].rearrange("p s g -> p (s g)")
                link(v.tensor_reduce(gs, r_pair[:, :, :], AX_X, ALU.max))

                def rank(out, val, n):
                    vi = val.unsqueeze(3).to_broadcast([P, n, 4, 4])
                    vj = val.unsqueeze(2).to_broadcast([P, n, 4, 4])
                    ge = r_ge[:, 0:n, :].rearrange("p n (i j) -> p n i j", i=4)
                    gt = r_gt[:, 0:n, :].rearrange("p n (i j) -> p n i j", i=4)
                    v.tensor_tensor(ge, vj, vi, ALU.is_ge)
                    link(v.tensor_tensor(gt, vj, vi, ALU.is_gt))
                    v.tensor_tensor(r_ge[:, 0:n, :], r_ge[:, 0:n, :], before.unsqueeze(1).to_broadcast([P, n, 16]), ALU.mult)
                    link(v.tensor_tensor(r_gt[:, 0:n, :], r_gt[:, 0:n, :], after.unsqueeze(1).to_broadcast([P, n, 16]), ALU.mult))
                    link(v.tensor_tensor(r_ge[:, 0:n, :], r_ge[:, 0:n, :], r_gt[:, 0:n, :], ALU.add))
                    link(v.tensor_reduce(out, ge, AX_X, ALU.add))

                best = r_best[:, :]
                rank(best.rearrange("p (s g) -> p s g", s=NSEQ), r_gs[:, :, :], NSEQ)
                link(v.tensor_scalar(best, best, 0.0, None, ALU.is_equal))
                rank(r_rank[:, :, :], sel, NSEQ * NG)
                link(v.tensor_scalar(r_rank[:, :, :], r_rank[:, :, :], 2.0, None, ALU.is_lt))
                mask = r_mask[:, :, :]
                v.tensor_tensor(mask.rearrange("p s (g e) -> p (s g) e", e=GROUP), r_rank[:, :, :],
                                best.unsqueeze(2).to_broadcast([P, NSEQ * NG, GROUP]), ALU.mult).then_inc(s_mask, 1)
                v.wait_ge(s_mask, l + 1)
                link(v.tensor_tensor(r_w[:, :, :], sc, mask, ALU.mult))
                link(v.tensor_reduce(r_den[:, :], r_w[:, :, :], AX_X, ALU.add))
                link(v.reciprocal(r_den[:, :], r_den[:, :]))
                for s in range(NSEQ):
                    v.tensor_scalar(gx[:, :, s, :], r_w[:, s, :].rearrange("p (g e) -> p g e", g=NG),
                                    r_den[:, s:s + 1], None, ALU.mult)
                for b in range(4):
                    v.wait_ge(s_thi, 4 * l + b + 1)
                    piece = (slice(None), b // 2, slice((b % 2) * 512, (b % 2 + 1) * 512))
                    v.tensor_tensor(h_lo[piece], ps[:, b, :], h_hi[piece].bitcast(F32), ALU.subtract).then_inc(s_tlo, 1)
                v.wait_ge(s_pos, l + 1)
                pm = r_pm[:, :, :, :]
                link(v.scalar_tensor_tensor(pm.rearrange("p s g e -> p s (g e)"),
                                            ps[:, B_M, 0:2 * E].rearrange("p (s e) -> p s e", s=NSEQ),
                                            1.0, mask, ALU.add, ALU.mult))
                for r in range(MAX_ROUNDS):
                    v.tensor_scalar(posx[:, r * NG:(r + 1) * NG, :, :], pm.rearrange("p s g e -> p g s e"),
                                    -1.0 - SLOTS * r, None, ALU.add)
                link(v.memset(gcol[:, :], 0.0))
                link(v.tensor_reduce(r_cnt[:, 0:1], ps[:, B_M, 2 * E:3 * E], AX_X, ALU.max))
                link(v.tensor_tensor(r_cnt[:, 1:4], r_cnt[:, 0:1].to_broadcast([P, 3]), limits, ALU.is_gt))
                link(v.tensor_reduce(r_cnt[:, 4:5], r_cnt[:, 1:4], AX_X, ALU.add))
                v.tensor_scalar(rounds[:, l:l + 1], r_cnt[:, 4:5], 1.0, None, ALU.add).then_inc(s_rounds, 1)
                v.wait_ge(s_rounds, l + 1)

            base = ada_base = 0
            for l in range(DEPTH):
                norm(2 * l, n1g[:, l * DB:(l + 1) * DB], mod(l, 1), mod(l, 0), ((6, 8), (0, 2)) if l == 0 else None)
                (mixer_pool, mixer_attention, mixer_fourier)[KINDS[l]](l)
                norm(2 * l + 1, n2g[:, l * DB:(l + 1) * DB], mod(l, 4), mod(l, 3), ((14, 24), (3, 6)) if l == 0 else None)
                router(l)

                def onehots(group, g):
                    pos = posx[:, :, :, :].rearrange("p k s e -> p (k s e)")[:, bass.ds(group * 8, 8)]
                    v.tensor_tensor(onehot[:, :, :, :].rearrange("p s e c -> p (s e) c"),
                                    iota.unsqueeze(1).to_broadcast([P, 8, P]),
                                    pos.unsqueeze(2).to_broadcast([P, 8, P]), ALU.is_equal).then_inc(s_oh, 1)
                    v.tensor_copy(gsel[:, :, :].rearrange("p s e -> p (s e)"),
                                  gx[:, :, :, :].rearrange("p g s e -> p (g s e)")[:, bass.ds(g * 8, 8)]).then_inc(s_oh, 1)

                def output_lo(e, count):
                    for b in range(2):
                        v.wait_ge(s_yhi, count + (b + 1))
                        piece = (slice(None), e % 2, slice(b * 512, (b + 1) * 512))
                        v.scalar_tensor_tensor(y_lo[piece], ps[:, B_Y + b, :], gcol[:, e:e + 1],
                                               y_hi[piece].bitcast(F32), ALU.mult, ALU.subtract).then_inc(s_ylo, 1)

                def add_up(q, count):
                    v.wait_ge(s_comb, count)
                    h = quarter(hT, q)
                    v.tensor_tensor(h, h, ps[:, B_A + q % 2, :].rearrange("p (d t) -> p d t", d=2),
                                    ALU.add).then_inc(s_acc, 1)

                if l in MIX_LAYERS:
                    for n in range(2):
                        m = 2 * MIX_LAYERS.index(l) + n
                        if n == 0:
                            v.wait_ge(s_mixt, m + 2)
                        v.tensor_tensor(mod(l + 1, n), ps[:, B_T, n * 2 * DB:(n + 1) * 2 * DB].rearrange(
                            "p (n s) -> p n s", s=NSEQ),
                            adab[:, (l + 1) * NB_MOD + n * DB:(l + 1) * NB_MOD + (n + 1) * DB].unsqueeze(2).to_broadcast(
                                [P, DB, NSEQ]), ALU.add).then_inc(s_mixs, 1)
                v.wait_ge(s_posx, 2)
                onehots(0, 0)
                n = v.value_load(rounds[0:1, l:l + 1], min_val=1, max_val=MAX_ROUNDS)
                v.wait_ge(s_acc0, 4 * (l + 1))
                with v.Fori(0, n * NG) as k:
                    it = v.snap(base + k)
                    ada_it = v.snap(ada_base + k * ADA_PER[l])
                    it8 = v.snap(it * 8)
                    it48 = v.snap(it * NU)
                    g = v.snap(k & (NG - 1))
                    g_next = v.snap((k + 1) & (NG - 1))
                    k_next = v.snap(k + 1)

                    def split_lo(u):
                        v.wait_ge(s_hi, it48 + (u + 1))
                        v.tensor_tensor(w_lo[:, u % RING, :], raw[:, (u // 2) % RAW, u % 2, :],
                                        w_hi[:, u % RING, :].bitcast(F32), ALU.subtract).then_inc(s_lo, 1)

                    for u in range(NU):
                        split_lo(u)
                        if u in ADD_LAST:
                            add_up(ADD_LAST[u], it8 + (4 * l + ADD_LAST[u] + 1))
                        if u == GATES_COPIED:
                            v.wait_ge(s_gc, it + 1)
                            v.tensor_copy(gcol[:, :], ps[:, B_Y, 0:GROUP]).then_inc(s_gcs, 1)
                        if u in HIDDEN:
                            e = HIDDEN[u]
                            v.wait_ge(s_silu, it * GROUP + (e + 1))
                            v.tensor_tensor(act[:, :], sg[:, :], ps[:, B_T, FB * SLOTS:2 * FB * SLOTS],
                                            ALU.mult).then_inc(s_prod, 1)
                            v.wait_ge(s_prod, it * GROUP + (e + 1) + GRANT)
                            if e >= 2:
                                v.wait_ge(s_unit, it48 + (RING + END_DN[e - 2] + 1))
                            else:
                                v.wait_ge(s_unit, it48 + RING - (NU - 1 - END_DN[e + 2]))
                            a3 = act[:, :].rearrange("p (b s) -> p b s", b=FB)
                            v.tensor_copy(a_hl[:, e % 2, :, 0:SLOTS], a3).then_inc(s_ahi, 1)
                            v.wait_ge(s_ahi, it * GROUP + (e + 1))
                            v.tensor_tensor(a_hl[:, e % 2, :, SLOTS:2 * SLOTS], a3, a_hl[:, e % 2, :, 0:SLOTS].bitcast(F32),
                                            ALU.subtract).then_inc(s_alo, 1)
                        if u == NEXT_ONEHOT:
                            onehots(k_next, g_next)
                        if u == LAST_LO:
                            output_lo(3, it8 + 2 * l)
                        if u in OUTPUT_LO:
                            e = OUTPUT_LO[u]
                            output_lo(e, it8 + (2 * l + 2 + 2 * e))
                        if u in ADD_FIRST:
                            add_up(ADD_FIRST[u], it8 + (4 * l + 4 + ADD_FIRST[u] + 1))
                        if u in ADA_STORED[l]:
                            j = ADA_STORED[l][u]
                            store_ada(l + 1, g * ADA_PER[l] + (ADA_CHUNKS - NG * ADA_PER[l] + j), ada_it + (6 + j + 1))
                base = v.snap(base + n * NG)
                ada_base = v.snap(ada_base + n * (NG * ADA_PER[l]))
                output_lo(3, base * 8 + 2 * l)
                for q in range(4):
                    add_up(q, base * 8 + (4 * l + q + 1))
                v.wait_ge(s_acc, base * 8 + (4 * l + 4 + GRANT))
                for q in range(4):
                    residual(lambda d, s: hT[:, 2 * q + d, s * SEQ:(s + 1) * SEQ], mod(l, 5), q)
            norm(2 * DEPTH, fing, None, None)

        @block.tensor
        def _(pe):
            pe.wait_ge(s_load_v, 16 * N_VECTOR_LOADS)
            pe.transpose(ps[:, 4, 0:104], vrow[0:104, 0, :], ident[0:104, 0:104]).then_inc(s_rows, 1)
            for i in range(2):
                pe.transpose(ps[:, 5, 96 * i:96 * (i + 1)], vrow[0:96, 1 + i, :], ident[0:96, 0:96]).then_inc(s_rows, 1)
            def ada_product(slot, landed, count):
                pe.wait_ge(s_ada_in[slot], landed)
                pe.wait_ge(s_adac, count)
                for b in range(DB):
                    mm = pe.matmul(ps[0:NSEQ, B_M, T:T + ADA_COLS], cact[:, :, b], ada_in[:, slot, b, :],
                                   start=(b == 0), stop=(b == DB - 1))
                mm.then_inc(s_ada, 1)

            def ada_turn(count):
                pe.wait_ge(s_adac, count + 1)
                for n in range(ADA_NB):
                    mm = pe.matmul(ps[:, B_M, NSEQ * n:NSEQ * (n + 1)], ada_row[:, n * P:(n + 1) * P],
                                   ident[:, 0:NSEQ], start=True, stop=True)
                mm.then_inc(s_adat, 1)

            def mixer_products(l, a, b):
                for i in range(a, b):
                    m = MIX_CHUNKS * MIX_LAYERS.index(l) + i
                    pe.wait_ge(s_mix_in[i % ADA_SLOTS], 16 * (m // ADA_SLOTS + 1))
                    if i >= 1 and (i >= 2 or MIX_BANKS[l][0] == MIX_BANKS[l][1]):
                        pe.wait_ge(s_mixr, m - (0 if MIX_BANKS[l][i - 1] == MIX_BANKS[l][i] else 1))
                    for b8 in range(DB):
                        mm = pe.matmul(ps[0:NSEQ, MIX_BANKS[l][i], T:T + ADA_COLS], cact[:, :, b8], ada_in[:, i % ADA_SLOTS, b8, :],
                                       start=(b8 == 0), stop=(b8 == DB - 1))
                    mm.then_inc(s_mixp, 1)

            def mixer_rows_read(l, i):
                pe.wait_ge(s_mixr, MIX_CHUNKS * MIX_LAYERS.index(l) + i)

            def first_chunks(a, b):
                for c in range(a, b):
                    if c > 0:
                        pe.wait_ge(s_adac, c)
                    for half in range(2):
                        u = 2 * c + half
                        pe.wait_ge(s_flo, u + 1)
                        for w, first_half in ((f_hi, True), (f_lo, False)):
                            for b in range(4):
                                mm = pe.matmul(ps[0:2 * NSEQ, B_M, T:T + ADA_COLS], cond_hl[:, 4 * half + b, :],
                                               w[:, u % FIRST_RING, b * ADA_COLS:(b + 1) * ADA_COLS],
                                               start=(half == 0 and first_half and b == 0),
                                               stop=(half == 1 and not first_half and b == 3))
                        mm.then_inc(s_fu, 1)

            def turn_first(a, b):
                for n in range(a, b):
                    pe.wait_ge(s_adac, (n + 1) * MOD_CHUNKS)
                    if n >= 3:
                        pe.wait_ge(s_adas, n - 1)
                    for j in range(DB):
                        mm = pe.matmul(ps[:, MOD_BANK[n], NSEQ * j:NSEQ * (j + 1)],
                                       ada_rows[:, n * D + j * P:n * D + (j + 1) * P], fold, start=True, stop=True)
                    mm.then_inc(s_adat, 1)

            pe.wait_ge(s_clo, 1)
            first_chunks(0, 2)
            pe.wait_ge(s_load, 16 * N_X_LOADS)
            for q in range(4):
                for d in range(2):
                    for s in range(NSEQ):
                        mm = pe.transpose(ps[:, q, (2 * d + s) * SEQ:(2 * d + s + 1) * SEQ],
                                          xio[:, s, (2 * q + d) * P:(2 * q + d + 1) * P], ident)
                mm.then_inc(s_xt, 1)

            first_chunks(2, 4)
            pe.wait_ge(s_adac, 4)

            def norm(n):
                for b in range(DB):
                    if b % 2 == 0:
                        pe.wait_ge(s_sq, 4 * n + b // 2 + 1)
                    mm = pe.matmul(ps[:, B_M, 0:T], ones, work[:, b, :], start=(b == 0), stop=(b == DB - 1))
                mm.then_inc(s_ss, 1)

            def router(l):
                n = 2 * l + 1
                for s in range(NSEQ):
                    for b in range(DB):
                        if s == 0 and b % 2 == 0:
                            pe.wait_ge(s_hq, 4 * n + b // 2 + 1)
                        mm = pe.matmul(ps[:, B_M, s * E:(s + 1) * E], hT[:, b, s * SEQ:(s + 1) * SEQ], rw[:, b, :],
                                       start=(b == 0), stop=(b == DB - 1))
                mm.then_inc(s_lg, 1)
                for b in range(4):
                    s, half = b // 2, b % 2
                    for i in range(4):
                        mm = pe.transpose(ps[:, b, i * P:(i + 1) * P], hT[:, 4 * half + i, s * SEQ:(s + 1) * SEQ], ident)
                    mm.then_inc(s_tok, 1)
                if l in MIX_LAYERS:
                    mixer_products(l, MIX_CHUNKS - 1, MIX_CHUNKS)
                pe.wait_ge(s_mask, l + 1)
                pe.matmul(ps[:, B_M, 0:E], tri, r_mask[:, 0, :], start=True, stop=True)
                pe.matmul(ps[:, B_M, E:2 * E], ones, r_mask[:, 0, :], start=True, stop=False)
                pe.matmul(ps[:, B_M, E:2 * E], tri, r_mask[:, 1, :], start=False, stop=True)
                pe.matmul(ps[:, B_M, 2 * E:3 * E], ones, r_mask[:, 0, :], start=True, stop=False)
                pe.matmul(ps[:, B_M, 2 * E:3 * E], ones, r_mask[:, 1, :], start=False, stop=True).then_inc(s_pos, 1)
                if l in MIX_LAYERS:
                    mixer_rows_read(l, MIX_CHUNKS)
                    for v2 in range(2):
                        for j in range(DB):
                            mm = pe.transpose(ps[:, B_T, NSEQ * (v2 * DB + j):NSEQ * (v2 * DB + j + 1)],
                                              mix_rows[:, v2 * D + j * P:v2 * D + (j + 1) * P], ident[0:NSEQ, 0:NSEQ])
                        mm.then_inc(s_mixt, 1)

            def mixer_pool(l):
                if l == 0:
                    pe.wait_ge(s_ms, 1)
                    first_chunks(4, 8)
                    turn_first(0, 2)
                    mixer_products(l, 0, 1)
                    first_chunks(8, 10)
                    mixer_products(l, 1, 2)
                pe.wait_ge(s_kc, KC_AFTER[l])
                j = l // 3
                for g in range(4):
                    pe.wait_ge(s_hq, 4 * (2 * l) + g + 1)
                    for s in range(NSEQ):
                        for b in range(2):
                            mm = pe.matmul(ps[:, g, s * T:(s + 1) * T], hT[:, 2 * g + b, s * SEQ:(s + 1) * SEQ],
                                           wp[:, g, b, :], start=(b == 0), stop=(b == 1))
                    mm.then_inc(s_z, 1)
                if l == 0:
                    first_chunks(10, 12)
                    mixer_rows_read(l, 2)
                    turn_first(2, 3)
                for g in range(4):
                    pe.wait_ge(s_zo if g % 2 else s_ze, 2 * j + g // 2 + 1)
                    for d in range(2):
                        for s in range(NSEQ):
                            mm = pe.matmul(ps[:, g, (2 * d + s) * SEQ:(2 * d + s + 1) * SEQ],
                                           ztok[:, g, s, d * P:(d + 1) * P], kpool[:, g, :], start=True, stop=True)
                    mm.then_inc(s_mix, 1)

            def mixer_attention(l):
                for t in range(12):
                    n = WM_AT[("qkv", t)]
                    if t == 0:
                        pe.wait_ge(s_hq, 4 * (2 * l) + 4)
                    pe.wait_ge(s_wm[n % WM_RING], 16 * (n // WM_RING + 1))
                    if t >= 4:
                        if t % 2 == 0:
                            pe.wait_ge(s_qkve, (t - 4) // 2 + 1)
                        else:
                            pe.wait_ge(s_qkvo, (t - 5) // 2 + 1)
                    for d in range(2):
                        for b in range(DB):
                            if t < 8:
                                lhs, rhs = wm[:, n % WM_RING, b, d * P:(d + 1) * P], hT[:, b, :]
                            else:
                                lhs, rhs = hT[:, b, d * SEQ:(d + 1) * SEQ], wm[:, n % WM_RING, b, :]
                            mm = pe.matmul(ps[:, t % 4, d * T:(d + 1) * T], lhs, rhs, start=(b == 0), stop=(b == DB - 1))
                    mm.then_inc(s_wmu, 1)
                pe.wait_ge(s_kc, KC_AFTER[l])
                pe.wait_ge(s_ms, 2 * l + 1)
                pe.wait_ge(s_bias, 16 * 6)
                rows = oT[:, :, :].rearrange("p d t -> p (d t)")
                for b in range(4):
                    pe.matmul(ps[:, 4 + b, :], kattn[:, 1, :], rows[:, b * 512:(b + 1) * 512],
                              start=True, stop=True).then_inc(s_flip, 1)
                pe.wait_ge(s_biass, 4)
                for b in range(4):
                    for i in range(4):
                        j = 4 * (b % 2) + i
                        src = ck[:, j * P:(j + 1) * P] if b < 2 else kT[:, j, 0:SEQ]
                        if b == 2 and i == 0:
                            pe.wait_ge(s_qkve, 4)
                            pe.wait_ge(s_qkvo, 4)
                        mm = pe.transpose(ps[:, 4 + b, i * P:(i + 1) * P], src, ident)
                    mm.then_inc(s_kt, 1)
                pe.wait_ge(s_kts, 4)
                pe.wait_ge(s_qkve, 6)
                pe.wait_ge(s_qkvo, 6)

                def scores(hp):
                    if hp >= 2:
                        pe.wait_ge(s_max, hp - 1)
                    for e in range(2):
                        rows = slice(e * HD, (e + 1) * HD)
                        bank = ps[:, 2 * (hp % 2) + e, :]
                        q_ctx, q_lat = work[rows, hp, 0:SEQ], work[rows, hp, SEQ:T]
                        pe.matmul(bank[:, 0:P], q_ctx, kT[rows, hp, 0:SEQ], start=True, stop=True)
                        pe.matmul(bank[:, P:2 * P], q_lat, kT[rows, hp, SEQ:T], start=True, stop=True)
                        mm = pe.matmul(bank[:, 2 * P:3 * P], q_lat, ckT[rows, hp, :], start=True, stop=True)
                    mm.then_inc(s_sc, 1)

                def turn(hp):
                    pe.wait_ge(s_prob, hp + 1)
                    if hp >= 1:
                        pe.wait_ge(s_pts, hp)
                    for e in range(2):
                        for i in range(3):
                            mm = pe.transpose(ps[:, 4 + e, i * P:(i + 1) * P], soft[:, hp % 2, e, i * P:(i + 1) * P], ident)
                    mm.then_inc(s_pt2, 1)

                def attend(hp):
                    pe.wait_ge(s_pts, hp + 1)
                    if hp >= 2:
                        pe.wait_ge(s_os, hp - 1)
                    for e in range(2):
                        cols = slice((2 * hp + e) * HD, (2 * hp + e + 1) * HD)
                        out = ps[e * HD:(e + 1) * HD, 6 + hp % 2, :]
                        p = pT[:, hp % 2, e, :]
                        pe.matmul(out[:, 0:SEQ], vtok[:, 0, cols], p[:, 0:P], start=True, stop=True)
                        pe.matmul(out[:, SEQ:T], vtok[:, 1, cols], p[:, P:2 * P], start=True, stop=False)
                        mm = pe.matmul(out[:, SEQ:T], cv[:, cols], p[:, 2 * P:3 * P], start=False, stop=True)
                    mm.then_inc(s_o, 1)

                scores(0)
                scores(1)
                mixer_products(l, 3, 4)
                mixer_rows_read(l, 4)
                for hp in range(PAIRS):
                    turn(hp)
                    if hp + 2 < PAIRS:
                        scores(hp + 2)
                    attend(hp)
                pe.wait_ge(s_os, PAIRS)
                out_project("wo", oT, 0)

            def out_project(name, src, first_bank):
                for i in range(4):
                    n = WM_AT[(name, i)]
                    pe.wait_ge(s_wm[n % WM_RING], 16 * (n // WM_RING + 1))
                    for d in range(2):
                        for b in range(DB):
                            mm = pe.matmul(ps[:, first_bank + i, d * T:(d + 1) * T], wm[:, n % WM_RING, b, d * P:(d + 1) * P],
                                           src[:, b, :], start=(b == 0), stop=(b == DB - 1))
                    mm.then_inc(s_wmu, 1)

            def mixer_fourier(l):
                pe.wait_ge(s_kc, KC_AFTER[l])
                chan = kfour[:, 2 * P:].rearrange("p (b n) -> p b n", b=2)
                for b8 in range(8):
                    s, g = b8 // 4, b8 % 4
                    pe.wait_ge(s_hq, 4 * (2 * l) + g + 1)
                    for b in range(2):
                        mm = pe.matmul(ps[:, b8, :], hT[:, 2 * g + b, s * SEQ:(s + 1) * SEQ], chan[:, b, :],
                                       start=(b == 0), stop=(b == 1))
                    mm.then_inc(s_f1, 1)
                pe.wait_ge(s_f1e, 4)
                pe.wait_ge(s_f1o, 4)
                for g in range(4):
                    for d in range(2):
                        for s in range(NSEQ):
                            out = ps[:, g, (2 * d + s) * SEQ:(2 * d + s + 1) * SEQ]
                            pe.matmul(out, ftok[:, s, g, d * P:(d + 1) * P], kfour[:, 0:P], start=True, stop=False)
                            mm = pe.matmul(out, ftok[:, s, g, 256 + d * P:256 + (d + 1) * P], kfour[:, P:2 * P],
                                           start=False, stop=True)
                    mm.then_inc(s_f2, 1)
                pe.wait_ge(s_f2s, 4)
                out_project("four", fT, 0)

            base = ada_base = 0
            for l in range(DEPTH):
                if l > 0:
                    pe.wait_ge(s_adas, ada_base + 6)
                else:
                    pe.wait_ge(s_cact, 1)
                    pe.wait_ge(s_vecs, 2)
                if l in MIX_LAYERS and l > 0:
                    mixer_products(l, 0, 1)
                norm(2 * l)
                if l in MIX_LAYERS and l > 0:
                    pe.wait_ge(s_ms, 2 * l + 1)
                    mixer_products(l, 1, 3)
                    mixer_rows_read(l, 3)
                (mixer_pool, mixer_attention, mixer_fourier)[KINDS[l]](l)
                if l == 0:
                    pe.wait_ge(s_adac, 3 * MOD_CHUNKS)
                if l in MIX_LAYERS:
                    mixer_products(l, MIX_SECOND[l], MIX_SECOND[l] + 1)
                norm(2 * l + 1)
                pe.wait_ge(s_ms, 2 * l + 2)
                if l in MIX_LAYERS and l > 0:
                    mixer_products(l, MIX_SECOND[l] + 1, MIX_CHUNKS - 1)
                if l == 0:
                    for i in range(4):
                        first_chunks(12 + 3 * i, 15 + 3 * i)
                        mixer_products(l, 3 + i, 4 + i)
                    mixer_rows_read(l, 7)
                    turn_first(3, 6)
                router(l)

                def gather(gi, db, bank=None):
                    if db >= (2 if bank is None else 6):
                        pe.wait_ge(s_gev, gi * 8 + (db - 1))
                    for half, h in enumerate((h_hi, h_lo)):
                        for s in range(NSEQ):
                            mm = pe.matmul(ps[:, B_A + db % 2 if bank is None else bank, half * 256:(half + 1) * 256],
                                           h[:, s, db * P:(db + 1) * P], onehot[:, s, :, 0:SLOTS],
                                           start=(s == 0), stop=(s == NSEQ - 1))
                    mm.then_inc(s_ga, 1)

                def combine(pair, q):
                    for d in range(2):
                        n2 = 0
                        for e in range(2):
                            for y in (y_hi, y_lo):
                                mm = pe.matmul(ps[:, B_A + q % 2, d * T:(d + 1) * T],
                                               y[:, e, (2 * q + d) * P:(2 * q + d + 1) * P],
                                               onehotT[:, 2 * pair + e, :], start=(n2 == 0), stop=(n2 == 3))
                                n2 += 1
                    mm.then_inc(s_comb, 1)

                def combine_last(q, it8, gi):
                    if q == 0:
                        pe.wait_ge(s_ylo, it8 + (2 * l + 2 + GRANT))
                    if q < 2:
                        pe.wait_ge(s_gev, gi * 8 + (7 + q))
                    else:
                        pe.wait_ge(s_acc, it8 + (4 * l + q - 1 + GRANT))
                    combine(1, q)

                pe.wait_ge(s_rounds, l + 1)
                pe.wait_ge(s_tlo, 4 * l + 4)
                first = pe.snap(base + l)
                pe.wait_ge(s_oh, first * 2 + 2)
                for db in range(DB):
                    gather(first, db, FIRST_GATHER_BANKS[db])
                n = pe.value_load(rounds[0:1, l:l + 1], min_val=1, max_val=MAX_ROUNDS)
                pe.wait_ge(s_acc0, 4 * (l + 1))
                with pe.Fori(0, n * NG) as k:
                    it = pe.snap(base + k)
                    ada_it = pe.snap(ada_base + k * ADA_PER[l])
                    it4 = pe.snap(it * 4)
                    it8 = pe.snap(it * 8)
                    it48 = pe.snap(it * NU)
                    gi = pe.snap(it + l)
                    following = pe.snap(it + (l + 1))

                    def gate_up_unit(e, b):
                        u = FIRST[("gu", e)] + b
                        if e == 0:
                            pe.wait_ge(s_gev, gi * 8 + (b + 1))
                        if b == 0:
                            pe.wait_ge(s_gus, it8 + 2 * e + GRANT)
                        pe.wait_ge(s_lo, it48 + (u + 1 + RAW_CREDIT))
                        for w, first_half in ((w_hi, True), (w_lo, False)):
                            for n2 in range(2):
                                mm = pe.matmul(ps[:, B_G + n2, :], xg[:, b, e, :], w[:, u % RING, n2 * F:(n2 + 1) * F],
                                               start=(b == 0 and first_half), stop=(b == DB - 1 and not first_half))
                        mm.then_inc(s_unit, 1)

                    def down_unit(e, b):
                        u = FIRST[("dn", e)] + b
                        if b == 0:
                            pe.wait_ge(s_alo, it4 + (e + 1))
                            pe.wait_ge(s_ylo, it8 + (2 * l + 2 + 2 * e + GRANT))
                            if e == 0:
                                pe.wait_ge(s_gcs, it + 1)
                        pe.wait_ge(s_lo, it48 + (u + 1 + RAW_CREDIT))
                        for w, first_half in ((w_hi, True), (w_lo, False)):
                            for n2 in range(2):
                                mm = pe.matmul(ps[:, B_Y + n2, :], a_hl[:, e % 2, b, :], w[:, u % RING, n2 * 512:(n2 + 1) * 512],
                                               start=(b == 0 and first_half), stop=(b == FB - 1 and not first_half))
                        mm.then_inc(s_unit, 1)

                    def turn(e):
                        pe.wait_ge(s_gus, it8 + (2 * e + 2) + GRANT)
                        pe.wait_ge(s_prod, it4 + e + GRANT)
                        for i in range(2 * FB):
                            mm = pe.matmul(ps[:, B_T, i * SLOTS:(i + 1) * SLOTS], gu[:, i * P:(i + 1) * P], halves,
                                           start=True, stop=True)
                        mm.then_inc(s_turn, 1)

                    def turn_onehots():
                        pe.wait_ge(s_acc, it8 + (4 * l + 4 + GRANT))
                        for e in range(GROUP):
                            for s in range(NSEQ):
                                at = (e % 2) * T + s * SEQ
                                mm = pe.transpose(ps[:, B_A + e // 2, at:at + SEQ], onehot[:, s, e, :].bitcast(F32), ident)
                            if e % 2:
                                mm.then_inc(s_oht, 1)

                    def slot_gates():
                        for e in range(GROUP):
                            for s in range(NSEQ):
                                mm = pe.matmul(ps[:, B_Y, e:e + 1], onehot[:, s, e, :].bitcast(F32), gsel[:, s, e:e + 1],
                                               start=(s == 0), stop=(s == NSEQ - 1))
                        mm.then_inc(s_gc, 1)

                    def combine_first(q):
                        if q == 0:
                            pe.wait_ge(s_ylo, it8 + (2 * l + 6 + GRANT))
                        if q < 2:
                            pe.wait_ge(s_ohs, it * 2 + 2)
                        else:
                            pe.wait_ge(s_acc, it8 + (4 * l + 4 + q - 1 + GRANT))
                        combine(0, q)

                    for u, (kind, e, i) in enumerate(UNITS):
                        (gate_up_unit if kind == "gu" else down_unit)(e, i)
                        if u in PE_COMBINE_LAST:
                            combine_last(PE_COMBINE_LAST[u], it8, gi)
                        if u == PE_ONEHOT_TURN:
                            turn_onehots()
                        if u == PE_GATES:
                            slot_gates()
                        if u in PE_TURN:
                            turn(PE_TURN[u])
                        if u in PE_COMBINE_FIRST:
                            combine_first(PE_COMBINE_FIRST[u])
                        for db in PE_GATHER.get(u, []):
                            if db == 0:
                                pe.wait_ge(s_oh, following * 2 + 2)
                                pe.wait_ge(s_acc, it8 + (4 * l + 8 + GRANT))
                            gather(following, db)
                        if u in PE_ADA[l]:
                            j = PE_ADA[l][u]
                            pe.wait_ge(s_adas, ada_it + (6 + j))
                            ada_product(j % ADA_SLOTS, ada_it * (16 // ADA_SLOTS) + 16 * (j // ADA_SLOTS + 1),
                                        ada_it + (ADA_CHUNKS + j))
                        if u in PE_ADA_TURN[l]:
                            ada_turn(ada_it + (ADA_CHUNKS + PE_ADA_TURN[l][u]))
                base = pe.snap(base + n * NG)
                ada_base = pe.snap(ada_base + n * (NG * ADA_PER[l]))
                for q in range(4):
                    combine_last(q, base * 8, base + l)
            norm(2 * DEPTH)
            for b in range(4):
                s, half = b // 2, b % 2
                for i in range(4):
                    if s == 0:
                        pe.wait_ge(s_hq, 4 * 2 * DEPTH + (4 * half + i) // 2 + 1)
                    mm = pe.transpose(ps[:, b, i * P:(i + 1) * P], hT[:, 4 * half + i, s * SEQ:(s + 1) * SEQ], ident)
                mm.then_inc(s_yt, 1)


_INS = ["x_prompt", "x_sample", "cache_k", "cache_v", "c", "c_ctx", "ada_w", "ada_b", "norm1_g", "norm2_g", "pool_w",
        "pool_scale", "attn_wqkv", "attn_wo", "attn_rpb", "fourier_w", "router_w", "router_b", "moe_w_gate", "moe_w_up",
        "moe_w_down", "final_norm_g"]
_OUTS = [((1, 128, 1024), "float32"), ((1, 128, 1024), "float32"),
         ((1, 1, 128, 16, 64), "float32"), ((1, 1, 128, 16, 64), "float32")]


def kernel(**inputs):
    import numpy as _np
    import concourse.bacc as _bacc
    from concourse import mybir as _mybir
    from concourse.bass_utils import run_bass_kernel_spmd as _run

    nc = _bacc.Bacc("TRN2", target_bir_lowering=False, num_devices=1)
    arrays, args = {}, []
    given = {name: _np.ascontiguousarray(inputs[name]) for name in _INS}
    given.update(host_constants())
    for name, a in given.items():
        arrays[f"in_{name}_dram"] = a
        args.append(nc.dram_tensor(f"in_{name}_dram", a.shape, _mybir.dt.from_np(a.dtype), kind="ExternalInput").ap())
    for i, (shape, dtype) in enumerate(_OUTS):
        dt = _mybir.dt.from_np(_np.dtype(dtype))
        args.append(nc.dram_tensor(f"out_{i}_dram", shape, dt, kind="ExternalOutput").ap())
    build(nc, *args)
    r = _run(nc, [arrays], core_ids=[0])
    return tuple(r.results[0][f"out_{i}_dram"] for i in range(len(_OUTS)))
```
